# Optimizing a Trainium2 kernel written in Bass

```python
import math
import jax, jax.numpy as jnp
from jax import lax
import numpy as np

D_MODEL = 1024
BATCH = 1
SEQ = 1024
DEPTH = 1

MLA_HEADS = 8
QK_NOPE_DIM = 128
QK_ROPE_DIM = 64
V_HEAD_DIM = 128
Q_LORA_RANK = 384
KV_LORA_RANK = 256
MLA_WIDTH = MLA_HEADS * V_HEAD_DIM
QK_HEAD_DIM = QK_NOPE_DIM + QK_ROPE_DIM
ROPE_THETA = 10000.0
ATTN_BLOCK = 128

SSM_HEAD_DIM = 64
SSM_HEADS = 16
SSM_WIDTH = SSM_HEADS * SSM_HEAD_DIM
SSM_GROUPS = 2
SSM_STATE = 128
CONV_WIDTH = 4
CHUNK = 128
CONV_CH = SSM_WIDTH + 2 * SSM_GROUPS * SSM_STATE

MIX_WIDTH = MLA_WIDTH + SSM_WIDTH

IN_SPLITS = (Q_LORA_RANK, KV_LORA_RANK + QK_ROPE_DIM, MLA_WIDTH, CONV_CH, SSM_HEADS, SSM_WIDTH)
IN_WIDTH = sum(IN_SPLITS)

DEEPNORM_ALPHA = (2.0 * DEPTH) ** 0.25
DEEPNORM_BETA = (8.0 * DEPTH) ** -0.25
RMS_EPS = 1e-6
LN_EPS = 1e-5

kernel_name = "hybrid_mla_ssd_parallel_heads_deepnorm_adaln"

def split_last(x, sizes):
    out, start = [], 0
    for s in sizes:
        out.append(x[..., start:start + s])
        start += s
    return out

def rms_norm(x, g):
    xf = x.astype(jnp.float32)
    y = xf * lax.rsqrt(jnp.mean(xf * xf, axis=-1, keepdims=True) + RMS_EPS)
    return (y * g.astype(jnp.float32)).astype(x.dtype)

def layer_norm(x, g, b):
    xf = x.astype(jnp.float32)
    mu = jnp.mean(xf, axis=-1, keepdims=True)
    var = jnp.mean(jnp.square(xf - mu), axis=-1, keepdims=True)
    y = (xf - mu) * lax.rsqrt(var + LN_EPS)
    return (y * g.astype(jnp.float32) + b.astype(jnp.float32)).astype(x.dtype)

def apply_rope(x, positions):
    half = QK_ROPE_DIM // 2
    inv_freq = 1.0 / (ROPE_THETA ** (jnp.arange(half, dtype=jnp.float32) / half))
    ang = positions.astype(jnp.float32)[..., None] * inv_freq
    cos = jnp.cos(ang)[:, :, None, :]
    sin = jnp.sin(ang)[:, :, None, :]
    xf = x.astype(jnp.float32)
    x1, x2 = xf[..., :half], xf[..., half:]
    out = jnp.concatenate([x1 * cos - x2 * sin, x2 * cos + x1 * sin], axis=-1)
    return out.astype(x.dtype)

def causal_block_attention(q, k, v, scale):
    b, s, h, dq = q.shape
    nb = s // ATTN_BLOCK
    qb = q.reshape(b, nb, ATTN_BLOCK, h, dq).transpose(1, 0, 2, 3, 4)
    key_pos = jnp.arange(s)

    def one_block(args):
        q_blk, i = args
        sc = jnp.einsum('bqhd,bkhd->bhqk', q_blk, k,
                        preferred_element_type=jnp.float32) * scale
        q_pos = i * ATTN_BLOCK + jnp.arange(ATTN_BLOCK)
        mask = key_pos[None, :] <= q_pos[:, None]
        sc = jnp.where(mask[None, None], sc, -jnp.inf)
        p = jax.nn.softmax(sc, axis=-1).astype(v.dtype)
        return jnp.einsum('bhqk,bkhd->bqhd', p, v)

    out = lax.map(one_block, (qb, jnp.arange(nb)))
    return out.transpose(1, 0, 2, 3, 4).reshape(b, s, h, v.shape[-1])

def mla_branch(q_lat, kv_lat, positions, q_norm_g, w_qb, kv_norm_g, w_kvb):
    b, s, _ = q_lat.shape
    q = (rms_norm(q_lat, q_norm_g) @ w_qb).reshape(b, s, MLA_HEADS, QK_HEAD_DIM)
    q_nope, q_rope = q[..., :QK_NOPE_DIM], q[..., QK_NOPE_DIM:]
    c_kv, k_rope = kv_lat[..., :KV_LORA_RANK], kv_lat[..., KV_LORA_RANK:]
    kv = (rms_norm(c_kv, kv_norm_g) @ w_kvb).reshape(b, s, MLA_HEADS, QK_NOPE_DIM + V_HEAD_DIM)
    k_nope, v = kv[..., :QK_NOPE_DIM], kv[..., QK_NOPE_DIM:]
    q_rope = apply_rope(q_rope, positions)
    k_rope = apply_rope(k_rope[:, :, None, :], positions)
    q = jnp.concatenate([q_nope, q_rope], axis=-1)
    k = jnp.concatenate([k_nope, jnp.broadcast_to(k_rope, (b, s, MLA_HEADS, QK_ROPE_DIM))], axis=-1)
    o = causal_block_attention(q, k, v, QK_HEAD_DIM ** -0.5)
    return o.reshape(b, s, MLA_WIDTH)

def causal_depthwise_conv(x, w, bias):
    out = lax.conv_general_dilated(
        x, w[:, None, :], window_strides=(1,), padding=[(CONV_WIDTH - 1, 0)],
        dimension_numbers=('NWC', 'WIO', 'NWC'), feature_group_count=x.shape[-1])
    return out + bias

def ssd_chunked(x, da, bm, cm):
    out_dtype = x.dtype
    b, s, h, p = x.shape
    nc, r = s // CHUNK, h // SSM_GROUPS
    f32 = jnp.float32
    X = x.astype(f32).reshape(b, nc, CHUNK, SSM_GROUPS, r, p)
    A = da.astype(f32).reshape(b, nc, CHUNK, SSM_GROUPS, r)
    Bc = bm.astype(f32).reshape(b, nc, CHUNK, SSM_GROUPS, SSM_STATE)
    Cc = cm.astype(f32).reshape(b, nc, CHUNK, SSM_GROUPS, SSM_STATE)
    a_cum = jnp.cumsum(A, axis=2)
    seg = a_cum[:, :, :, None] - a_cum[:, :, None, :]
    tri = jnp.tril(jnp.ones((CHUNK, CHUNK), dtype=bool))[:, :, None, None]
    decay = jnp.exp(jnp.where(tri, seg, -jnp.inf))
    cb = jnp.einsum('bclgn,bcsgn->bclsg', Cc, Bc)
    y_diag = jnp.einsum('bclsgr,bcsgrp->bclgrp', cb[..., None] * decay, X)
    decay_to_end = jnp.exp(a_cum[:, :, -1:] - a_cum)
    states = jnp.einsum('bclgn,bclgr,bclgrp->bcgrpn', Bc, decay_to_end, X)
    chunk_decay = jnp.exp(a_cum[:, :, -1])

    def step(hc, inp):
        st, dc = inp
        return hc * dc[..., None, None] + st, hc

    h0 = jnp.zeros((b, SSM_GROUPS, r, p, SSM_STATE), f32)
    _, prev = lax.scan(step, h0, (states.transpose(1, 0, 2, 3, 4, 5),
                                   chunk_decay.transpose(1, 0, 2, 3)))
    prev = prev.transpose(1, 0, 2, 3, 4, 5)
    y_off = jnp.einsum('bclgn,bcgrpn,bclgr->bclgrp', Cc, prev, jnp.exp(a_cum))
    return (y_diag + y_off).reshape(b, s, h, p).astype(out_dtype)

def ssd_branch(xbc_raw, dt_raw, z, conv_w, conv_b, dt_bias, a_log, d_skip, ssm_norm_g):
    b, s, _ = xbc_raw.shape
    xbc = jax.nn.silu(causal_depthwise_conv(xbc_raw, conv_w, conv_b))
    xs, bm, cm = split_last(xbc, (SSM_WIDTH, SSM_GROUPS * SSM_STATE, SSM_GROUPS * SSM_STATE))
    xs = xs.reshape(b, s, SSM_HEADS, SSM_HEAD_DIM)
    bm = bm.reshape(b, s, SSM_GROUPS, SSM_STATE)
    cm = cm.reshape(b, s, SSM_GROUPS, SSM_STATE)
    dt = jax.nn.softplus(dt_raw.astype(jnp.float32) + dt_bias.astype(jnp.float32))
    a = -jnp.exp(a_log.astype(jnp.float32))
    y = ssd_chunked(xs * dt[..., None].astype(xs.dtype), dt * a, bm, cm)
    y = y + xs * d_skip[:, None]
    hf = (y.reshape(b, s, SSM_WIDTH).astype(jnp.float32)
          * jax.nn.silu(z.astype(jnp.float32))).reshape(b, s, SSM_GROUPS, -1)
    hf = hf * lax.rsqrt(jnp.mean(hf * hf, axis=-1, keepdims=True) + RMS_EPS)
    return (hf.reshape(b, s, SSM_WIDTH) * ssm_norm_g.astype(jnp.float32)).astype(xbc_raw.dtype)

def hybrid_layer(x, c, positions, w_ada, b_ada, w_in, q_norm_g, w_qb, kv_norm_g, w_kvb,
                 conv_w, conv_b, dt_bias, a_log, d_skip, ssm_norm_g, w_out, ln_g, ln_b):
    mod = c @ w_ada + b_ada
    shift, scale, gate = mod[:, :D_MODEL], mod[:, D_MODEL:2 * D_MODEL], mod[:, 2 * D_MODEL:]
    u = x * (1.0 + scale[:, None, :]) + shift[:, None, :]
    proj = u @ w_in
    q_lat, kv_lat, z_attn, xbc, dt_raw, z_ssm = split_last(proj, IN_SPLITS)
    o_attn = mla_branch(q_lat, kv_lat, positions, q_norm_g, w_qb, kv_norm_g, w_kvb) * jax.nn.silu(z_attn)
    o_ssm = ssd_branch(xbc, dt_raw, z_ssm, conv_w, conv_b, dt_bias, a_log, d_skip, ssm_norm_g)
    mixed = jnp.concatenate([o_attn, o_ssm], axis=-1) @ w_out
    return layer_norm(DEEPNORM_ALPHA * x + gate[:, None, :] * mixed, ln_g, ln_b)

def setup_inputs(seed: int = 0) -> dict:
    key = jax.random.key(seed)
    ks = jax.random.split(key, 20)
    f32 = jnp.float32
    n = lambda k, shape, s: jax.random.normal(k, shape, f32) * s
    L = DEPTH
    dt0 = jnp.exp(jax.random.uniform(ks[12], (L, SSM_HEADS), f32, math.log(1e-3), math.log(1e-1)))
    return {
        "x": jax.random.normal(ks[0], (BATCH, SEQ, D_MODEL), f32),
        "c": jax.random.normal(ks[1], (BATCH, D_MODEL), f32),
        "positions": jnp.broadcast_to(jnp.arange(SEQ, dtype=jnp.int32), (BATCH, SEQ)),
        "w_ada": n(ks[2], (L, D_MODEL, 3 * D_MODEL), 0.5 * D_MODEL ** -0.5),
        "b_ada": n(ks[3], (L, 3 * D_MODEL), 0.02),
        "w_in": n(ks[4], (L, D_MODEL, IN_WIDTH), D_MODEL ** -0.5),
        "q_norm_g": 1.0 + n(ks[5], (L, Q_LORA_RANK), 0.05),
        "w_qb": n(ks[6], (L, Q_LORA_RANK, MLA_HEADS * QK_HEAD_DIM), Q_LORA_RANK ** -0.5),
        "kv_norm_g": 1.0 + n(ks[7], (L, KV_LORA_RANK), 0.05),
        "w_kvb": n(ks[8], (L, KV_LORA_RANK, MLA_HEADS * (QK_NOPE_DIM + V_HEAD_DIM)), KV_LORA_RANK ** -0.5),
        "conv_w": n(ks[9], (L, CONV_WIDTH, CONV_CH), CONV_WIDTH ** -0.5),
        "conv_b": n(ks[10], (L, CONV_CH), 0.02),
        "dt_bias": dt0 + jnp.log(-jnp.expm1(-dt0)),
        "a_log": jnp.log(jax.random.uniform(ks[13], (L, SSM_HEADS), f32, 1.0, 16.0)),
        "d_skip": 1.0 + n(ks[14], (L, SSM_HEADS), 0.1),
        "ssm_norm_g": 1.0 + n(ks[15], (L, SSM_WIDTH), 0.05),
        "w_out": n(ks[16], (L, MIX_WIDTH, D_MODEL), DEEPNORM_BETA * MIX_WIDTH ** -0.5),
        "ln_g": 1.0 + n(ks[17], (L, D_MODEL), 0.05),
        "ln_b": n(ks[18], (L, D_MODEL), 0.02),
    }

def reference(x, c, positions, w_ada, b_ada, w_in, q_norm_g, w_qb, kv_norm_g, w_kvb,
              conv_w, conv_b, dt_bias, a_log, d_skip, ssm_norm_g, w_out, ln_g, ln_b):
    h = x
    for l in range(DEPTH):
        h = hybrid_layer(h, c, positions, w_ada[l], b_ada[l], w_in[l], q_norm_g[l], w_qb[l],
                         kv_norm_g[l], w_kvb[l], conv_w[l], conv_b[l], dt_bias[l], a_log[l],
                         d_skip[l], ssm_norm_g[l], w_out[l], ln_g[l], ln_b[l])
    return h


_drawn_inputs = setup_inputs


def setup_inputs(seed=0):
    import zlib

    import numpy as np

    out = dict(_drawn_inputs(seed))
    spreads = {}
    factors = {'b_ada': 5.685,
     'q_norm_g': 8.0,
     'w_qb': 4.023,
     'kv_norm_g': 8.0,
     'conv_b': 8.0,
     'd_skip': 5.303,
     'ssm_norm_g': 6.446,
     'ln_b': 2.909}
    for name, (base, spread) in spreads.items():
        noise = np.random.default_rng([zlib.crc32(name.encode()), seed]).standard_normal(out[name].shape)
        drawn = base * np.exp(spread * noise) if base else spread * noise
        out[name] = __import__('jax').numpy.asarray(drawn.astype(out[name].dtype))
    for name, factor in factors.items():
        out[name] = (out[name] * factor).astype(out[name].dtype)
    return out
```

```python
from contextlib import ExitStack

import numpy as np

import concourse.bass as bass
from concourse import mybir

F32 = mybir.dt.float32
F32R = mybir.dt.float32r
I32 = mybir.dt.int32
ALU = mybir.AluOpType
ACT = mybir.ActivationFunctionType
AX = mybir.AxisListType

P = 128
D = 1024
S = 1024
KT = D // P
HB = 512
NHALF = S // HB
HEADS = 8
ROPE = 64
QW = 192
QLT = 3
KLT = 2
LAT = QLT + KLT
SSM_H = 16
NST = 8
CONVT = 12
TAPS = 4
CHUNKS = S // P
W_KV_ROPE = 640
W_ZATT = 704
W_XBC = 1728
W_DT = 3264
W_ZSSM = 3280
Z_ATT0 = 6
Z_SSM0 = 14
C_CONVW, C_CONVB, C_QG, C_KVG, C_SG, NVEC = 24, 72, 84, 87, 89, 97
ALPHA = 2.0 ** 0.25
RMS_EPS = 1e-6
LN_EPS = 1e-5
SCALE = 192.0 ** -0.5
NEG = -1.0e30
MAGIC = 12582912.0
PI2_A = 6.28125
PI2_B = 0.0019350051879882812
PI2_C = float(2 * np.pi - 6.28125 - 0.0019350051879882812)
DT0, AC0 = 64, 96


def build_layer(nc, x, c, pos, w_ada, b_ada, w_in, qg, w_qb, kvg, w_kvb, conv_w, conv_b, dt_bias,
                a_log, d_skip, ssmg, w_out, ln_g, ln_b, ropec, out):
    scr = nc.dram_tensor("proj_scratch", [22, P, S], F32).ap()
    scy = nc.dram_tensor("ssm_scratch", [NST, P, S], F32).ap()
    scg = nc.dram_tensor("ssm_gated_scratch", [NST, P, S], F32).ap()
    sco = nc.dram_tensor("attn_scratch", [HEADS, P, S], F32).ap()

    ctx = ExitStack()
    with ctx:
        def at(offset, spec):
            made = []
            for name, shape, dt in spec:
                made.append(nc.alloc_sbuf_tensor_at(name, shape, dt, offset=offset))
                offset += -(-int(np.prod(shape[1:])) * 4 // 32) * 32
            return made, offset

        def sem(name):
            return ctx.enter_context(nc.semaphore(name))

        base = -(-nc.sbuf_base // 64) * 64
        (ident, ones, mask_qk, mask_ls, colv, modc, gate_b, dsk, dsr, dtb, alg, ccol, rcst, small), end_c = at(base, [
            ("ident", [P, P], F32), ("ones", [P, P], F32), ("mask_qk", [P, P], F32), ("mask_ls", [P, P], F32),
            ("colv", [P, NVEC], F32), ("modc", [P, 16], F32), ("gate_b", [P, D], F32), ("dsk", [P, NST], F32), ("dsr", [P, SSM_H], F32),
            ("dtb", [P, 1], F32), ("alg", [P, 1], F32), ("ccol", [P, KT], F32), ("rcst", [P, 4], F32),
            ("small", [P, 64], F32)])
        reg_a, reg_b = end_c, end_c + 13 * S * 4
        limit = nc.sbuf_usable_end

        (xin,), _ = at(reg_a, [("xin", [P, CHUNKS, D], F32)])
        (cx,), e = at(reg_a, [("cx", [P, 13, S], F32)])
        assert e <= reg_b
        (qlh, qll, ckh, ckl, rl), e = at(reg_a, [
            ("qlh", [P, QLT, S], F32R), ("qll", [P, QLT, S], F32R), ("ckh", [P, KLT, S], F32R),
            ("ckl", [P, KLT, S], F32R), ("rl", [P, 3, S], F32)])
        assert e <= reg_b

        (uh, ul, wraw, wh, wl, ost), b1 = at(reg_b, [
            ("uh", [P, KT, S], F32R), ("ul", [P, KT, S], F32R), ("wraw", [P, 2, KT, P], F32),
            ("wh", [P, 2, KT, P], F32R), ("wl", [P, 2, KT, P], F32R), ("ost", [P, 2, S], F32)])
        (acc, wada, uf, vrow), e = at(b1, [("acc", [P, 3 * D], F32), ("wada", [P, 2, 3 * D], F32),
                                           ("uf", [P, 2, S], F32), ("vrow", [NVEC, P], F32)])
        assert e <= limit
        (qk, xr, rb, sqs, dtv, dtw), e = at(b1, [
            ("qk", [P, LAT, S], F32), ("xr", [P, 2, S + 4], F32), ("rb", [P, 2, S], F32),
            ("sqs", [P, S], F32), ("dtv", [P, S], F32), ("dtw", [P, S], F32)])
        assert e <= limit
        (stg, xdt, xdte, bdt, cbs, dec, exa, cts, state, yts, xd, cdv), e = at(b1, [
            ("stg", [P, 13, P], F32), ("xdt", [P, D], F32), ("xdte", [P, D], F32), ("bdt", [P, 3 * P], F32),
            ("cbs", [P, 2 * P], F32), ("dec", [P, 2, HB], F32), ("exa", [P, 2, HB], F32),
            ("cts", [P, 2, HB], F32), ("state", [P, D], F32), ("yts", [P, NST, P], F32),
            ("xd", [P, NST, P], F32), ("cdv", [P, 3, SSM_H], F32)])
        assert e <= limit

        hd = [at(reg_b + i * 28 * 1024, [
            (f"qnh{i}", [P, S], F32R), (f"qnl{i}", [P, S], F32R), (f"knh{i}", [P, S], F32R),
            (f"knl{i}", [P, S], F32R), (f"qr{i}", [P, S], F32R), (f"vh{i}", [P, CHUNKS, P], F32R),
            (f"vl{i}", [P, CHUNKS, P], F32R)])[0] for i in range(2)]
        (hwr, hwh, hwl, krh, krl, csn, pth, ptl, prob, zs, ob, ta, tb, sqa), e = at(reg_b + 56 * 1024, [
            ("hwr", [P, 1280], F32), ("hwh", [P, 1280], F32R), ("hwl", [P, 1280], F32R),
            ("krh", [P, S], F32R), ("krl", [P, S], F32R), ("csn", [P, S], F32),
            ("pth", [P, CHUNKS, HB], F32R), ("ptl", [P, CHUNKS, HB], F32R), ("prob", [P, 2, S], F32),
            ("zs", [P, S], F32), ("ob", [P, S], F32), ("ta", [P, S], F32), ("tb", [P, S], F32),
            ("sqa", [P, 2, S], F32)])
        assert e <= limit, (e, limit)
        posi = nc.alloc_sbuf_tensor_at("posi", [P, S], I32, offset=reg_b + 56 * 1024 + 4 * (3 * 1280 + 3 * S + 2 * CHUNKS * HB + 2 * S + S))

        (mxr, mxh, mxl, owr, owh, owl), e = at(reg_a, [
            ("mxr", [P, 2, S], F32), ("mxh", [P, 2, S], F32R), ("mxl", [P, 2, S], F32R),
            ("owr", [P, 2, HB], F32), ("owh", [P, 2, HB], F32R), ("owl", [P, 2, HB], F32R)])
        assert e <= reg_b
        (res, ev, lgb, lbb, rs, yn, tmpo), e = at(reg_b, [
            ("res", [P, CHUNKS, D], F32), ("ev", [P, CHUNKS, HB], F32), ("lgb", [P, D], F32),
            ("lbb", [P, D], F32), ("rs", [P, 2, S], F32), ("yn", [P, 2, D], F32), ("tmpo", [P, 2, HB], F32)])
        (bns,), e = at(e, [("bns", [P, CHUNKS, 24], F32)])

        bank = [ctx.enter_context(nc.psum_tensor(f"bank{i}", [P, 2, HB], F32)) for i in range(4)]

        def bk(i):
            return bank[i // 2][:, i % 2, :]

        small_in = sem("small_in")
        x_in = sem("x_in")
        ada_in = [sem("ada_in0"), sem("ada_in1")]
        consts = sem("consts")
        eps_ready = sem("eps_ready")
        ada_acc = sem("ada_acc")
        xt_ready = sem("xt_ready")
        uf_ready = sem("uf_ready")
        u_split = sem("u_split")
        mod_mm = sem("mod_mm")
        mod_ready = sem("mod_ready")
        w_in_sem = [sem("w_raw_in0"), sem("w_raw_in1")]
        w_hi = sem("w_hi")
        w_split = sem("w_split")
        proj_ready = sem("proj_ready")
        proj_evac = sem("proj_evac")
        dt_v = sem("dt_v")
        dt_abs = sem("dt_abs")
        dt_log = sem("dt_log")
        dt_done = sem("dt_done")
        conv_done = sem("conv_done")
        silu_done = sem("silu_done")
        sq_ready = sem("sq_ready")
        ss_mm = sem("ss_mm")
        root_ready = sem("root_ready")
        lat_ready = sem("lat_ready")
        z_out = [sem("z_out0"), sem("z_out1")]
        dvec = sem("dve_chain")
        poolc = sem("pool_chain")
        actc = sem("act_chain")
        stage_ready = sem("stage_ready")
        t_ready = sem("t_ready")
        bdt_ready = sem("bdt_ready")
        xdt_ready = sem("xdt_ready")
        acb_ready = sem("acb_ready")
        exa_ready = sem("exa_ready")
        arg_ready = sem("arg_ready")
        dec_ready = sem("dec_ready")
        g_ready = sem("g_ready")
        y_ready = sem("y_ready")
        y_evac = sem("y_evac")
        xd_ready = sem("xd_ready")
        state_decayed = sem("state_decayed")
        dte_ready = sem("dte_ready")
        xdte_ready = sem("xdte_ready")
        st_ready = sem("st_ready")
        state_new = sem("state_new")
        y_out = sem("y_out")

        rl_in = [sem(f"rl_in{i}") for i in range(3)]
        lat_split = sem("lat_split")
        rope_in = sem("rope_in")
        csn_ready = sem("csn_ready")
        csn_arg = sem("csn_arg")
        kr_t = sem("kr_t")
        kr_swapped = sem("kr_swapped")
        kr_sum = sem("kr_sum")
        krh_ready = sem("krh_ready")
        kr_ready = sem("kr_ready")
        hw_in = sem("hw_in")
        hw_split = sem("hw_split")
        hp_ready = sem("hp_ready")
        hp_hi = sem("hp_hi")
        hp_evac = sem("hp_evac")
        qr_swapped = sem("qr_swapped")
        qr_sum = sem("qr_sum")
        qr_hi = sem("qr_hi")
        qr_ready = sem("qr_ready")
        s_ready = sem("s_ready")
        s_max = sem("s_max")
        exp_done = sem("exp_done")
        p_ready = sem("p_ready")
        pt_ready = sem("pt_ready")
        pt_hi = sem("pt_hi")
        pt_split = sem("pt_split")
        pv_ready = sem("pv_ready")
        o_ready = sem("o_ready")
        o_out = sem("o_out")
        z_in = sem("z_in")
        y_in = sem("y_in")
        zy_in = sem("zy_in")
        yg_ready = sem("yg_ready")
        yg_out = sem("yg_out")
        sqa_ready = sem("sqa_ready")
        sr_mm = sem("sr_mm")
        sr_root = sem("sr_root")

        mx_in = [sem("mx_in0"), sem("mx_in1")]
        mx_norm = sem("mx_norm")
        ow_in = [sem("ow_in0"), sem("ow_in1")]
        e_hi = sem("e_hi")
        e_split = sem("e_split")
        o_mm = sem("o_mm")
        bank_done = sem("bank_done")
        ev_ready = sem("ev_ready")
        res_in = sem("res_in")
        ln_in = sem("ln_in")
        rs_ready = sem("rs_ready")
        norm_ready = sem("norm_ready")
        root_ln = sem("root_ln")
        stat_ready = sem("stat_ready")
        var_ready = sem("var_ready")
        gain_ready = sem("gain_ready")
        y_final = sem("y_final")
        done = [sem("out_stored0"), sem("out_stored1")]

        block = ctx.enter_context(nc.Block())

        class Chain:

            def __init__(self, eng, s):
                self.eng, self.s, self.n, self.base = eng, s, 0, 0

            def link(self, ins):
                ins.then_inc(self.s, 1)
                self.n += 1
                self.eng.wait_ge(self.s, self.base + self.n)

            def loop(self, i, per):
                self.start, self.per = self.n, per
                self.base, self.n = self.start + per * i, 0

            def end(self, count):
                assert self.n == self.per, (self.n, self.per)
                self.base, self.n = 0, self.start + self.per * count

        w3 = w_in[0].rearrange("(k p) n -> p k n", p=P)

        @block.sync
        def _(sp):
            sp.dma_start(ccol[:], c[0].rearrange("(p t) -> p t", t=KT)).then_inc(small_in, 16)
            for dst, src in (
                (vrow[0:24], b_ada[0].rearrange("(t p) -> t p", p=P)),
                (vrow[24:72], conv_w[0].rearrange("k (j p) -> (k j) p", p=P)),
                (vrow[72:84], conv_b[0].rearrange("(t p) -> t p", p=P)),
                (vrow[84:87], qg[0].rearrange("(t p) -> t p", p=P)),
                (vrow[87:89], kvg[0].rearrange("(t p) -> t p", p=P)),
                (vrow[89:97], ssmg[0].rearrange("(t p) -> t p", p=P)),
                (gate_b[:], b_ada[0, 2 * D:3 * D].partition_broadcast(P)),
                (dsr[:], d_skip[0].partition_broadcast(P)),
                (dtb[DT0:DT0 + 16], dt_bias[0].rearrange("(h a) -> h a", a=1)),
                (alg[DT0:DT0 + 16], a_log[0].rearrange("(h a) -> h a", a=1)),
                (rcst[:], ropec),
            ):
                sp.dma_start(dst, src).then_inc(small_in, 16)
            ada = w_ada[0].rearrange("(p t) n -> p t n", t=KT)
            for t in range(KT):
                if t >= 2:
                    sp.wait_ge(ada_acc, t - 1)
                sp.dma_start(wada[:, t % 2, :], ada[:, t, :]).then_inc(ada_in[t % 2], 16)
                sp.dma_start(xin[:, t, :], x[0, t * P:(t + 1) * P, :]).then_inc(x_in, 16)

            def address(v):
                return v if isinstance(v, int) else sp.snap(v)

            def load_tile(p, col, wait):
                src = w3[:, :, bass.ds(address(col), P)]
                if wait is not None:
                    sp.wait_ge(w_split, wait)
                sp.dma_start(wraw[:, p], src).then_inc(w_in_sem[p], 16)

            def store_z(tile, p, i):
                dst = scr[bass.ds(address(i), 1)]
                sp.wait_ge(proj_evac, tile)
                sp.dma_start(dst, ost[:, p, :]).then_inc(z_out[p], 16)

            def store_y(i):
                col = address(i * P)
                sp.wait_ge(y_evac, 4 * i + 4)
                sp.dma_start(scy[:, :, bass.ds(col, P)].rearrange("j p l -> p j l"), yts[:]).then_inc(y_out, 16)

            sp.dma_start(wraw[:, 0, :, 0:ROPE], w3[:, :, W_KV_ROPE:W_KV_ROPE + ROPE]).then_inc(w_in_sem[0], 16)
            sp.dma_start(wraw[:, 0, :, ROPE:ROPE + 16], w3[:, :, W_DT:W_DT + 16]).then_inc(w_in_sem[0], 16)
            load_tile(1, 0, None)
            for t in range(2, 6):
                load_tile(t % 2, (t - 1) * P, t - 1)
            sp.wait_ge(proj_evac, 2)
            for q in range(2):
                sp.dma_start(scr[0, 32 * q:32 * q + 32, :], ost[32 * q:32 * q + 32, 0, :]).then_inc(z_out[q], 16)
            with sp.Fori(0, 4) as j:
                for p in range(2):
                    load_tile(p, W_XBC + (2 * j + p) * P, 2 * j + p + 5)
            sp.wait_ge(lat_ready, LAT)
            sp.dma_start(scr[1:6].rearrange("t p s -> p t s"), qk[:]).then_inc(y_out, 16)
            with sp.Fori(4, 6) as j:
                for p in range(2):
                    load_tile(p, W_XBC + (2 * j + p) * P, 2 * j + p + 5)
            load_tile(0, W_ZATT, 17)
            load_tile(1, W_ZSSM, 18)
            with sp.Fori(0, CHUNKS - 1) as i:
                load_tile(0, W_ZATT + (i + 1) * P, 2 * i + 19)
                load_tile(1, W_ZSSM + (i + 1) * P, 2 * i + 20)
                store_z(4 * i + 38, 0, i + Z_ATT0)
                store_z(4 * i + 40, 1, i + Z_SSM0)
                store_y(i)
            i = CHUNKS - 1
            sp.wait_ge(stage_ready, CHUNKS)
            sp.wait_ge(y_out, 16)
            for t in range(3):
                sp.dma_start(rl[:, t, :], scr[1 + t]).then_inc(rl_in[t], 16)
            for t in range(3, LAT):
                sp.wait_ge(lat_split, t - 2)
                sp.dma_start(rl[:, t % 3, :], scr[1 + t]).then_inc(rl_in[t % 3], 16)
            store_z(4 * i + 38, 0, i + Z_ATT0)
            store_z(4 * i + 40, 1, i + Z_SSM0)
            store_y(i)
            sp.wait_ge(z_out[0], 16 * 9)
            sp.wait_ge(z_out[1], 16 * 9)
            sp.wait_ge(y_out, 16 * CHUNKS + 16)
            sp.wait_ge(proj_ready, 68)
            sp.wait_ge(state_new, CHUNKS + 1)

            def head_weights(h, wait=None):
                q0, q1, q2 = (address(h * QW + o) for o in (0, 160, 128))
                kv0 = address(h * 256)
                if wait is not None:
                    sp.wait_ge(hw_split, wait)
                q = w_qb[0].rearrange("(k p) n -> p k n", p=P)
                kv = w_kvb[0].rearrange("(k p) n -> p k n", p=P)
                qv = hwr[:, 0:768].rearrange("p (k n) -> p k n", n=256)
                sp.dma_start(qv[:, :, 0:QW], q[:, :, bass.ds(q0, QW)]).then_inc(hw_in, 16)
                sp.dma_start(qv[:, :, 192:224], q[:, :, bass.ds(q1, 32)]).then_inc(hw_in, 16)
                sp.dma_start(qv[:, :, 224:256], q[:, :, bass.ds(q2, 32)]).then_inc(hw_in, 16)
                sp.dma_start(hwr[:, 768:1280].rearrange("p (k n) -> p k n", n=256),
                             kv[:, :, bass.ds(kv0, 256)]).then_inc(hw_in, 16)

            head_weights(0)
            sp.dma_start(ta[0:ROPE], scr[0, 0:ROPE, :]).then_inc(rope_in, 16)
            sp.dma_start(ta[64:96], scr[0, 32:64, :]).then_inc(rope_in, 16)
            sp.dma_start(ta[96:128], scr[0, 0:32, :]).then_inc(rope_in, 16)
            sp.dma_start(posi[:], pos[0].partition_broadcast(P)).then_inc(rope_in, 16)
            sp.wait_ge(kr_t, 1)
            sp.dma_start(tb[0:64], ta[64:128]).then_inc(kr_swapped, 16)
            sp.dma_start(tb[64:128], ta[0:64]).then_inc(kr_swapped, 16)

            def swap_q(h):
                sp.wait_ge(hp_evac, 10 * h + 4)
                sp.dma_start(tb[0:64], ta[64:128]).then_inc(qr_swapped, 16)
                sp.dma_start(tb[64:128], ta[0:64]).then_inc(qr_swapped, 16)

            swap_q(0)
            sp.wait_ge(lat_split, LAT)

            def head_io(h, fill):
                if fill and not (isinstance(h, int) and h == HEADS - 2):
                    head_weights(h + 2, h + 2)
                z_att, z_ssm, head = address(h + Z_ATT0), address(h + Z_SSM0), address(h)
                if not isinstance(h, int) or h > 0:
                    sp.wait_ge(o_ready, 2 * h)
                sp.dma_start(zs[:], scr[bass.ds(z_att, 1)]).then_inc(z_in, 16)
                if not isinstance(h, int) or h > 0:
                    sp.wait_ge(yg_out, 16 * h)
                    sp.wait_ge(sqa_ready, h)
                sp.dma_start(rl[:, 0, :], scr[bass.ds(z_ssm, 1)]).then_inc(zy_in, 16)
                sp.dma_start(rl[:, 1, :], scy[bass.ds(head, 1)]).then_inc(y_in, 16)
                if fill:
                    swap_q(h + 1)
                sp.wait_ge(yg_ready, h + 1)
                sp.dma_start(scg[bass.ds(head, 1)], rl[:, 1, :]).then_inc(yg_out, 16)
                sp.wait_ge(o_ready, 2 * h + 2)
                sp.dma_start(sco[bass.ds(head, 1)], ob[:]).then_inc(o_out, 16)

            head_weights(1, 1)
            head_io(0, True)
            with sp.Fori(1, HEADS - 2) as h:
                head_io(h, True)
            head_io(HEADS - 2, True)
            head_io(HEADS - 1, False)

            sp.wait_ge(o_out, 16 * HEADS)
            sp.wait_ge(yg_out, 16 * HEADS)
            sp.wait_ge(pv_ready, 2 * HEADS)
            sp.wait_ge(sr_mm, 1)
            sp.dma_start(lgb[:], ln_g[0].partition_broadcast(P)).then_inc(ln_in, 16)
            sp.dma_start(lbb[:], ln_b[0].partition_broadcast(P)).then_inc(ln_in, 16)
            sp.dma_start(res[:], x[0].rearrange("(s p) d -> p s d", p=P)).then_inc(res_in, 16)
            for half in range(2):
                for kt in range(16):
                    n = half * 16 + kt
                    p = n % 2
                    if n >= 2:
                        sp.wait_ge(e_split, 2 * n - 2)
                    src = sco[kt] if kt < 8 else scg[kt - 8]
                    sp.dma_start(mxr[:, p, :], src).then_inc(mx_in[p], 16)
                    sp.dma_start(owr[:, p, :], w_out[0, kt * P:(kt + 1) * P, half * HB:(half + 1) * HB]
                                 ).then_inc(ow_in[p], 16)
            for s in range(CHUNKS):
                sp.wait_ge(y_final, s + 1)
                sp.dma_start(out[0, s * P:(s + 1) * P, :], yn[:, s % 2, :]).then_inc(done[s % 2], 16)
            for q in range(2):
                sp.wait_ge(done[q], 16 * CHUNKS // 2)

        @block.gpsimd
        def _(pool):
            ch = Chain(pool, poolc)
            ch.link(pool.memset(ident[:], 0.0))
            pool.affine_select(ident[:], ident[:], pattern=[[-1, P]], compare_op=ALU.not_equal, fill=1.0,
                               base=0, channel_multiplier=1).then_inc(consts, 1)
            ch.link(pool.memset(mask_qk[:], 0.0))
            pool.affine_select(mask_qk[:], mask_qk[:], pattern=[[-1, P]], compare_op=ALU.is_ge, fill=NEG,
                               base=0, channel_multiplier=1).then_inc(consts, 1)
            ch.link(pool.memset(mask_ls[:], 0.0))
            pool.affine_select(mask_ls[:], mask_ls[:], pattern=[[1, P]], compare_op=ALU.is_ge, fill=NEG,
                               base=0, channel_multiplier=-1).then_inc(consts, 1)
            pool.memset(ones[:], 1.0).then_inc(consts, 1)

            def split_tile(p, tile, cols=P):
                pool.wait_ge(w_hi, tile + 1)
                pool.tensor_tensor(wl[:, p, :, 0:cols], wraw[:, p, :, 0:cols], wh[:, p, :, 0:cols].bitcast(F32),
                                   ALU.subtract).then_inc(w_split, 1)

            pool.wait_ge(small_in, 16 * 12)
            for q in range(2):
                ch.link(pool.tensor_copy(dsk[64 * q:64 * q + 64, :], dsr[64 * q:64 * q + 64, q:SSM_H:2]))
            split_tile(0, 0, ROPE + 16)
            split_tile(1, 1)
            with pool.Fori(1, 9) as j:
                for p in range(2):
                    split_tile(p, 2 * j + p)
            with pool.Fori(0, CHUNKS) as i:
                split_tile(0, 2 * i + 18)
                pool.wait_ge(stage_ready, i + 1)
                pool.tensor_tensor(xd[:], stg[:, 0:NST, :], dsk[:].unsqueeze(2).to_broadcast([P, NST, P]),
                                   ALU.mult).then_inc(xd_ready, 1)
                split_tile(1, 2 * i + 19)
            for t in range(LAT):
                hi = qlh[:, t, :] if t < QLT else ckh[:, t - QLT, :]
                lo = qll[:, t, :] if t < QLT else ckl[:, t - QLT, :]
                pool.wait_ge(rl_in[t % 3], 16 * (t // 3 + 1))
                ch.link(pool.tensor_copy(hi, rl[:, t % 3, :]))
                pool.tensor_tensor(lo, rl[:, t % 3, :], hi.bitcast(F32), ALU.subtract).then_inc(lat_split, 1)

            def split_head(h):
                pool.wait_ge(w_hi, h + 35)
                pool.tensor_tensor(hwl[:], hwr[:], hwh[:].bitcast(F32), ALU.subtract).then_inc(hw_split, 1)

            split_head(0)

            def ssm_tile(h, g, first):
                pool.wait_ge(y_in, 16 * h + 16)
                pool.wait_ge(zy_in, 16 * h + 16)
                pool.tensor_tensor(rl[:, 1, :], rl[:, 1, :], rl[:, 0, :], ALU.mult).then_inc(yg_ready, 1)
                pool.wait_ge(yg_ready, h + 1)
                sq = sqa[:, g, :] if first else rl[:, 2, :]
                m = pool.tensor_tensor(sq, rl[:, 1, :], rl[:, 1, :], ALU.mult)
                if first:
                    m.then_inc(sqa_ready, 1)
                else:
                    ch.link(m)
                    pool.wait_ge(sqa_ready, h)
                    pool.tensor_tensor(sqa[:, g, :], sqa[:, g, :], rl[:, 2, :], ALU.add).then_inc(sqa_ready, 1)

            for g in range(2):
                split_head(4 * g + 1)
                ssm_tile(4 * g, g, True)
                ch.loop(0, 1)
                last = 4 if g == 0 else 3
                with pool.Fori(1, last) as k:
                    ch.base = ch.start + (k - 1)
                    ch.n = 0
                    split_head(4 * g + k + 1)
                    ssm_tile(4 * g + k, g, False)
                ch.end(last - 1)
                if g == 1:
                    ssm_tile(7, g, False)
            pool.wait_ge(ln_in, 32)
            for s in range(CHUNKS):
                pool.wait_ge(norm_ready, s + 1)
                pool.tensor_tensor(yn[:, s % 2, :], yn[:, s % 2, :], lgb[:], ALU.mult).then_inc(gain_ready, 1)
                pool.wait_ge(gain_ready, s + 1)
                pool.tensor_tensor(yn[:, s % 2, :], yn[:, s % 2, :], lbb[:], ALU.add).then_inc(y_final, 1)

        @block.tensor
        def _(pe):
            def three(dst, ah, al, bh, bl, start, stop):
                pe.matmul(dst, ah, bh, start=start, stop=False)
                pe.matmul(dst, ah, bl, start=False, stop=False)
                return pe.matmul(dst, al, bh, start=False, stop=stop)

            pe.wait_ge(consts, 4)
            pe.wait_ge(small_in, 16 * 12)
            pe.transpose(bk(3)[:, 0:NVEC], vrow[:], ident[0:NVEC, 0:NVEC]).then_inc(mod_mm, 1)

            def x_transposes(k):
                if k >= 2:
                    pe.wait_ge(uf_ready, k - 1)
                for s in range(CHUNKS):
                    m = pe.transpose(bk(4 + 2 * (k % 2) + s // 4)[:, (s % 4) * P:(s % 4 + 1) * P],
                                     xin[:, s, k * P:(k + 1) * P], ident[:])
                m.then_inc(xt_ready, 1)

            pe.wait_ge(x_in, 16 * CHUNKS)
            x_transposes(0)
            x_transposes(1)
            pe.wait_ge(ada_acc, KT)
            for m in range(16):
                mm = pe.matmul(bk(0)[:, m:m + 1], acc[:, m * P:(m + 1) * P], ones[:, 0:1], start=True, stop=True)
            for n in range(2):
                mm = pe.matmul(bk(1 + n), ones[:], acc[:, 2 * D + n * HB:2 * D + (n + 1) * HB], start=True, stop=True)
            mm.then_inc(mod_mm, 1)

            def proj_mm(p, n, k, start, stop, cols=P):
                r = slice(n * HB, (n + 1) * HB)
                return three(bk(2 * p + n)[0:cols], wh[:, p, k, 0:cols], wl[:, p, k, 0:cols],
                             uh[:, k, r], ul[:, k, r], start, stop)

            pe.wait_ge(mod_ready, 2)
            pe.wait_ge(w_split, 2)
            for k in range(KT):
                pe.wait_ge(u_split, k + 1)
                for p in range(2):
                    for n in range(NHALF):
                        mm = proj_mm(p, n, k, k == 0, k == KT - 1, ROPE + 16 if p == 0 else P)
                        if k == KT - 1:
                            mm.then_inc(proj_ready, 1)
                if k + 2 < KT:
                    x_transposes(k + 2)

            def proj_tile(p, tile):
                pe.wait_ge(w_split, tile + 1)
                for n in range(NHALF):
                    pe.wait_ge(proj_evac, 2 * tile + n - 3)
                    for k in range(KT):
                        mm = proj_mm(p, n, k, k == 0, k == KT - 1)
                    mm.then_inc(proj_ready, 1)

            with pe.Fori(1, 4) as j:
                for p in range(2):
                    proj_tile(p, 2 * j + p)
            pe.wait_ge(sq_ready, 1)
            for g in range(2):
                for n in range(2):
                    mm = pe.matmul(bk(4 + 2 * g + n), ones[:], rb[:, g, n * HB:(n + 1) * HB], start=True, stop=True)
            mm.then_inc(ss_mm, 1)
            with pe.Fori(4, 9) as j:
                for p in range(2):
                    proj_tile(p, 2 * j + p)

            def proj_part(p, n, part, tile):
                if part == 0:
                    if n == 0:
                        pe.wait_ge(w_split, tile + 1)
                    pe.wait_ge(proj_evac, 2 * tile + n - 3)
                steps = [(k, q) for k in range(KT) for q in range(3)][8 * part:8 * part + 8]
                for k, q in steps:
                    a = wl if q == 2 else wh
                    b = ul if q == 1 else uh
                    mm = pe.matmul(bk(2 * p + n), a[:, p, k, :], b[:, k, n * HB:(n + 1) * HB],
                                   start=(k == 0 and q == 0), stop=(k == KT - 1 and q == 2))
                if part == 2:
                    mm.then_inc(proj_ready, 1)

            def acum_rows(r, c):
                if r == 0:
                    pe.wait_ge(xdt_ready, c + 1)
                if r >= 2:
                    pe.wait_ge(arg_ready, 4 * c + r - 1)
                for i in range(4):
                    j = AC0 + 4 * r + i
                    mm = pe.matmul(bk(4 + r % 2)[:, i * P:(i + 1) * P], ident[:, j:j + 1].to_broadcast([P, P]),
                                   stg[:, 12, :], start=True, stop=True)
                mm.then_inc(acb_ready, 1)

            def y_round(r, c):
                pe.wait_ge(g_ready, 4 * c + r + 1)
                if r >= 2:
                    pe.wait_ge(y_evac, 4 * c + r - 1)
                for i in range(2):
                    j = 2 * r + i
                    d = bk(6 + r % 2)[:, i * 256:(i + 1) * 256]
                    pe.matmul(d, xdt[:, j * P:(j + 1) * P], dec[:, r % 2, i * 256:(i + 1) * 256], start=True, stop=False)
                    mm = pe.matmul(d, state[:, j * P:(j + 1) * P], cts[:, r % 2, i * 256:(i + 1) * 256],
                                   start=False, stop=True)
                mm.then_inc(y_ready, 1)

            with pe.Fori(0, CHUNKS) as c:
                parts = [(p, n, part) for p in range(2) for n in range(2) for part in range(3)]

                def fill(count):
                    for _ in range(count):
                        p, n, part = parts.pop(0)
                        proj_part(p, n, part, 2 * c + 18 + p)

                fill(1)
                pe.wait_ge(stage_ready, c + 1)
                pe.wait_ge(state_new, c + 1)
                for j in range(8):
                    pe.transpose(bk(4 + j // 4)[:, (j % 4) * P:(j % 4 + 1) * P], stg[:, j, :], ident[:])
                for q, j in enumerate((8, 9, 12)):
                    pe.transpose(bk(6)[:, q * P:(q + 1) * P], stg[:, j, :], ident[:])
                for g in range(2):
                    mm = pe.matmul(bk(7)[:, g * P:(g + 1) * P], stg[:, 8 + g, :], stg[:, 10 + g, :], start=True, stop=True)
                mm.then_inc(t_ready, 1)
                fill(2)
                acum_rows(0, c)
                fill(1)
                acum_rows(1, c)
                fill(2)
                y_round(0, c)
                acum_rows(2, c)
                fill(2)
                y_round(1, c)
                acum_rows(3, c)
                fill(2)
                y_round(2, c)
                fill(1)
                y_round(3, c)
                fill(1)
                pe.wait_ge(xdte_ready, c + 1)
                for g in range(2):
                    mm = pe.matmul(bk(4 + g), bdt[:, g * P:(g + 1) * P], xdte[:, g * HB:(g + 1) * HB],
                                   start=True, stop=True)
                mm.then_inc(st_ready, 1)

            pe.wait_ge(lat_split, LAT)
            pe.wait_ge(proj_evac, 68)
            pe.wait_ge(state_new, CHUNKS + 1)
            pe.wait_ge(y_evac, 4 * CHUNKS)
            wq = [t[:, 0:768].rearrange("p (k n) -> p k n", n=256) for t in (hwh, hwl)]
            wk = [t[:, 768:1280].rearrange("p (k n) -> p k n", n=256) for t in (hwh, hwl)]

            def head_proj(u, b, h):
                if u == 0:
                    pe.wait_ge(hw_split, h + 1)
                first = isinstance(h, int) and h == 0 and u == 0
                if not first:
                    pe.wait_ge(hp_evac, 10 * h + u)
                n = u % 2
                r = slice(n * HB, (n + 1) * HB)
                if u < 4:
                    m0 = P * (u // 2)
                    for k in range(QLT):
                        mm = three(bk(7), wq[0][:, k, m0:m0 + P], wq[1][:, k, m0:m0 + P], qlh[:, k, r], qll[:, k, r],
                                   k == 0, k == QLT - 1)
                elif u < 8:
                    m0 = P * (u // 2 - 2)
                    for k in range(KLT):
                        mm = three(bk(7), wk[0][:, k, m0:m0 + P], wk[1][:, k, m0:m0 + P], ckh[:, k, r], ckl[:, k, r],
                                   k == 0, k == KLT - 1)
                else:
                    for j in range(4):
                        t = 4 * (u - 8) + j
                        mm = pe.transpose(bk(7)[:, j * P:(j + 1) * P], tb[:, t * P:(t + 1) * P], ident[:])
                mm.then_inc(hp_ready, 1)

            def scores(i, b, h):
                qnh, qnl, knh, knl, qr, _, _ = hd[b]
                if i == 0:
                    pe.wait_ge(qr_ready, h + 1)
                    pe.wait_ge(hp_evac, 10 * h + 10)
                first = isinstance(h, int) and h == 0 and i < 2
                if not first:
                    pe.wait_ge(exp_done, 8 * h + i - 1)
                q = slice(i * P, (i + 1) * P)
                end = (i + 1) * P
                for k0 in range(0, end, HB):
                    n = max(256, min(HB, end - k0))
                    d = bank[i % 2][:, k0 // HB, 0:n]
                    k = slice(k0, k0 + n)
                    pe.matmul(d, qnh[:, q], knh[:, k], start=True, stop=False)
                    pe.matmul(d, qnh[:, q], knl[:, k], start=False, stop=False)
                    pe.matmul(d, qnl[:, q], knh[:, k], start=False, stop=False)
                    pe.matmul(d, qr[:, q], krh[:, k], start=False, stop=False)
                    mm = pe.matmul(d, qr[:, q], krl[:, k], start=False, stop=True)
                mm.then_inc(s_ready, 1)

            batch = [0]

            def turn_probs(i, h):
                pe.wait_ge(p_ready, 8 * h + i + 1)
                for t0 in range(0, i + 1, 4):
                    n = batch[0] % 12
                    batch[0] += 1
                    if not (isinstance(h, int) and h == 0 and n < 2):
                        pe.wait_ge(pt_split, 12 * h + n - 1)
                    for t in range(t0, min(i + 1, t0 + 4)):
                        mm = pe.transpose(bk(4 + n % 2)[:, (t - t0) * P:(t - t0 + 1) * P],
                                          prob[:, i % 2, t * P:(t + 1) * P], ident[:])
                    mm.then_inc(pt_ready, 1)

            def values(g, b, h):
                vh, vl = hd[b][5:]
                pe.wait_ge(pt_split, 12 * h + (4, 12)[g])
                if not (isinstance(h, int) and h == 0 and g == 0):
                    pe.wait_ge(o_ready, 2 * h + g)
                last = 4 * g + 3
                for t in range(last + 1):
                    c0 = max(0, t - 4 * g) * P
                    mm = three(bk(6)[:, c0:HB], vh[:, t, :], vl[:, t, :], pth[:, t, c0:HB], ptl[:, t, c0:HB],
                               t == 0, t == last)
                mm.then_inc(pv_ready, 1)

            def head(h, b, fill):
                scores(0, b, h)
                scores(1, b, h)
                for i in range(8):
                    if i + 2 < 8:
                        scores(i + 2, b, h)
                    if fill:
                        head_proj(i, 1 - b, h + 1)
                    if i == 4:
                        values(0, b, h)
                    turn_probs(i, h)
                if fill:
                    head_proj(8, 1 - b, h + 1)
                    head_proj(9, 1 - b, h + 1)
                values(1, b, h)

            for u in range(10):
                if u == 8:
                    pe.wait_ge(hp_evac, 8)
                head_proj(u, 0, 0)
            pe.wait_ge(kr_ready, 1)
            head(0, 0, True)
            with pe.Fori(0, 3) as hp:
                head(2 * hp + 1, 1, True)
                head(2 * hp + 2, 0, True)
            head(7, 1, False)
            pe.wait_ge(sqa_ready, 8)
            pe.wait_ge(exp_done, 64)
            for g in range(2):
                for n in range(2):
                    mm = pe.matmul(bk(2 * g + n), ones[:], sqa[:, g, n * HB:(n + 1) * HB], start=True, stop=True)
            mm.then_inc(sr_mm, 1)

            for half in range(2):
                for kt in range(16):
                    n = half * 16 + kt
                    p = n % 2
                    pe.wait_ge(e_split, 2 * n + 2)
                    for s in range(CHUNKS):
                        if kt == 0:
                            if half == 0 and s == 0:
                                pe.wait_ge(sr_root, 1)
                                pe.wait_ge(pt_split, 96)
                                pe.wait_ge(o_ready, 16)
                            if half == 1:
                                pe.wait_ge(ev_ready, s + 1)
                        q = slice(s * P, (s + 1) * P)
                        mm = three(bk(s), mxh[:, p, q], mxl[:, p, q], owh[:, p, :], owl[:, p, :], kt == 0, kt == 15)
                        if kt == 15:
                            mm.then_inc(bank_done, 1)
                        elif s == CHUNKS - 1:
                            mm.then_inc(o_mm, 1)

        @block.scalar
        def _(act):
            ch = Chain(act, actc)
            act.wait_ge(w_in_sem[0], 32)
            act.activation(wh[:, 0, :, 0:ROPE + 16], wraw[:, 0, :, 0:ROPE + 16], ACT.Copy).then_inc(w_hi, 1)
            act.wait_ge(w_in_sem[1], 16)
            act.activation(wh[:, 1], wraw[:, 1], ACT.Copy).then_inc(w_hi, 1)
            act.wait_ge(small_in, 16 * 12)
            act.activation(small[DT0:DT0 + 16, 0:1], alg[DT0:DT0 + 16], ACT.Exp).then_inc(mod_ready, 1)
            act.wait_ge(ada_acc, KT + 1)
            for k in range(KT):
                act.wait_ge(xt_ready, k + 1)
                if k >= 2:
                    act.wait_ge(u_split, k - 1)
                act.activation(uf[:, k % 2, :], bank[2 + k % 2][:].rearrange("p a b -> p (a b)"), ACT.Identity,
                               bias=modc[:, k:k + 1], scale=modc[:, 8 + k:9 + k]).then_inc(uf_ready, 1)
            for n in range(NHALF):
                r = slice(n * HB, (n + 1) * HB)
                act.wait_ge(proj_ready, 4 * 0 + 1 + n)
                act.activation(dtv[DT0:DT0 + 16, r], bk(n)[DT0:DT0 + 16], ACT.Identity,
                               bias=dtb[DT0:DT0 + 16]).then_inc(dt_v, 1)
                act.activation(ost[0:ROPE, 0, r], bk(n)[0:ROPE], ACT.Copy).then_inc(proj_evac, 1)

            def high(p, arrived, tile, cols=P):
                act.wait_ge(w_in_sem[p], arrived)
                if not isinstance(tile, int) or tile >= 2:
                    act.wait_ge(proj_ready, 2 * tile - 2)
                act.activation(wh[:, p, :, 0:cols], wraw[:, p, :, 0:cols], ACT.Copy).then_inc(w_hi, 1)

            def evac(tile, p, dst):
                for n in range(NHALF):
                    act.wait_ge(proj_ready, 2 * tile + n + 1)
                    act.activation(dst[:, n * HB:(n + 1) * HB], bk(2 * p + n), ACT.Copy).then_inc(proj_evac, 1)

            high(0, 48, 2)
            evac(1, 1, qk[:, 0, :])
            high(1, 32, 3)
            act.wait_ge(dt_abs, 1)
            ch.link(act.activation(dtw[DT0:DT0 + 16], dtw[DT0:DT0 + 16], ACT.Exp))
            act.activation(dtw[DT0:DT0 + 16], dtw[DT0:DT0 + 16], ACT.Ln, bias=1.0).then_inc(dt_log, 1)
            for t in range(2, 6):
                evac(t, t % 2, qk[:, t - 1, :])
                high(t % 2, 16 * (t // 2 + 2) + (16 if t % 2 == 0 else 0), t + 2)

            def conv_tile(j, p, free, before):
                if free:
                    act.wait_ge(conv_done, j - 1)
                evac(j + 6, p, xr[:, p, 3:3 + S])
                high(p, 16 * (j // 2 + 5) + (16 if p == 0 else 0), j + 8)
                if before is not None:
                    act.wait_ge(conv_done, j)
                    act.activation(cx[:, before, :], cx[:, before, :], ACT.Silu).then_inc(silu_done, 1)

            conv_tile(0, 0, False, None)
            conv_tile(1, 1, False, 0)
            act.wait_ge(ss_mm, 1)
            for g in range(2):
                act.activation(rb[:, g, :], bank[2 + g][:].rearrange("p a b -> p (a b)"), ACT.Sqrt,
                               bias=rcst[:, 3:4], scale=1.0 / (384, 256)[g]).then_inc(root_ready, 1)
            with act.Fori(1, 6) as j2:
                for p in range(2):
                    j = 2 * j2 + p
                    act.wait_ge(conv_done, j - 1)
                    evac(j + 6, p, xr[:, p, 3:3 + S])
                    high(p, 16 * j2 + (96 if p == 0 else 80), j + 8)
                    act.wait_ge(conv_done, j)
                    v = cx[:, bass.ds(j - 1, 1), :]
                    act.activation(v, v, ACT.Silu).then_inc(silu_done, 1)
            act.wait_ge(conv_done, CONVT)
            act.activation(cx[:, CONVT - 1, :], cx[:, CONVT - 1, :], ACT.Silu).then_inc(silu_done, 1)

            def z_half(i, p, n):
                act.wait_ge(proj_ready, 4 * i + 36 + 2 * p + n + 1)
                if n == 0:
                    act.wait_ge(z_out[p], 16 * i + 16)
                act.activation(ost[:, p, n * HB:(n + 1) * HB], bk(2 * p + n), ACT.Silu).then_inc(proj_evac, 1)

            def exp_rows(r, c):
                act.wait_ge(acb_ready, 4 * c + r + 1)
                act.activation(exa[:, r % 2, :], bk(4 + r % 2), ACT.Exp).then_inc(exa_ready, 1)

            def exp_decay(r, c):
                act.wait_ge(arg_ready, 4 * c + r + 1)
                act.activation(dec[:, r % 2, :], dec[:, r % 2, :], ACT.Exp).then_inc(dec_ready, 1)

            def chunk(c, more):
                exp_rows(0, c)
                exp_decay(0, c)
                exp_rows(1, c)
                exp_decay(1, c)
                act.wait_ge(g_ready, 4 * c + 1)
                exp_rows(2, c)
                exp_decay(2, c)
                z_half(c, 0, 0)
                z_half(c, 0, 1)
                if more:
                    high(0, 16 * c + 192, 2 * c + 20)
                act.wait_ge(g_ready, 4 * c + 2)
                exp_rows(3, c)
                exp_decay(3, c)
                act.wait_ge(arg_ready, 4 * c + 4)
                act.activation(cdv[:, 2, :], cdv[:, 1, :], ACT.Exp).then_inc(dte_ready, 1)
                z_half(c, 1, 0)
                z_half(c, 1, 1)
                if more:
                    high(1, 16 * c + 176, 2 * c + 21)

            with act.Fori(0, CHUNKS - 1) as c:
                chunk(c, True)
            chunk(CHUNKS - 1, False)

            act.wait_ge(hw_in, 64)
            act.activation(hwh[:], hwr[:], ACT.Copy).then_inc(w_hi, 1)
            act.wait_ge(csn_arg, 1)
            act.activation(csn[:], csn[:], ACT.Sin).then_inc(csn_ready, 1)

            def head_high(h):
                act.wait_ge(hw_in, 64 * h + 64)
                if not isinstance(h, int) or h > 0:
                    act.wait_ge(hp_ready, 10 * h - 2)
                act.activation(hwh[:], hwr[:], ACT.Copy).then_inc(w_hi, 1)

            def hi_part(u, b, h):
                qnh, _, knh, _, _, vh, _ = hd[b]
                act.wait_ge(hp_ready, 10 * h + u + 1)
                n = u % 2
                r = slice(n * HB, (n + 1) * HB)
                if u < 2:
                    act.activation(qnh[:, r], bk(7), ACT.Copy).then_inc(hp_hi, 1)
                elif u in (4, 5):
                    act.activation(knh[:, r], bk(7), ACT.Copy).then_inc(hp_hi, 1)
                elif u in (6, 7):
                    if u == 6:
                        act.wait_ge(qr_sum, h + 1)
                    act.activation(tb[:, r], bk(7), ACT.Copy).then_inc(hp_evac, 1)
                elif u >= 8:
                    act.activation(vh[:, 4 * (u - 8):4 * (u - 8) + 4, :], bk(7).rearrange("p (t v) -> p t v", v=P),
                                   ACT.Copy).then_inc(hp_hi, 1)

            def qr_high(b, h):
                act.wait_ge(qr_sum, h + 1)
                act.activation(hd[b][4][:], ta[:], ACT.Copy).then_inc(qr_hi, 1)

            def probs(i, b, h):
                act.wait_ge(s_max, 8 * h + i + 1)
                if not (isinstance(h, int) and h == 0 and i < 2):
                    act.wait_ge(pt_ready, 12 * h + (-2, 0, 1, 2, 3, 4, 6, 8)[i])
                n = (i + 1) * P
                act.activation(prob[:, i % 2, 0:n], bank[i % 2][:].rearrange("p a b -> p (a b)")[:, 0:n], ACT.Exp,
                               bias=small[:, 8 + i % 2:9 + i % 2], scale=SCALE,
                               accum_out=small[:, 12 + i % 2:13 + i % 2]).then_inc(exp_done, 1)

            def turned_high(i, h):
                for t0 in range(0, i + 1, 4):
                    n = batch[0] % 12
                    batch[0] += 1
                    w = min(i + 1, t0 + 4) - t0
                    act.wait_ge(pt_ready, 12 * h + n + 1)
                    if n == 4:
                        act.wait_ge(pv_ready, 2 * h + 1)
                    if n == 0 and not (isinstance(h, int) and h == 0):
                        act.wait_ge(pv_ready, 2 * h)
                    act.activation(pth[:, t0:t0 + w, (i % 4) * P:(i % 4 + 1) * P],
                                   bk(4 + n % 2)[:, 0:w * P].rearrange("p (t q) -> p t q", q=P),
                                   ACT.Copy).then_inc(pt_hi, 1)

            batch = [0]

            def head(h, b, fill, more=True):
                probs(0, b, h)
                for i in range(8):
                    if i + 1 < 8:
                        probs(i + 1, b, h)
                    if fill and i not in (2, 3):
                        if i == 5:
                            qr_high(1 - b, h + 1)
                        hi_part(i, 1 - b, h + 1)
                    turned_high(i, h)
                if fill:
                    hi_part(8, 1 - b, h + 1)
                    hi_part(9, 1 - b, h + 1)
                if fill and more:
                    head_high(h + 2)

            act.wait_ge(kr_sum, 1)
            act.activation(krh[:], ta[:], ACT.Copy).then_inc(krh_ready, 1)
            for u in range(10):
                if u == 6:
                    qr_high(0, 0)
                if u not in (2, 3):
                    hi_part(u, 0, 0)
            head_high(1)
            head(0, 0, True)
            with act.Fori(0, 2) as hp:
                head(2 * hp + 1, 1, True)
                head(2 * hp + 2, 0, True)
            head(5, 1, True)
            head(6, 0, True, False)
            head(7, 1, False)
            act.wait_ge(sr_mm, 1)
            for g in range(2):
                ins = act.activation(rs[:, g, :], bank[g][:].rearrange("p a b -> p (a b)"), ACT.Sqrt,
                                     bias=rcst[:, 3:4], scale=1.0 / HB)
            ins.then_inc(sr_root, 1)

            for n in range(32):
                p = n % 2
                kt = n % 16
                if n >= 2:
                    m = n - 2
                    if m % 16 == 15:
                        act.wait_ge(bank_done, 8 * (m // 16) + 8)
                    else:
                        act.wait_ge(o_mm, m - m // 16 + 1)
                act.wait_ge(ow_in[p], 16 * (n // 2 + 1))
                act.activation(owh[:, p, :], owr[:, p, :], ACT.Copy).then_inc(e_hi, 1)
                act.wait_ge(mx_in[p], 16 * (n // 2 + 1))
                if kt >= 8:
                    act.wait_ge(mx_norm, 8 * (n // 16) + kt - 7)
                act.activation(mxh[:, p, :], mxr[:, p, :], ACT.Copy).then_inc(e_hi, 1)
                if n == 16:
                    for s in range(CHUNKS):
                        act.wait_ge(bank_done, s + 1)
                        act.activation(ev[:, s, :], bk(s), ACT.Copy).then_inc(ev_ready, 1)
            for s in range(CHUNKS):
                act.wait_ge(bank_done, CHUNKS + s + 1)
                act.activation(ev[:, s, :], bk(s), ACT.Copy).then_inc(ev_ready, 1)
                act.wait_ge(stat_ready, s + 1)
                act.activation(bns[:, s, 16:17], bns[:, s, 13:14], ACT.Sqrt, bias=small[:, 20:21]).then_inc(root_ln, 1)
                act.wait_ge(var_ready, s + 1)
                if s >= 2:
                    act.wait_ge(done[s % 2], 16 * (s // 2))
                act.activation(yn[:, s % 2, :], res[:, s, :], ACT.Identity, bias=bns[:, s, 18:19],
                               scale=bns[:, s, 17:18]).then_inc(norm_ready, 1)

        @block.vector
        def _(dve):
            ch = Chain(dve, dvec)
            dve.memset(small[:, 20:21], LN_EPS).then_inc(eps_ready, 1)
            dve.wait_ge(small_in, 16)
            for t in range(KT):
                dve.wait_ge(ada_in[t % 2], 16 * (t // 2 + 1))
                if t == 0:
                    dve.tensor_scalar(acc[:], wada[:, 0, :], ccol[:, 0:1], None, ALU.mult).then_inc(ada_acc, 1)
                else:
                    dve.wait_ge(ada_acc, t)
                    dve.scalar_tensor_tensor(acc[:], wada[:, t % 2, :], ccol[:, t:t + 1], acc[:], ALU.mult,
                                             ALU.add).then_inc(ada_acc, 1)
            dve.wait_ge(mod_mm, 1)
            ch.link(dve.tensor_copy(colv[:], bk(3)[:, 0:NVEC]))
            dve.wait_ge(mod_mm, 2)
            ch.link(dve.tensor_tensor(modc[:], bk(0)[:, 0:16], colv[:, 0:16], ALU.add))
            dve.tensor_scalar(modc[:, 8:16], modc[:, 8:16], 1.0, None, ALU.add).then_inc(ada_acc, 1)
            dve.wait_ge(small_in, 16 * 12)
            ch.link(dve.tensor_tensor(gate_b[:, 0:HB], gate_b[:, 0:HB], bk(1), ALU.add))
            dve.tensor_tensor(gate_b[:, HB:D], gate_b[:, HB:D], bk(2), ALU.add).then_inc(mod_ready, 1)
            for k in range(KT):
                dve.wait_ge(uf_ready, k + 1)
                ch.link(dve.tensor_copy(uh[:, k, :], uf[:, k % 2, :]))
                dve.tensor_tensor(ul[:, k, :], uf[:, k % 2, :], uh[:, k, :].bitcast(F32), ALU.subtract).then_inc(u_split, 1)

            ch.link(dve.memset(cx[:, 12, :], 0.0))
            d16 = slice(DT0, DT0 + 16)
            dve.wait_ge(dt_v, 2)
            dve.scalar_tensor_tensor(dtw[d16], dtv[d16], -1.0, dtv[d16], ALU.mult, ALU.min).then_inc(dt_abs, 1)
            dve.wait_ge(dt_log, 1)
            ch.link(dve.scalar_tensor_tensor(cx[d16, 12, :], dtv[d16], 0.0, dtw[d16], ALU.max, ALU.add))
            ch.link(dve.tensor_scalar(dtv[d16], cx[d16, 12, :], small[d16, 0:1], -1.0, ALU.mult, ALU.mult))
            for k in range(CHUNKS):
                r = slice(k * P, (k + 1) * P)
                dve.tensor_tensor_scan(cx[AC0:AC0 + 16, 12, r], ones[d16, 0:P], dtv[d16, r], 0.0, ALU.mult,
                                       ALU.add).then_inc(dt_done, 1)
            dve.wait_ge(proj_evac, 12)
            ch.link(dve.tensor_tensor(rb[:, 0, :], qk[:, 0, :], qk[:, 0, :], ALU.mult))
            for t in (1, 2):
                ch.link(dve.tensor_tensor(sqs[:], qk[:, t, :], qk[:, t, :], ALU.mult))
                ch.link(dve.tensor_tensor(rb[:, 0, :], rb[:, 0, :], sqs[:], ALU.add))
            ch.link(dve.tensor_tensor(rb[:, 1, :], qk[:, 3, :], qk[:, 3, :], ALU.mult))
            ch.link(dve.tensor_tensor(sqs[:], qk[:, 4, :], qk[:, 4, :], ALU.mult))
            dve.tensor_tensor(rb[:, 1, :], rb[:, 1, :], sqs[:], ALU.add).then_inc(sq_ready, 1)
            for p in range(2):
                ch.link(dve.memset(xr[:, p, 0:3], 0.0))

            def conv(j, p, taps, bias, dst):
                dve.wait_ge(proj_evac, 2 * j + 14)
                ch.link(dve.tensor_scalar(dst, xr[:, p, 3:3 + S], taps(3), bias, ALU.mult, ALU.add))
                for k in (2, 1):
                    ch.link(dve.scalar_tensor_tensor(dst, xr[:, p, k:k + S], taps(k), dst, ALU.mult, ALU.add))
                dve.scalar_tensor_tensor(dst, xr[:, p, 0:S], taps(0), dst, ALU.mult, ALU.add).then_inc(conv_done, 1)

            for j in range(2):
                conv(j, j, lambda k, j=j: colv[:, C_CONVW + 12 * k + j:C_CONVW + 12 * k + j + 1],
                     colv[:, C_CONVB + j:C_CONVB + j + 1], cx[:, j, :])
            for g in range(2):
                dve.wait_ge(root_ready, g + 1)
                ch.link(dve.reciprocal(rb[:, g, :], rb[:, g, :]))
            for t in range(LAT):
                g = 0 if t < QLT else 1
                dve.scalar_tensor_tensor(qk[:, t, :], qk[:, t, :], colv[:, C_QG + t:C_QG + t + 1], rb[:, g, :],
                                         ALU.mult, ALU.mult).then_inc(lat_ready, 1)
            ch.loop(0, 6)
            with dve.Fori(1, 6) as j2:
                ch.base, ch.n = ch.start + 6 * (j2 - 1), 0
                for p in range(2):
                    j = 2 * j2 + p
                    conv(j, p, lambda k, j=j: colv[:, bass.ds(j + (C_CONVW + 12 * k), 1)],
                         colv[:, bass.ds(j + C_CONVB, 1)], cx[:, bass.ds(j, 1), :].rearrange("p a s -> p (a s)"))
            ch.end(5)

            dve.wait_ge(y_out, 16)
            dve.wait_ge(dt_done, CHUNKS)
            dve.wait_ge(silu_done, CONVT)
            dve.memset(state[:], 0.0).then_inc(state_new, 1)

            def heads(v, a, b):
                return v.rearrange("p (h l) -> p h l", h=a)

            def ssd_round(r, c):
                g = r // 2
                dve.wait_ge(exa_ready, 4 * c + r + 1)
                for i in range(4):
                    h = 4 * r + i
                    dve.scalar_tensor_tensor(dec[:, r % 2, i * P:(i + 1) * P], bk(4 + r % 2)[:, i * P:(i + 1) * P],
                                             bdt[:, 256 + AC0 + h:257 + AC0 + h], mask_ls[:], ALU.subtract, ALU.add)
                dve.tensor_tensor(cdv[:, 1, 4 * r:4 * r + 4], bk(4 + r % 2)[:, P - 1:HB:P],
                                  bdt[:, 256 + AC0 + 4 * r:260 + AC0 + 4 * r], ALU.subtract).then_inc(arg_ready, 1)
                dve.tensor_copy(cdv[:, 0, 4 * r:4 * r + 4], exa[:, r % 2, P - 1:HB:P])
                if r >= 2:
                    dve.wait_ge(y_ready, 4 * c + r - 1)
                ex = exa[:, r % 2, :].rearrange("p (h l) -> p h l", h=4)
                dve.tensor_tensor(cts[:, r % 2, :].rearrange("p (h l) -> p h l", h=4), ex,
                                  stg[:, 10 + g, :].unsqueeze(1).to_broadcast([P, 4, P]), ALU.mult)
                dve.wait_ge(dec_ready, 4 * c + r + 1)
                de = dec[:, r % 2, :].rearrange("p (h l) -> p h l", h=4)
                dve.tensor_tensor(de, de, cbs[:, g * P:(g + 1) * P].unsqueeze(1).to_broadcast([P, 4, P]),
                                  ALU.mult).then_inc(g_ready, 1)

            def y_out_round(r, c):
                dve.wait_ge(y_ready, 4 * c + r + 1)
                if r == 0:
                    dve.wait_ge(xd_ready, c + 1)
                    dve.wait_ge(y_out, 16 * c + 16)
                v = bk(6 + r % 2).rearrange("p (j l) -> p j l", j=2)
                for q in range(2):
                    rows = slice(64 * q, 64 * q + 64)
                    ins = dve.tensor_tensor(yts[rows, 2 * r:2 * r + 2, :], v[rows, :, q * P:(q + 1) * P],
                                            xd[rows, 2 * r:2 * r + 2, :], ALU.add)
                ins.then_inc(y_evac, 1)

            with dve.Fori(0, CHUNKS) as c:
                dve.tensor_copy(stg[:], cx[:, :, bass.ds(c * P, P)]).then_inc(stage_ready, 1)
                dve.wait_ge(t_ready, c + 1)
                dve.tensor_copy(bdt[:], bk(6)[:, 0:3 * P]).then_inc(bdt_ready, 1)
                dve.tensor_copy(cbs[:], bk(7)[:, 0:2 * P])
                dve.wait_ge(bdt_ready, c + 1)
                for n in range(2):
                    ins = dve.tensor_tensor(xdt[:, n * HB:(n + 1) * HB].rearrange("p (h d) -> p h d", h=8),
                                            bk(4 + n).rearrange("p (h d) -> p h d", h=8),
                                            bdt[:, 256 + DT0 + 8 * n:264 + DT0 + 8 * n].unsqueeze(2).to_broadcast([P, 8, 64]),
                                            ALU.mult)
                ins.then_inc(xdt_ready, 1)
                ssd_round(0, c)
                ssd_round(1, c)
                y_out_round(0, c)
                ssd_round(2, c)
                y_out_round(1, c)
                ssd_round(3, c)
                y_out_round(2, c)
                dve.wait_ge(dte_ready, c + 1)
                dve.wait_ge(xdt_ready, c + 1)
                dve.tensor_tensor(xdte[:].rearrange("p (h d) -> p h d", h=16), xdt[:].rearrange("p (h d) -> p h d", h=16),
                                  cdv[:, 2, :].unsqueeze(2).to_broadcast([P, 16, 64]), ALU.mult).then_inc(xdte_ready, 1)
                y_out_round(3, c)
                st3 = state[:].rearrange("p (h d) -> p h d", h=16)
                dve.tensor_tensor(st3, st3, cdv[:, 0, :].unsqueeze(2).to_broadcast([P, 16, 64]),
                                  ALU.mult).then_inc(state_decayed, 1)
                dve.wait_ge(state_decayed, c + 1)
                dve.wait_ge(st_ready, c + 1)
                dve.tensor_tensor(state[:], state[:], bank[2][:].rearrange("p a b -> p (a b)"), ALU.add
                                  ).then_inc(state_new, 1)

            dve.wait_ge(proj_ready, 68)
            dve.wait_ge(state_new, CHUNKS + 1)
            dve.wait_ge(rope_in, 64)
            ang, turns = csn, prob[:, 0, :]
            ch.link(dve.tensor_copy(turns, posi[:]))
            ch.link(dve.tensor_scalar(ang[:], turns, rcst[:, 0:1], None, ALU.mult))
            ch.link(dve.tensor_scalar(turns, ang[:], 1.0 / (2 * np.pi), rcst[:, 2:3], ALU.mult, ALU.add))
            ch.link(dve.tensor_scalar(turns, turns, MAGIC, None, ALU.add))
            ch.link(dve.tensor_scalar(turns, turns, MAGIC, None, ALU.subtract))
            for part in (PI2_A, PI2_B, PI2_C):
                ch.link(dve.scalar_tensor_tensor(ang[:], turns, -part, ang[:], ALU.mult, ALU.add))
            ch.link(dve.tensor_scalar(ang[:], ang[:], rcst[:, 1:2], None, ALU.add))
            dve.tensor_scalar(ang[:], ang[:], 3.1415925, -3.1415925, ALU.min, ALU.max).then_inc(csn_arg, 1)
            dve.wait_ge(csn_ready, 1)
            dve.tensor_tensor(ta[:], ta[:], csn[:], ALU.mult).then_inc(kr_t, 1)
            dve.wait_ge(kr_swapped, 32)
            dve.tensor_tensor(ta[:], ta[:], tb[:], ALU.add).then_inc(kr_sum, 1)
            dve.wait_ge(krh_ready, 1)
            dve.tensor_tensor(krl[:], ta[:], krh[:].bitcast(F32), ALU.subtract).then_inc(kr_ready, 1)
            dve.wait_ge(kr_ready, 1)

            def lo_part(u, b, h):
                qnh, qnl, knh, knl, qr, vh, vl = hd[b]
                n = u % 2
                r = slice(n * HB, (n + 1) * HB)
                order = (0, 1, 4, 5, 8, 9)
                if u in order:
                    dve.wait_ge(hp_hi, 6 * h + order.index(u) + 1)
                if u < 2:
                    dve.tensor_tensor(qnl[:, r], bk(7), qnh[:, r].bitcast(F32), ALU.subtract).then_inc(hp_evac, 1)
                elif u < 4:
                    dve.wait_ge(hp_ready, 10 * h + u + 1)
                    if u == 2 and not (isinstance(h, int) and h == 0):
                        dve.wait_ge(qr_hi, h)
                    dve.tensor_tensor(ta[:, r], bk(7), csn[:, r], ALU.mult).then_inc(hp_evac, 1)
                elif u < 6:
                    dve.tensor_tensor(knl[:, r], bk(7), knh[:, r].bitcast(F32), ALU.subtract).then_inc(hp_evac, 1)
                elif u >= 8:
                    t = 4 * (u - 8)
                    dve.tensor_tensor(vl[:, t:t + 4, :], bk(7).rearrange("p (t v) -> p t v", v=P),
                                      vh[:, t:t + 4, :].bitcast(F32), ALU.subtract).then_inc(hp_evac, 1)

            def q_rope_sum(h):
                dve.wait_ge(qr_swapped, 32 * h + 32)
                dve.tensor_tensor(ta[:], ta[:], tb[:], ALU.add).then_inc(qr_sum, 1)

            def q_rope_low(b, h):
                qr = hd[b][4]
                dve.wait_ge(qr_hi, h + 1)
                dve.tensor_tensor(qr[64:128, :], ta[64:128, :], qr[64:128, :].bitcast(F32),
                                  ALU.subtract).then_inc(qr_ready, 1)

            def row_max(i, h):
                dve.wait_ge(s_ready, 8 * h + i + 1)
                v = bank[i % 2][:].rearrange("p a b -> p (a b)")
                ch.link(dve.tensor_tensor(v[:, i * P:(i + 1) * P], v[:, i * P:(i + 1) * P], mask_qk[:], ALU.add))
                ch.link(dve.tensor_reduce(small[:, 4 + i % 2:5 + i % 2], v[:, 0:(i + 1) * P], AX.X, ALU.max))
                if not (isinstance(h, int) and h == 0 and i < 2):
                    dve.wait_ge(exp_done, 8 * h + i - 1)
                dve.tensor_scalar(small[:, 8 + i % 2:9 + i % 2], small[:, 4 + i % 2:5 + i % 2], -SCALE, None,
                                  ALU.mult).then_inc(s_max, 1)

            def normalise(i, h):
                dve.wait_ge(exp_done, 8 * h + i + 1)
                ch.link(dve.reciprocal(small[:, 16 + i % 2:17 + i % 2], small[:, 12 + i % 2:13 + i % 2]))
                n = (i + 1) * P
                dve.tensor_scalar(prob[:, i % 2, 0:n], prob[:, i % 2, 0:n], small[:, 16 + i % 2:17 + i % 2], None,
                                  ALU.mult).then_inc(p_ready, 1)

            batch = [0]

            def turned_low(i, h):
                for t0 in range(0, i + 1, 4):
                    n = batch[0] % 12
                    batch[0] += 1
                    w = min(i + 1, t0 + 4) - t0
                    dve.wait_ge(pt_hi, 12 * h + n + 1)
                    q = slice((i % 4) * P, (i % 4 + 1) * P)
                    dve.tensor_tensor(ptl[:, t0:t0 + w, q], bk(4 + n % 2)[:, 0:w * P].rearrange("p (t q) -> p t q", q=P),
                                      pth[:, t0:t0 + w, q].bitcast(F32), ALU.subtract).then_inc(pt_split, 1)

            def gate_out(g, h):
                dve.wait_ge(pv_ready, 2 * h + g + 1)
                if g == 0:
                    dve.wait_ge(z_in, 16 * h + 16)
                    if not isinstance(h, int) or h > 0:
                        dve.wait_ge(o_out, 16 * h)
                r = slice(g * HB, (g + 1) * HB)
                dve.tensor_tensor(ob[:, r], bk(6), zs[:, r], ALU.mult).then_inc(o_ready, 1)

            def head(h, b, fill):
                row_max(0, h)
                row_max(1, h)
                normalise(0, h)
                for i in range(8):
                    if i + 1 < 8:
                        normalise(i + 1, h)
                    if i + 2 < 8:
                        row_max(i + 2, h)
                    if fill:
                        lo_part(i, 1 - b, h + 1)
                        if i == 4:
                            q_rope_sum(h + 1)
                        if i == 5:
                            q_rope_low(1 - b, h + 1)
                    turned_low(i, h)
                    if i == 4:
                        gate_out(0, h)
                if fill:
                    lo_part(8, 1 - b, h + 1)
                    lo_part(9, 1 - b, h + 1)
                gate_out(1, h)

            for u in range(10):
                lo_part(u, 0, 0)
                if u == 5:
                    q_rope_sum(0)
                    q_rope_low(0, 0)
            head(0, 0, True)
            per = 2 * (8 * 2 + 8)
            ch.loop(0, per)
            with dve.Fori(0, 3) as hp:
                ch.base, ch.n = ch.start + per * hp, 0
                head(2 * hp + 1, 1, True)
                head(2 * hp + 2, 0, True)
            ch.end(3)
            head(7, 1, False)

            dve.wait_ge(sr_root, 1)
            for g in range(2):
                ins = dve.reciprocal(rs[:, g, :], rs[:, g, :])
            ins.then_inc(rs_ready, 1)
            dve.wait_ge(rs_ready, 1)

            def residual(s, half):
                r = slice(half * HB, (half + 1) * HB)
                dve.wait_ge(ev_ready, CHUNKS * half + s + 1)
                ch.link(dve.tensor_tensor(tmpo[:, s % 2, :], ev[:, s, :], gate_b[:, r], ALU.mult))
                ins = dve.scalar_tensor_tensor(res[:, s, r], res[:, s, r], ALPHA, tmpo[:, s % 2, :], ALU.mult, ALU.add)
                return ins, r

            for n in range(32):
                p = n % 2
                kt = n % 16
                if kt >= 8:
                    dve.wait_ge(mx_in[p], 16 * (n // 2 + 1))
                    dve.scalar_tensor_tensor(mxr[:, p, :], mxr[:, p, :], colv[:, C_SG + kt - 8:C_SG + kt - 7],
                                             rs[:, (kt - 8) // 4, :], ALU.mult, ALU.mult).then_inc(mx_norm, 1)
                dve.wait_ge(e_hi, 2 * n + 1)
                dve.tensor_tensor(owl[:, p, :], owr[:, p, :], owh[:, p, :].bitcast(F32), ALU.subtract
                                  ).then_inc(e_split, 1)
                dve.wait_ge(e_hi, 2 * n + 2)
                dve.tensor_tensor(mxl[:, p, :], mxr[:, p, :], mxh[:, p, :].bitcast(F32), ALU.subtract
                                  ).then_inc(e_split, 1)
                if n == 17:
                    dve.wait_ge(res_in, 16)
                if 17 <= n < 25:
                    ins, r = residual(n - 17, 0)
                    ch.link(ins)
                    ch.link(dve.bn_stats(bns[:, n - 17, 0:6], res[:, n - 17, r]))
            for s in range(CHUNKS):
                ins, r = residual(s, 1)
                ch.link(ins)
                ch.link(dve.bn_stats(bns[:, s, 6:12], res[:, s, r]))
                dve.bn_aggr(bns[:, s, 12:14], bns[:, s, 0:12]).then_inc(stat_ready, 1)
                dve.wait_ge(root_ln, s + 1)
                ch.link(dve.reciprocal(bns[:, s, 17:18], bns[:, s, 16:17]))
                dve.scalar_tensor_tensor(bns[:, s, 18:19], bns[:, s, 12:13], -1.0, bns[:, s, 17:18], ALU.mult,
                                         ALU.mult).then_inc(var_ready, 1)


_INS = ["x", "c", "positions", "w_ada", "b_ada", "w_in", "q_norm_g", "w_qb", "kv_norm_g", "w_kvb", "conv_w", "conv_b",
        "dt_bias", "a_log", "d_skip", "ssm_norm_g", "w_out", "ln_g", "ln_b"]


def rope_constants():
    half = ROPE // 2
    inv = (np.float32(1.0) / np.power(np.float32(10000.0), np.arange(half, dtype=np.float32) / np.float32(half))).astype(np.float32)
    phase = np.repeat([np.pi / 2, np.pi / 2, np.pi, 0.0], half)
    return np.stack([np.tile(inv, 4), phase, phase / (2 * np.pi), np.full(P, RMS_EPS)], axis=1).astype(np.float32)


def kernel(**inputs):
    import concourse.bacc as bacc
    from concourse.bass_utils import run_bass_kernel_spmd

    nc = bacc.Bacc("TRN2", target_bir_lowering=False, num_devices=1)
    arrays, args = {}, []
    for name in _INS:
        a = np.ascontiguousarray(inputs[name])
        arrays[f"in_{name}"] = a
        args.append(nc.dram_tensor(f"in_{name}", a.shape, mybir.dt.from_np(a.dtype), kind="ExternalInput").ap())
    arrays["in_rope_constants"] = rope_constants()
    args.append(nc.dram_tensor("in_rope_constants", [P, 4], F32, kind="ExternalInput").ap())
    args.append(nc.dram_tensor("out_0", [1, S, D], F32, kind="ExternalOutput").ap())
    build_layer(nc, *args)
    r = run_bass_kernel_spmd(nc, [arrays], core_ids=[0])
    return r.results[0]["out_0"]
```

```python
from contextlib import ExitStack

import numpy as np

import concourse.bass as bass
from concourse import mybir

F32 = mybir.dt.float32
F32R = mybir.dt.float32r
I32 = mybir.dt.int32
ALU = mybir.AluOpType
ACT = mybir.ActivationFunctionType
AX = mybir.AxisListType

P = 128
D = 1024
S = 1024
KT = D // P
HB = 512
NHALF = S // HB
HEADS = 8
ROPE = 64
QW = 192
QLT = 3
KLT = 2
LAT = QLT + KLT
SSM_H = 16
NST = 8
CONVT = 12
TAPS = 4
CHUNKS = S // P
W_KV_ROPE = 640
W_ZATT = 704
W_XBC = 1728
W_DT = 3264
W_ZSSM = 3280
Z_ATT0 = 5
Z_SSM0 = 13
C_CONVW, C_CONVB, C_QG, C_KVG, C_SG, NVEC = 24, 72, 84, 87, 89, 97
ALPHA = 2.0 ** 0.25
RMS_EPS = 1e-6
LN_EPS = 1e-5
SCALE = 192.0 ** -0.5
NEG = -1.0e30
MAGIC = 12582912.0
PI2_A = 6.28125
PI2_B = 0.0019350051879882812
PI2_C = float(2 * np.pi - 6.28125 - 0.0019350051879882812)
RT = 4
RING = 4
TURNED = (0, 1, 2, 3, 4, 6, 8, 10)
DT0, AC0 = 64, 96


def build_layer(nc, x, c, pos, w_ada, b_ada, w_in, qg, w_qb, kvg, w_kvb, conv_w, conv_b, dt_bias,
                a_log, d_skip, ssmg, w_out, ln_g, ln_b, ropec, out):
    scr = nc.dram_tensor("proj_scratch", [21, P, S], F32).ap()
    scy = nc.dram_tensor("ssm_scratch", [NST, P, S], F32).ap()
    scg = nc.dram_tensor("ssm_gated_scratch", [NST, P, S], F32).ap()
    sco = nc.dram_tensor("attn_scratch", [HEADS, P, S], F32).ap()

    ctx = ExitStack()
    with ctx:
        def at(offset, spec):
            made = []
            for name, shape, dt in spec:
                made.append(nc.alloc_sbuf_tensor_at(name, shape, dt, offset=offset))
                offset += -(-int(np.prod(shape[1:])) * 4 // 32) * 32
            return made, offset

        def sem(name):
            return ctx.enter_context(nc.semaphore(name))

        base = -(-nc.sbuf_base // 64) * 64
        (ident, ones, mask_qk, mask_ls, colv, modc, gate_b, dsk, dsr, dtb, alg, ccol, rcst, small), end_c = at(base, [
            ("ident", [P, P], F32), ("ones", [P, P], F32), ("mask_qk", [P, P], F32), ("mask_ls", [P, P], F32),
            ("colv", [P, NVEC], F32), ("modc", [P, 16], F32), ("gate_b", [P, D], F32), ("dsk", [P, NST], F32), ("dsr", [P, SSM_H], F32),
            ("dtb", [P, 1], F32), ("alg", [P, 1], F32), ("ccol", [P, KT], F32), ("rcst", [P, 4], F32),
            ("small", [P, 64], F32)])
        reg_a, reg_b = end_c, end_c + 55 * 1024
        limit = nc.sbuf_usable_end

        (xin,), _ = at(reg_a, [("xin", [P, CHUNKS, D], F32)])
        (cx,), e = at(reg_a, [("cx", [P, 13, S], F32)])
        assert e <= reg_b
        (qlh, qll, ckh, ckl, hwr, hwh, hwl), e = at(reg_a, [
            ("qlh", [P, QLT, S], F32R), ("qll", [P, QLT, S], F32R), ("ckh", [P, KLT, S], F32R),
            ("ckl", [P, KLT, S], F32R), ("hwr", [P, 1280], F32), ("hwh", [P, 1280], F32R), ("hwl", [P, 1280], F32R)])
        assert e <= reg_b
        top = (limit - 3 * S * 4) // 64 * 64
        (csn, krh, krl), _ = at(top, [("csn", [P, S], F32), ("krh", [P, S], F32R), ("krl", [P, S], F32R)])

        (uh, ul, wraw, wh, wl, ost), b1 = at(reg_b, [
            ("uh", [P, KT, S], F32R), ("ul", [P, KT, S], F32R), ("wraw", [P, 2, KT, P], F32),
            ("wh", [P, 2, KT, P], F32R), ("wl", [P, 2, KT, P], F32R), ("ost", [P, 2, S], F32)])
        (acc, wada, uf, vrow), e = at(b1, [("acc", [P, 3 * D], F32), ("wada", [P, 2, 3 * D], F32),
                                           ("uf", [P, 2, S], F32), ("vrow", [NVEC, P], F32)])
        assert e <= limit
        (qk, xr, rb), e = at(b1, [("qk", [P, LAT, S], F32), ("xr", [P, 2, S + 4], F32), ("rb", [P, 2, S], F32)])
        assert e <= top
        posi = nc.alloc_sbuf_tensor_at("posi", [P, S], I32, offset=e - 8 * S)
        ropex, ropes, turns, dtv, sqs, dtw = cx[:, 8, :], cx[:, 9, :], cx[:, 10, :], cx[:, 11, :], cx[:, 10, :], rb[:, 1, :]
        (stg, xdt, xdte, bdt, cbs, dec, exa, cts, state, xd, cdv), e = at(b1, [
            ("stg", [P, 13, P], F32), ("xdt", [P, D], F32), ("xdte", [P, D], F32), ("bdt", [P, 3 * P], F32),
            ("cbs", [P, 2 * P], F32), ("dec", [P, 2, HB], F32), ("exa", [P, 2, HB], F32),
            ("cts", [P, 2, HB], F32), ("state", [P, D], F32), ("xd", [P, NST, P], F32), ("cdv", [P, 3, SSM_H], F32)])
        assert e <= top

        hd = [at(reg_b + i * 28 * 1024, [
            (f"qnh{i}", [P, S], F32R), (f"qnl{i}", [P, S], F32R), (f"knh{i}", [P, S], F32R),
            (f"knl{i}", [P, S], F32R), (f"qr{i}", [P, S], F32R), (f"vh{i}", [P, CHUNKS, P], F32R),
            (f"vl{i}", [P, CHUNKS, P], F32R)])[0] for i in range(2)]
        (rl, pth, ptl, prob, zs, ob), ta_at = at(reg_b + 56 * 1024, [
            ("rl", [P, 2, S], F32), ("pth", [P, CHUNKS, HB], F32R), ("ptl", [P, CHUNKS, HB], F32R),
            ("prob", [P, 2, S], F32), ("zs", [P, S], F32), ("ob", [P, S], F32)])
        (ta, tb, sqa), e = at(ta_at, [("ta", [P, S], F32), ("tb", [P, S], F32), ("sqa", [P, 2, S], F32)])
        assert e <= top

        MX, OW = HB * 4, D * 4
        slot_at = [reg_a + q * 2 * (MX + OW) for q in range(3)] + [reg_b]
        raw_at = [reg_b + 2 * (MX + OW), reg_b + 3 * (MX + OW), reg_a + 40 * 1024, reg_a + 40 * 1024 + MX + OW]
        mxh, mxl, owh, owl = zip(*[at(o, [(f"mxh{q}", [P, HB], F32R), (f"mxl{q}", [P, HB], F32R), (f"owh{q}", [P, D], F32R),
                                          (f"owl{q}", [P, D], F32R)])[0] for q, o in enumerate(slot_at)])
        mxr, owr = zip(*[at(o, [(f"mxr{q}", [P, HB], F32), (f"owr{q}", [P, D], F32)])[0] for q, o in enumerate(raw_at)])
        (rs,), _ = at(ta_at, [("rs", [P, 2, S], F32)])
        (res, lgb, lbb, yn, bns), e = at(reg_b + 28 * 1024, [
            ("res", [P, CHUNKS, D], F32), ("lgb", [P, D], F32), ("lbb", [P, D], F32), ("yn", [P, RT, D], F32),
            ("bns", [P, CHUNKS, 24], F32)])
        assert e <= ta_at

        bank = [ctx.enter_context(nc.psum_tensor(f"bank{i}", [P, 2, HB], F32)) for i in range(4)]

        def bk(i):
            return bank[i // 2][:, i % 2, :]

        def unit_bank(u, h):
            return bk(u % 4) if isinstance(h, int) and h == 0 else bk(7)

        small_in = sem("small_in")
        x_in = sem("x_in")
        ada_in = [sem("ada_in0"), sem("ada_in1")]
        consts = sem("consts")
        eps_ready = sem("eps_ready")
        ada_acc = sem("ada_acc")
        xt_ready = sem("xt_ready")
        uf_ready = sem("uf_ready")
        u_split = sem("u_split")
        mod_mm = sem("mod_mm")
        mod_ready = sem("mod_ready")
        w_in_sem = [sem("w_raw_in0"), sem("w_raw_in1")]
        w_hi = sem("w_hi")
        w_split = sem("w_split")
        proj_ready = sem("proj_ready")
        proj_evac = sem("proj_evac")
        dt_v = sem("dt_v")
        dt_abs = sem("dt_abs")
        dt_log = sem("dt_log")
        dt_done = sem("dt_done")
        conv_done = sem("conv_done")
        silu_done = sem("silu_done")
        sq_ready = sem("sq_ready")
        ss_mm = sem("ss_mm")
        root_ready = sem("root_ready")
        lat_ready = sem("lat_ready")
        z_out = [sem("z_out0"), sem("z_out1")]
        dvec = sem("dve_chain")
        poolc = sem("pool_chain")
        actc = sem("act_chain")
        stage_ready = sem("stage_ready")
        t_ready = sem("t_ready")
        bdt_ready = sem("bdt_ready")
        xdt_ready = sem("xdt_ready")
        acb_ready = sem("acb_ready")
        exa_ready = sem("exa_ready")
        arg_ready = sem("arg_ready")
        dec_ready = sem("dec_ready")
        g_ready = sem("g_ready")
        y_ready = sem("y_ready")
        y_evac = sem("y_evac")
        xd_ready = sem("xd_ready")
        state_decayed = sem("state_decayed")
        dte_ready = sem("dte_ready")
        xdte_ready = sem("xdte_ready")
        st_ready = sem("st_ready")
        state_new = sem("state_new")
        y_out = sem("y_out")

        lat_in = [sem("lat_in0"), sem("lat_in1")]
        lat_hi = sem("lat_hi")
        lat_split = sem("lat_split")
        rope_in = sem("rope_in")
        csn_ready = sem("csn_ready")
        csn_arg = sem("csn_arg")
        kr_t = sem("kr_t")
        kr_swapped = sem("kr_swapped")
        kr_sum = sem("kr_sum")
        krh_ready = sem("krh_ready")
        kr_ready = sem("kr_ready")
        hw_in = sem("hw_in")
        hw_split = sem("hw_split")
        hp_ready = sem("hp_ready")
        hp_hi = sem("hp_hi")
        hp_evac = sem("hp_evac")
        qr_swapped = sem("qr_swapped")
        qr_sum = sem("qr_sum")
        qr_hi = sem("qr_hi")
        qr_ready = sem("qr_ready")
        s_ready = sem("s_ready")
        s_max = sem("s_max")
        exp_done = sem("exp_done")
        p_ready = sem("p_ready")
        pt_ready = sem("pt_ready")
        pt_hi = sem("pt_hi")
        pt_split = sem("pt_split")
        pv_ready = sem("pv_ready")
        o_ready = sem("o_ready")
        o_out = sem("o_out")
        z_in = sem("z_in")
        y_in = sem("y_in")
        zy_in = sem("zy_in")
        yg_ready = sem("yg_ready")
        yg_out = sem("yg_out")
        sqa_ready = sem("sqa_ready")
        sr_mm = sem("sr_mm")
        sr_copied = sem("sr_copied")
        sr_inverse = sem("sr_inverse")

        mx_in = [sem(f"mx_in{q}") for q in range(RING)]
        mx_norm = sem("mx_norm")
        ow_in = [sem(f"ow_in{q}") for q in range(RING)]
        ow_gated = sem("ow_gated")
        e_hi = sem("e_hi")
        e_split = sem("e_split")
        o_mm = sem("o_mm")
        bank_done = sem("bank_done")
        res_ready = sem("res_ready")
        res_in = sem("res_in")
        ln_in = sem("ln_in")
        rs_ready = sem("rs_ready")
        norm_ready = sem("norm_ready")
        root_ln = sem("root_ln")
        stat_ready = sem("stat_ready")
        var_ready = sem("var_ready")
        gain_ready = sem("gain_ready")
        y_final = sem("y_final")
        y_final_pool = sem("y_final_pool")
        done = [sem(f"out_stored{q}") for q in range(RT)]

        block = ctx.enter_context(nc.Block())

        class Chain:

            def __init__(self, eng, s):
                self.eng, self.s, self.n, self.base = eng, s, 0, 0

            def link(self, ins):
                ins.then_inc(self.s, 1)
                self.n += 1
                self.eng.wait_ge(self.s, self.base + self.n)

            def loop(self, i, per):
                self.start, self.per = self.n, per
                self.base, self.n = self.start + per * i, 0

            def end(self, count):
                assert self.n == self.per, (self.n, self.per)
                self.base, self.n = 0, self.start + self.per * count

        def shift_right(pool, s):
            pool.wait_ge(gain_ready, s + 1)
            pool.tensor_tensor(yn[:, s % RT, HB:D], yn[:, s % RT, HB:D], lbb[:, HB:D], ALU.add).then_inc(y_final_pool, 1)

        w3 = w_in[0].rearrange("(k p) n -> p k n", p=P)

        @block.sync
        def _(sp):
            sp.dma_start(ccol[:], c[0].rearrange("(p t) -> p t", t=KT)).then_inc(small_in, 16)
            for dst, src in (
                (vrow[0:24], b_ada[0].rearrange("(t p) -> t p", p=P)),
                (vrow[24:72], conv_w[0].rearrange("k (j p) -> (k j) p", p=P)),
                (vrow[72:84], conv_b[0].rearrange("(t p) -> t p", p=P)),
                (vrow[84:87], qg[0].rearrange("(t p) -> t p", p=P)),
                (vrow[87:89], kvg[0].rearrange("(t p) -> t p", p=P)),
                (vrow[89:97], ssmg[0].rearrange("(t p) -> t p", p=P)),
                (gate_b[:], b_ada[0, 2 * D:3 * D].partition_broadcast(P)),
                (dsr[:], d_skip[0].partition_broadcast(P)),
                (dtb[DT0:DT0 + 16], dt_bias[0].rearrange("(h a) -> h a", a=1)),
                (alg[DT0:DT0 + 16], a_log[0].rearrange("(h a) -> h a", a=1)),
                (rcst[:], ropec),
            ):
                sp.dma_start(dst, src).then_inc(small_in, 16)
            ada = w_ada[0].rearrange("(p t) n -> p t n", t=KT)
            for t in range(KT):
                if t >= 2:
                    sp.wait_ge(ada_acc, t - 1)
                sp.dma_start(wada[:, t % 2, :], ada[:, t, :]).then_inc(ada_in[t % 2], 16)
                sp.dma_start(xin[:, t, :], x[0, t * P:(t + 1) * P, :]).then_inc(x_in, 16)

            def address(v):
                return v if isinstance(v, int) else sp.snap(v)

            def load_tile(p, col, wait):
                src = w3[:, :, bass.ds(address(col), P)]
                if wait is not None:
                    sp.wait_ge(w_split, wait)
                sp.dma_start(wraw[:, p], src).then_inc(w_in_sem[p], 16)

            def store_z(tile, p, i):
                dst = scr[bass.ds(address(i), 1)]
                sp.wait_ge(proj_evac, tile)
                sp.dma_start(dst, ost[:, p, :]).then_inc(z_out[p], 16)

            def store_y(i):
                col = address(i * P)
                sp.wait_ge(y_evac, 4 * i + 4)
                sp.dma_start(scy[:, :, bass.ds(col, P)].rearrange("j p l -> p j l"), xd[:]).then_inc(y_out, 16)

            sp.dma_start(wraw[:, 0, :, 0:ROPE], w3[:, :, W_KV_ROPE:W_KV_ROPE + ROPE]).then_inc(w_in_sem[0], 16)
            sp.dma_start(wraw[:, 0, :, ROPE:ROPE + 16], w3[:, :, W_DT:W_DT + 16]).then_inc(w_in_sem[0], 16)
            load_tile(1, 0, None)
            for t in range(2, 6):
                load_tile(t % 2, (t - 1) * P, t - 1)
            sp.dma_start(posi[:], pos[0].partition_broadcast(P)).then_inc(rope_in, 16)
            sp.wait_ge(proj_evac, 2)
            sp.dma_start(ropex[96:128], ost[0:32, 0, :]).then_inc(rope_in, 16)
            sp.dma_start(ropex[0:64], ost[0:64, 0, :]).then_inc(z_out[0], 16)
            sp.dma_start(ropex[64:96], ost[32:64, 0, :]).then_inc(z_out[1], 16)
            with sp.Fori(0, 4) as j:
                for p in range(2):
                    load_tile(p, W_XBC + (2 * j + p) * P, 2 * j + p + 5)
            sp.wait_ge(lat_ready, LAT)
            sp.dma_start(scr[0:5].rearrange("t p s -> p t s"), qk[:]).then_inc(y_out, 16)
            with sp.Fori(4, 6) as j:
                for p in range(2):
                    load_tile(p, W_XBC + (2 * j + p) * P, 2 * j + p + 5)
            load_tile(0, W_ZATT, 17)
            load_tile(1, W_ZSSM, 18)
            with sp.Fori(0, CHUNKS - 1) as i:
                load_tile(0, W_ZATT + (i + 1) * P, 2 * i + 19)
                load_tile(1, W_ZSSM + (i + 1) * P, 2 * i + 20)
                store_z(4 * i + 38, 0, i + Z_ATT0)
                store_z(4 * i + 40, 1, i + Z_SSM0)
                store_y(i)
            def head_weights(h, wait=None):
                q0, q1, q2 = (address(h * QW + o) for o in (0, 160, 128))
                kv0 = address(h * 256)
                if wait is not None:
                    sp.wait_ge(hw_split, wait)
                q = w_qb[0].rearrange("(k p) n -> p k n", p=P)
                kv = w_kvb[0].rearrange("(k p) n -> p k n", p=P)
                qv = hwr[:, 0:768].rearrange("p (k n) -> p k n", n=256)
                sp.dma_start(qv[:, :, 0:QW], q[:, :, bass.ds(q0, QW)]).then_inc(hw_in, 16)
                sp.dma_start(qv[:, :, 192:224], q[:, :, bass.ds(q1, 32)]).then_inc(hw_in, 16)
                sp.dma_start(qv[:, :, 224:256], q[:, :, bass.ds(q2, 32)]).then_inc(hw_in, 16)
                sp.dma_start(hwr[:, 768:1280].rearrange("p (k n) -> p k n", n=256),
                             kv[:, :, bass.ds(kv0, 256)]).then_inc(hw_in, 16)

            i = CHUNKS - 1
            def latent(t):
                sp.wait_ge(w_split, 33 + t if t < 2 else 34)
                if t >= 2:
                    sp.wait_ge(lat_split, t - 1)
                sp.dma_start(wraw[:, t % 2], scr[t].rearrange("p (k n) -> p k n", n=P)).then_inc(lat_in[t % 2], 16)

            sp.wait_ge(stage_ready, CHUNKS)
            sp.wait_ge(y_out, 16)
            latent(0)
            latent(1)
            head_weights(0)
            store_z(4 * i + 38, 0, i + Z_ATT0)
            latent(2)
            latent(3)
            latent(4)
            store_z(4 * i + 40, 1, i + Z_SSM0)
            store_y(i)
            sp.wait_ge(z_out[0], 16 * 9)
            sp.wait_ge(z_out[1], 16 * 9)
            sp.wait_ge(y_out, 16 * CHUNKS + 16)
            sp.wait_ge(proj_ready, 68)
            sp.wait_ge(state_new, CHUNKS + 1)

            def swap_q(h):
                sp.wait_ge(hp_evac, 10 * h + 4)
                sp.dma_start(tb[0:64], ta[64:128]).then_inc(qr_swapped, 16)
                sp.dma_start(tb[64:128], ta[0:64]).then_inc(qr_swapped, 16)

            swap_q(0)

            def mixed_and_weights(n):
                q, half, kt = n % RING, n // 16, n % 16
                if n >= RING:
                    sp.wait_ge(e_split, 2 * (n - RING) + 2)
                sp.dma_start(owr[q][:], w_out[0, kt * P:(kt + 1) * P, :]).then_inc(ow_in[q], 16)
                if kt == HEADS - 1:
                    sp.wait_ge(o_out, 16 * HEADS)
                src = sco[kt] if kt < HEADS else scg[kt - HEADS]
                sp.dma_start(mxr[q][:], src[:, half * HB:(half + 1) * HB]).then_inc(mx_in[q], 16)

            def head_io(h, fill):
                if fill and not (isinstance(h, int) and h == HEADS - 2):
                    head_weights(h + 2, h + 2)
                z_att, z_ssm, head = address(h + Z_ATT0), address(h + Z_SSM0), address(h)
                if not isinstance(h, int) or h > 0:
                    sp.wait_ge(o_ready, 2 * h)
                sp.dma_start(zs[:], scr[bass.ds(z_att, 1)]).then_inc(z_in, 16)
                if not isinstance(h, int) or h > 0:
                    sp.wait_ge(yg_out, 16 * h)
                    sp.wait_ge(sqa_ready, h)
                sp.dma_start(rl[:, 0, :], scr[bass.ds(z_ssm, 1)]).then_inc(zy_in, 16)
                sp.dma_start(rl[:, 1, :], scy[bass.ds(head, 1)]).then_inc(y_in, 16)
                if fill:
                    swap_q(h + 1)
                else:
                    sp.wait_ge(pv_ready, 2 * HEADS - 2)
                    sp.wait_ge(hp_ready, 10 * HEADS)
                    for n in range(RING):
                        mixed_and_weights(n)
                sp.wait_ge(yg_ready, h + 1)
                sp.dma_start(scg[bass.ds(head, 1)], rl[:, 1, :]).then_inc(yg_out, 16)
                sp.wait_ge(o_ready, 2 * h + 2)
                sp.dma_start(sco[bass.ds(head, 1)], ob[:]).then_inc(o_out, 16)

            def store_rows(s):
                sp.wait_ge(y_final, s + 1)
                sp.wait_ge(y_final_pool, s + 1)
                sp.dma_start(out[0, s * P:(s + 1) * P, :], yn[:, s % RT, :]).then_inc(done[s % RT], 16)

            head_weights(1, 1)
            head_io(0, True)
            with sp.Fori(1, HEADS - 2) as h:
                head_io(h, True)
            head_io(HEADS - 2, True)
            head_io(HEADS - 1, False)

            for n in range(4, 32):
                mixed_and_weights(n)
                if n == 8:
                    sp.wait_ge(pv_ready, 2 * HEADS)
                    sp.dma_start(res[:], x[0].rearrange("(s p) d -> p s d", p=P)).then_inc(res_in, 16)
                    sp.dma_start(lgb[:], ln_g[0].partition_broadcast(P)).then_inc(ln_in, 16)
                    sp.dma_start(lbb[:], ln_b[0].partition_broadcast(P)).then_inc(ln_in, 16)
                if 26 <= n < 30:
                    store_rows(n - 26)
            for s in range(RT, CHUNKS):
                store_rows(s)
            for q in range(RT):
                sp.wait_ge(done[q], 16 * CHUNKS // RT)

        @block.gpsimd
        def _(pool):
            ch = Chain(pool, poolc)
            ch.link(pool.memset(ident[:], 0.0))
            pool.affine_select(ident[:], ident[:], pattern=[[-1, P]], compare_op=ALU.not_equal, fill=1.0,
                               base=0, channel_multiplier=1).then_inc(consts, 1)
            ch.link(pool.memset(mask_qk[:], 0.0))
            pool.affine_select(mask_qk[:], mask_qk[:], pattern=[[-1, P]], compare_op=ALU.is_ge, fill=NEG,
                               base=0, channel_multiplier=1).then_inc(consts, 1)
            ch.link(pool.memset(mask_ls[:], 0.0))
            pool.affine_select(mask_ls[:], mask_ls[:], pattern=[[1, P]], compare_op=ALU.is_ge, fill=NEG,
                               base=0, channel_multiplier=-1).then_inc(consts, 1)
            pool.memset(ones[:], 1.0).then_inc(consts, 1)

            def split_tile(p, tile, cols=P):
                pool.wait_ge(w_hi, tile + 1)
                pool.tensor_tensor(wl[:, p, :, 0:cols], wraw[:, p, :, 0:cols], wh[:, p, :, 0:cols].bitcast(F32),
                                   ALU.subtract).then_inc(w_split, 1)

            pool.wait_ge(small_in, 16 * 12)
            for q in range(2):
                ch.link(pool.tensor_copy(dsk[64 * q:64 * q + 64, :], dsr[64 * q:64 * q + 64, q:SSM_H:2]))
            split_tile(0, 0, ROPE + 16)
            split_tile(1, 1)
            with pool.Fori(1, 9) as j:
                for p in range(2):
                    split_tile(p, 2 * j + p)
            with pool.Fori(0, CHUNKS) as i:
                split_tile(0, 2 * i + 18)
                pool.wait_ge(stage_ready, i + 1)
                pool.wait_ge(y_out, 16 * i + 16)
                pool.tensor_tensor(xd[:], stg[:, 0:NST, :], dsk[:].unsqueeze(2).to_broadcast([P, NST, P]),
                                   ALU.mult).then_inc(xd_ready, 1)
                split_tile(1, 2 * i + 19)
            def split_head(h):
                pool.wait_ge(w_hi, h + 35)
                pool.tensor_tensor(hwl[:], hwr[:], hwh[:].bitcast(F32), ALU.subtract).then_inc(hw_split, 1)

            for t in range(LAT):
                if t == 2:
                    split_head(0)
                hi, lo = (v[:, t, :] if t < QLT else w[:, t - QLT, :] for v, w in ((qlh, ckh), (qll, ckl)))
                pool.wait_ge(lat_hi, t + 1)
                pool.tensor_tensor(lo, wraw[:, t % 2].rearrange("p k n -> p (k n)"), hi.bitcast(F32),
                                   ALU.subtract).then_inc(lat_split, 1)

            def ssm_tile(h, g, first):
                pool.wait_ge(y_in, 16 * h + 16)
                pool.wait_ge(zy_in, 16 * h + 16)
                pool.tensor_tensor(rl[:, 1, :], rl[:, 1, :], rl[:, 0, :], ALU.mult).then_inc(yg_ready, 1)
                pool.wait_ge(yg_ready, h + 1)
                sq = sqa[:, g, :] if first else rl[:, 0, :]
                m = pool.tensor_tensor(sq, rl[:, 1, :], rl[:, 1, :], ALU.mult)
                if first:
                    m.then_inc(sqa_ready, 1)
                else:
                    ch.link(m)
                    pool.wait_ge(sqa_ready, h)
                    pool.tensor_tensor(sqa[:, g, :], sqa[:, g, :], rl[:, 0, :], ALU.add).then_inc(sqa_ready, 1)

            for g in range(2):
                split_head(4 * g + 1)
                ssm_tile(4 * g, g, True)
                ch.loop(0, 1)
                last = 4 if g == 0 else 3
                with pool.Fori(1, last) as k:
                    ch.base = ch.start + (k - 1)
                    ch.n = 0
                    split_head(4 * g + k + 1)
                    ssm_tile(4 * g + k, g, False)
                ch.end(last - 1)
                if g == 1:
                    ssm_tile(7, g, False)
            for n in range(32):
                q = n % RING
                pool.wait_ge(ow_in[q], 16 * (n // RING + 1))
                pool.tensor_tensor(owr[q][:], owr[q][:], gate_b[:], ALU.mult).then_inc(ow_gated, 1)
                if n == 22:
                    pool.wait_ge(ln_in, 32)
                if 24 <= n < 28:
                    shift_right(pool, n - 24)
            for s in range(RT, CHUNKS):
                shift_right(pool, s)

        @block.tensor
        def _(pe):
            def three(dst, ah, al, bh, bl, start, stop):
                pe.matmul(dst, ah, bh, start=start, stop=False)
                pe.matmul(dst, ah, bl, start=False, stop=False)
                return pe.matmul(dst, al, bh, start=False, stop=stop)

            pe.wait_ge(consts, 4)
            pe.wait_ge(small_in, 16 * 12)
            pe.transpose(bk(3)[:, 0:NVEC], vrow[:], ident[0:NVEC, 0:NVEC]).then_inc(mod_mm, 1)

            def x_transposes(k):
                if k >= 2:
                    pe.wait_ge(uf_ready, k - 1)
                for s in range(CHUNKS):
                    m = pe.transpose(bk(4 + 2 * (k % 2) + s // 4)[:, (s % 4) * P:(s % 4 + 1) * P],
                                     xin[:, s, k * P:(k + 1) * P], ident[:])
                m.then_inc(xt_ready, 1)

            pe.wait_ge(x_in, 16 * CHUNKS)
            x_transposes(0)
            x_transposes(1)
            pe.wait_ge(ada_acc, KT)
            for m in range(16):
                mm = pe.matmul(bk(0)[:, m:m + 1], acc[:, m * P:(m + 1) * P], ones[:, 0:1], start=True, stop=True)
            for n in range(2):
                mm = pe.matmul(bk(1 + n), ones[:], acc[:, 2 * D + n * HB:2 * D + (n + 1) * HB], start=True, stop=True)
            mm.then_inc(mod_mm, 1)

            def proj_mm(p, n, k, start, stop, cols=P):
                r = slice(n * HB, (n + 1) * HB)
                return three(bk(2 * p + n)[0:cols], wh[:, p, k, 0:cols], wl[:, p, k, 0:cols],
                             uh[:, k, r], ul[:, k, r], start, stop)

            pe.wait_ge(mod_ready, 2)
            pe.wait_ge(w_split, 2)
            for k in range(KT):
                pe.wait_ge(u_split, k + 1)
                for p in range(2):
                    for n in range(NHALF):
                        mm = proj_mm(p, n, k, k == 0, k == KT - 1, ROPE + 16 if p == 0 else P)
                        if k == KT - 1:
                            mm.then_inc(proj_ready, 1)
                if k + 2 < KT:
                    x_transposes(k + 2)

            def proj_tile(p, tile):
                pe.wait_ge(w_split, tile + 1)
                for n in range(NHALF):
                    pe.wait_ge(proj_evac, 2 * tile + n - 3)
                    for k in range(KT):
                        mm = proj_mm(p, n, k, k == 0, k == KT - 1)
                    mm.then_inc(proj_ready, 1)

            with pe.Fori(1, 4) as j:
                for p in range(2):
                    proj_tile(p, 2 * j + p)
            pe.wait_ge(sq_ready, 1)
            for g in range(2):
                for n in range(2):
                    mm = pe.matmul(bk(4 + 2 * g + n), ones[:], rb[:, g, n * HB:(n + 1) * HB], start=True, stop=True)
            mm.then_inc(ss_mm, 1)
            with pe.Fori(4, 9) as j:
                for p in range(2):
                    proj_tile(p, 2 * j + p)

            def proj_part(p, n, part, tile):
                if part == 0:
                    if n == 0:
                        pe.wait_ge(w_split, tile + 1)
                    pe.wait_ge(proj_evac, 2 * tile + n - 3)
                steps = [(k, q) for k in range(KT) for q in range(3)][8 * part:8 * part + 8]
                for k, q in steps:
                    a = wl if q == 2 else wh
                    b = ul if q == 1 else uh
                    mm = pe.matmul(bk(2 * p + n), a[:, p, k, :], b[:, k, n * HB:(n + 1) * HB],
                                   start=(k == 0 and q == 0), stop=(k == KT - 1 and q == 2))
                if part == 2:
                    mm.then_inc(proj_ready, 1)

            def acum_rows(r, c):
                if r == 0:
                    pe.wait_ge(xdt_ready, c + 1)
                if r >= 2:
                    pe.wait_ge(arg_ready, 4 * c + r - 1)
                for i in range(4):
                    j = AC0 + 4 * r + i
                    mm = pe.matmul(bk(4 + r % 2)[:, i * P:(i + 1) * P], ident[:, j:j + 1].to_broadcast([P, P]),
                                   stg[:, 12, :], start=True, stop=True)
                mm.then_inc(acb_ready, 1)

            def y_round(r, c):
                pe.wait_ge(g_ready, 4 * c + r + 1)
                if r >= 2:
                    pe.wait_ge(y_evac, 4 * c + r - 1)
                for i in range(2):
                    j = 2 * r + i
                    d = bk(6 + r % 2)[:, i * 256:(i + 1) * 256]
                    pe.matmul(d, xdt[:, j * P:(j + 1) * P], dec[:, r % 2, i * 256:(i + 1) * 256], start=True, stop=False)
                    mm = pe.matmul(d, state[:, j * P:(j + 1) * P], cts[:, r % 2, i * 256:(i + 1) * 256],
                                   start=False, stop=True)
                mm.then_inc(y_ready, 1)

            with pe.Fori(0, CHUNKS) as c:
                parts = [(p, n, part) for p in range(2) for n in range(2) for part in range(3)]

                def fill(count):
                    for _ in range(count):
                        p, n, part = parts.pop(0)
                        proj_part(p, n, part, 2 * c + 18 + p)

                fill(1)
                pe.wait_ge(stage_ready, c + 1)
                pe.wait_ge(state_new, c + 1)
                for j in range(8):
                    pe.transpose(bk(4 + j // 4)[:, (j % 4) * P:(j % 4 + 1) * P], stg[:, j, :], ident[:])
                for q, j in enumerate((8, 9, 12)):
                    pe.transpose(bk(6)[:, q * P:(q + 1) * P], stg[:, j, :], ident[:])
                for g in range(2):
                    mm = pe.matmul(bk(7)[:, g * P:(g + 1) * P], stg[:, 8 + g, :], stg[:, 10 + g, :], start=True, stop=True)
                mm.then_inc(t_ready, 1)
                fill(2)
                acum_rows(0, c)
                fill(1)
                acum_rows(1, c)
                fill(2)
                y_round(0, c)
                acum_rows(2, c)
                fill(2)
                y_round(1, c)
                acum_rows(3, c)
                fill(2)
                y_round(2, c)
                fill(1)
                y_round(3, c)
                fill(1)
                pe.wait_ge(xdte_ready, c + 1)
                for g in range(2):
                    mm = pe.matmul(bk(4 + g), bdt[:, g * P:(g + 1) * P], xdte[:, g * HB:(g + 1) * HB],
                                   start=True, stop=True)
                mm.then_inc(st_ready, 1)

            pe.wait_ge(lat_split, LAT)
            pe.wait_ge(proj_evac, 68)
            wq = [t[:, 0:768].rearrange("p (k n) -> p k n", n=256) for t in (hwh, hwl)]
            wk = [t[:, 768:1280].rearrange("p (k n) -> p k n", n=256) for t in (hwh, hwl)]

            def head_proj(u, b, h):
                if u == 0:
                    pe.wait_ge(hw_split, h + 1)
                if not (isinstance(h, int) and h == 0):
                    pe.wait_ge(hp_evac, 10 * h + u)
                elif u >= 4:
                    pe.wait_ge(hp_evac, max(u - 3, 8 if u >= 8 else 0))
                bk7 = unit_bank(u, h)
                n = u % 2
                r = slice(n * HB, (n + 1) * HB)
                if u < 4:
                    m0 = P * (u // 2)
                    for k in range(QLT):
                        mm = three(bk7, wq[0][:, k, m0:m0 + P], wq[1][:, k, m0:m0 + P], qlh[:, k, r], qll[:, k, r],
                                   k == 0, k == QLT - 1)
                elif u < 8:
                    m0 = P * (u // 2 - 2)
                    for k in range(KLT):
                        mm = three(bk7, wk[0][:, k, m0:m0 + P], wk[1][:, k, m0:m0 + P], ckh[:, k, r], ckl[:, k, r],
                                   k == 0, k == KLT - 1)
                else:
                    for j in range(4):
                        t = 4 * (u - 8) + j
                        mm = pe.transpose(bk7[:, j * P:(j + 1) * P], tb[:, t * P:(t + 1) * P], ident[:])
                mm.then_inc(hp_ready, 1)

            def scores(i, b, h):
                qnh, qnl, knh, knl, qr, _, _ = hd[b]
                if i == 0:
                    pe.wait_ge(qr_ready, h + 1)
                    pe.wait_ge(hp_evac, 10 * h + 10)
                first = isinstance(h, int) and h == 0 and i < 2
                if not first:
                    pe.wait_ge(exp_done, 8 * h + i - 1)
                q = slice(i * P, (i + 1) * P)
                end = (i + 1) * P
                for k0 in range(0, end, HB):
                    n = max(256, min(HB, end - k0))
                    d = bank[i % 2][:, k0 // HB, 0:n]
                    k = slice(k0, k0 + n)
                    pe.matmul(d, qnh[:, q], knh[:, k], start=True, stop=False)
                    pe.matmul(d, qnh[:, q], knl[:, k], start=False, stop=False)
                    pe.matmul(d, qnl[:, q], knh[:, k], start=False, stop=False)
                    pe.matmul(d, qr[:, q], krh[:, k], start=False, stop=False)
                    mm = pe.matmul(d, qr[:, q], krl[:, k], start=False, stop=True)
                mm.then_inc(s_ready, 1)

            def turn_probs(i, h):
                pe.wait_ge(p_ready, 8 * h + i + 1)
                for t0 in range(0, i + 1, 4):
                    n = TURNED[i] + t0 // 4
                    if not (isinstance(h, int) and h == 0 and n < 2):
                        pe.wait_ge(pt_split, 12 * h + n - 1)
                    for t in range(t0, min(i + 1, t0 + 4)):
                        mm = pe.transpose(bk(4 + n % 2)[:, (t - t0) * P:(t - t0 + 1) * P],
                                          prob[:, i % 2, t * P:(t + 1) * P], ident[:])
                    mm.then_inc(pt_ready, 1)

            def values(g, b, h):
                vh, vl = hd[b][5:]
                pe.wait_ge(pt_split, 12 * h + (4, 12)[g])
                if not (isinstance(h, int) and h == 0 and g == 0):
                    pe.wait_ge(o_ready, 2 * h + g)
                last = 4 * g + 3
                for t in range(last + 1):
                    c0 = max(0, t - 4 * g) * P
                    mm = three(bk(6)[:, c0:HB], vh[:, t, :], vl[:, t, :], pth[:, t, c0:HB], ptl[:, t, c0:HB],
                               t == 0, t == last)
                mm.then_inc(pv_ready, 1)

            def gated_sum(u):
                if u == 0:
                    pe.wait_ge(sqa_ready, HEADS)
                    pe.wait_ge(hp_evac, 10 * HEADS)
                else:
                    pe.wait_ge(sr_copied, u)
                pe.matmul(bk(7), ones[:], sqa[:, u // 2, (u % 2) * HB:(u % 2 + 1) * HB], start=True,
                          stop=True).then_inc(sr_mm, 1)

            def out_rows(n, s):
                q, half, kt = n % RING, n // 16, n % 16
                if s == 0:
                    pe.wait_ge(e_split, 2 * n + 2)
                if n == 0:
                    for ready, value in (((exp_done, 63),), ((exp_done, 64),), ((pt_split, 96),),
                                         ((o_ready, 16), (sr_copied, 4)))[s]:
                        pe.wait_ge(ready, value)
                if n == 16:
                    pe.wait_ge(res_ready, s + 1)
                rows = slice(s * P, (s + 1) * P)
                for col in range(2):
                    c = slice(col * HB, (col + 1) * HB)
                    mm = three(bk(2 * s + col), mxh[q][:, rows], mxl[q][:, rows], owh[q][:, c], owl[q][:, c],
                               kt == 0, kt == 15)
                if kt == 15:
                    mm.then_inc(bank_done, 1)
                elif s == RT - 1:
                    mm.then_inc(o_mm, 1)

            def head(h, b, fill):
                scores(0, b, h)
                scores(1, b, h)
                for i in range(8):
                    if i + 2 < 8:
                        scores(i + 2, b, h)
                    if fill:
                        head_proj(i, 1 - b, h + 1)
                    if i == 4:
                        values(0, b, h)
                    if not fill and 3 <= i < 7:
                        gated_sum(i - 3)
                    if not fill and i == 7:
                        for n in range(RING):
                            out_rows(n, 0)
                    turn_probs(i, h)
                if fill:
                    head_proj(8, 1 - b, h + 1)
                    head_proj(9, 1 - b, h + 1)
                else:
                    for n in range(RING):
                        out_rows(n, 1)
                values(1, b, h)

            for u in range(10):
                head_proj(u, 0, 0)
            pe.wait_ge(state_new, CHUNKS + 1)
            pe.wait_ge(y_evac, 4 * CHUNKS)
            pe.wait_ge(kr_ready, 1)
            head(0, 0, True)
            with pe.Fori(0, 3) as hp:
                head(2 * hp + 1, 1, True)
                head(2 * hp + 2, 0, True)
            head(7, 1, False)
            for s in (2, 3):
                for n in range(RING):
                    out_rows(n, s)
            for n in range(RING, 28):
                for s in range(RT):
                    out_rows(n, s)
            for s in range(RT):
                for n in range(28, 32):
                    out_rows(n, s)

        @block.scalar
        def _(act):
            ch = Chain(act, actc)
            act.wait_ge(w_in_sem[0], 32)
            act.activation(wh[:, 0, :, 0:ROPE + 16], wraw[:, 0, :, 0:ROPE + 16], ACT.Copy).then_inc(w_hi, 1)
            act.wait_ge(w_in_sem[1], 16)
            act.activation(wh[:, 1], wraw[:, 1], ACT.Copy).then_inc(w_hi, 1)
            act.wait_ge(small_in, 16 * 12)
            act.activation(small[DT0:DT0 + 16, 0:1], alg[DT0:DT0 + 16], ACT.Exp).then_inc(mod_ready, 1)
            act.wait_ge(ada_acc, KT + 1)
            for k in range(KT):
                act.wait_ge(xt_ready, k + 1)
                if k >= 2:
                    act.wait_ge(u_split, k - 1)
                act.activation(uf[:, k % 2, :], bank[2 + k % 2][:].rearrange("p a b -> p (a b)"), ACT.Identity,
                               bias=modc[:, k:k + 1], scale=modc[:, 8 + k:9 + k]).then_inc(uf_ready, 1)
            for n in range(NHALF):
                r = slice(n * HB, (n + 1) * HB)
                act.wait_ge(proj_ready, 4 * 0 + 1 + n)
                act.activation(dtv[DT0:DT0 + 16, r], bk(n)[DT0:DT0 + 16], ACT.Identity,
                               bias=dtb[DT0:DT0 + 16]).then_inc(dt_v, 1)
                act.activation(ost[0:ROPE, 0, r], bk(n)[0:ROPE], ACT.Copy).then_inc(proj_evac, 1)

            def high(p, arrived, tile, cols=P):
                act.wait_ge(w_in_sem[p], arrived)
                if not isinstance(tile, int) or tile >= 2:
                    act.wait_ge(proj_ready, 2 * tile - 2)
                act.activation(wh[:, p, :, 0:cols], wraw[:, p, :, 0:cols], ACT.Copy).then_inc(w_hi, 1)

            def evac(tile, p, dst):
                for n in range(NHALF):
                    act.wait_ge(proj_ready, 2 * tile + n + 1)
                    act.activation(dst[:, n * HB:(n + 1) * HB], bk(2 * p + n), ACT.Copy).then_inc(proj_evac, 1)

            high(0, 48, 2)
            evac(1, 1, qk[:, 0, :])
            high(1, 32, 3)
            act.wait_ge(dt_abs, 1)
            ch.link(act.activation(dtw[DT0:DT0 + 16], dtw[DT0:DT0 + 16], ACT.Exp))
            act.activation(dtw[DT0:DT0 + 16], dtw[DT0:DT0 + 16], ACT.Ln, bias=1.0).then_inc(dt_log, 1)
            for t in range(2, 6):
                evac(t, t % 2, qk[:, t - 1, :])
                high(t % 2, 16 * (t // 2 + 2) + (16 if t % 2 == 0 else 0), t + 2)
                if t == 3:
                    act.wait_ge(csn_arg, 1)
                    act.activation(csn[:], csn[:], ACT.Sin).then_inc(csn_ready, 1)
                if t == 4:
                    act.wait_ge(kr_t, 1)
                    act.dma_start(ropes[0:64], ropex[64:128]).then_inc(kr_swapped, 16)
                    act.dma_start(ropes[64:128], ropex[0:64]).then_inc(kr_swapped, 16)
                if t == 5:
                    act.wait_ge(kr_sum, 1)
                    act.activation(krh[:], ropex, ACT.Copy).then_inc(krh_ready, 1)

            def conv_tile(j, p, free, before):
                if free:
                    act.wait_ge(conv_done, j - 1)
                evac(j + 6, p, xr[:, p, 3:3 + S])
                high(p, 16 * (j // 2 + 5) + (16 if p == 0 else 0), j + 8)
                if before is not None:
                    act.wait_ge(conv_done, j)
                    act.activation(cx[:, before, :], cx[:, before, :], ACT.Silu).then_inc(silu_done, 1)

            conv_tile(0, 0, False, None)
            conv_tile(1, 1, False, 0)
            act.wait_ge(ss_mm, 1)
            for g in range(2):
                act.activation(rb[:, g, :], bank[2 + g][:].rearrange("p a b -> p (a b)"), ACT.Sqrt,
                               bias=rcst[:, 3:4], scale=1.0 / (384, 256)[g]).then_inc(root_ready, 1)
            with act.Fori(1, 6) as j2:
                for p in range(2):
                    j = 2 * j2 + p
                    act.wait_ge(conv_done, j - 1)
                    evac(j + 6, p, xr[:, p, 3:3 + S])
                    high(p, 16 * j2 + (96 if p == 0 else 80), j + 8)
                    act.wait_ge(conv_done, j)
                    v = cx[:, bass.ds(j - 1, 1), :]
                    act.activation(v, v, ACT.Silu).then_inc(silu_done, 1)
            act.wait_ge(conv_done, CONVT)
            act.activation(cx[:, CONVT - 1, :], cx[:, CONVT - 1, :], ACT.Silu).then_inc(silu_done, 1)

            def z_half(i, p, n):
                act.wait_ge(proj_ready, 4 * i + 36 + 2 * p + n + 1)
                if n == 0:
                    act.wait_ge(z_out[p], 16 * i + 16)
                act.activation(ost[:, p, n * HB:(n + 1) * HB], bk(2 * p + n), ACT.Silu).then_inc(proj_evac, 1)

            def exp_rows(r, c):
                act.wait_ge(acb_ready, 4 * c + r + 1)
                act.activation(exa[:, r % 2, :], bk(4 + r % 2), ACT.Exp).then_inc(exa_ready, 1)

            def exp_decay(r, c):
                act.wait_ge(arg_ready, 4 * c + r + 1)
                act.activation(dec[:, r % 2, :], dec[:, r % 2, :], ACT.Exp).then_inc(dec_ready, 1)

            def chunk(c, more):
                exp_rows(0, c)
                exp_decay(0, c)
                exp_rows(1, c)
                exp_decay(1, c)
                act.wait_ge(g_ready, 4 * c + 1)
                exp_rows(2, c)
                exp_decay(2, c)
                z_half(c, 0, 0)
                z_half(c, 0, 1)
                if more:
                    high(0, 16 * c + 192, 2 * c + 20)
                else:
                    latent_high(0)
                    latent_high(1)
                    act.wait_ge(hw_in, 64)
                    act.activation(hwh[:], hwr[:], ACT.Copy).then_inc(w_hi, 1)
                act.wait_ge(g_ready, 4 * c + 2)
                exp_rows(3, c)
                exp_decay(3, c)
                act.wait_ge(arg_ready, 4 * c + 4)
                act.activation(cdv[:, 2, :], cdv[:, 1, :], ACT.Exp).then_inc(dte_ready, 1)
                if not more:
                    latent_high(2)
                z_half(c, 1, 0)
                if not more:
                    latent_high(3)
                z_half(c, 1, 1)
                if more:
                    high(1, 16 * c + 176, 2 * c + 21)
                else:
                    latent_high(4)

            def latent_high(t):
                hi = qlh[:, t, :] if t < QLT else ckh[:, t - QLT, :]
                act.wait_ge(lat_in[t % 2], 16 * (t // 2 + 1))
                act.activation(hi, wraw[:, t % 2].rearrange("p k n -> p (k n)"), ACT.Copy).then_inc(lat_hi, 1)

            with act.Fori(0, CHUNKS - 1) as c:
                chunk(c, True)
            chunk(CHUNKS - 1, False)

            act.wait_ge(state_new, CHUNKS + 1)

            def head_high(h):
                act.wait_ge(hw_in, 64 * h + 64)
                if not isinstance(h, int) or h > 0:
                    act.wait_ge(hp_ready, 10 * h - 2)
                act.activation(hwh[:], hwr[:], ACT.Copy).then_inc(w_hi, 1)

            def hi_part(u, b, h):
                qnh, _, knh, _, _, vh, _ = hd[b]
                act.wait_ge(hp_ready, 10 * h + u + 1)
                n = u % 2
                r = slice(n * HB, (n + 1) * HB)
                if u < 2:
                    act.activation(qnh[:, r], unit_bank(u, h), ACT.Copy).then_inc(hp_hi, 1)
                elif u in (4, 5):
                    act.activation(knh[:, r], unit_bank(u, h), ACT.Copy).then_inc(hp_hi, 1)
                elif u in (6, 7):
                    if u == 6:
                        act.wait_ge(qr_sum, h + 1)
                    act.activation(tb[:, r], unit_bank(u, h), ACT.Copy).then_inc(hp_evac, 1)
                elif u >= 8:
                    act.activation(vh[:, 4 * (u - 8):4 * (u - 8) + 4, :], unit_bank(u, h).rearrange("p (t v) -> p t v", v=P),
                                   ACT.Copy).then_inc(hp_hi, 1)

            def qr_high(b, h):
                act.wait_ge(qr_sum, h + 1)
                act.activation(hd[b][4][:], ta[:], ACT.Copy).then_inc(qr_hi, 1)

            def probs(i, b, h):
                act.wait_ge(s_max, 8 * h + i + 1)
                if not (isinstance(h, int) and h == 0 and i < 2):
                    act.wait_ge(pt_ready, 12 * h + (-2, 0, 1, 2, 3, 4, 6, 8)[i])
                n = (i + 1) * P
                act.activation(prob[:, i % 2, 0:n], bank[i % 2][:].rearrange("p a b -> p (a b)")[:, 0:n], ACT.Exp,
                               bias=small[:, 8 + i % 2:9 + i % 2], scale=SCALE,
                               accum_out=small[:, 12 + i % 2:13 + i % 2]).then_inc(exp_done, 1)

            def turned_high(i, h):
                for t0 in range(0, i + 1, 4):
                    n = TURNED[i] + t0 // 4
                    w = min(i + 1, t0 + 4) - t0
                    act.wait_ge(pt_ready, 12 * h + n + 1)
                    if n == 4:
                        act.wait_ge(pv_ready, 2 * h + 1)
                    if n == 0 and not (isinstance(h, int) and h == 0):
                        act.wait_ge(pv_ready, 2 * h)
                    act.activation(pth[:, t0:t0 + w, (i % 4) * P:(i % 4 + 1) * P],
                                   bk(4 + n % 2)[:, 0:w * P].rearrange("p (t q) -> p t q", q=P),
                                   ACT.Copy).then_inc(pt_hi, 1)

            def gated_copy(u):
                act.wait_ge(sr_mm, u + 1)
                act.activation(rs[:, u // 2, (u % 2) * HB:(u % 2 + 1) * HB], bk(7), ACT.Identity, bias=rcst[:, 3:4],
                               scale=1.0 / HB).then_inc(sr_copied, 1)

            def out_high(n):
                q = n % RING
                if n == 0:
                    act.wait_ge(hp_ready, 10 * HEADS)
                if n == 3:
                    act.wait_ge(pv_ready, 2 * HEADS - 2)
                if n >= RING:
                    m = n - RING
                    if m % 16 == 15:
                        act.wait_ge(bank_done, RT)
                    else:
                        act.wait_ge(o_mm, m - m // 16 + 1)
                act.wait_ge(ow_gated, n + 1)
                act.activation(owh[q][:], owr[q][:], ACT.Copy).then_inc(e_hi, 1)
                act.wait_ge(mx_in[q], 16 * (n // RING + 1))
                if n % 16 >= HEADS:
                    act.wait_ge(mx_norm, 8 * (n // 16) + n % 16 - 7)
                act.activation(mxh[q][:], mxr[q][:], ACT.Copy).then_inc(e_hi, 1)

            def head(h, b, fill, more=True):
                probs(0, b, h)
                for i in range(8):
                    if i + 1 < 8:
                        probs(i + 1, b, h)
                    if fill and i not in (2, 3):
                        if i == 5:
                            qr_high(1 - b, h + 1)
                        hi_part(i, 1 - b, h + 1)
                    turned_high(i, h)
                    if not fill:
                        if 3 <= i < 7:
                            gated_copy(i - 3)
                        for n in {4: (0,), 5: (1,), 6: (2, 3)}.get(i, ()):
                            out_high(n)
                if fill:
                    hi_part(8, 1 - b, h + 1)
                    hi_part(9, 1 - b, h + 1)
                if fill and more:
                    head_high(h + 2)

            for u in range(10):
                if u == 6:
                    qr_high(0, 0)
                if u not in (2, 3):
                    hi_part(u, 0, 0)
            head_high(1)
            head(0, 0, True)
            with act.Fori(0, 2) as hp:
                head(2 * hp + 1, 1, True)
                head(2 * hp + 2, 0, True)
            head(5, 1, True)
            head(6, 0, True, False)
            head(7, 1, False)
            act.wait_ge(sr_inverse, 4)
            act.activation(rs[:].rearrange("p g s -> p (g s)"), rs[:].rearrange("p g s -> p (g s)"), ACT.Sqrt
                           ).then_inc(rs_ready, 1)

            def deviation(s):
                act.wait_ge(stat_ready, s + 1)
                act.activation(bns[:, s, 16:17], bns[:, s, 13:14], ACT.Sqrt, bias=small[:, 20:21]).then_inc(root_ln, 1)

            def centred(s):
                act.wait_ge(var_ready, s + 1)
                if s >= RT:
                    act.wait_ge(done[s % RT], 16)
                act.activation(yn[:, s % RT, :], res[:, s, :], ACT.Identity, bias=bns[:, s, 18:19],
                               scale=bns[:, s, 17:18]).then_inc(norm_ready, 1)

            for n in range(4, 32):
                out_high(n)
                if 20 <= n < 24:
                    deviation(n - 20)
                if 21 <= n < 25:
                    centred(n - 21)
            for s in range(RT, CHUNKS):
                deviation(s)
                centred(s)

        @block.vector
        def _(dve):
            ch = Chain(dve, dvec)
            dve.memset(small[:, 20:21], LN_EPS).then_inc(eps_ready, 1)
            dve.wait_ge(small_in, 16)
            for t in range(KT):
                dve.wait_ge(ada_in[t % 2], 16 * (t // 2 + 1))
                if t == 0:
                    dve.tensor_scalar(acc[:], wada[:, 0, :], ccol[:, 0:1], None, ALU.mult).then_inc(ada_acc, 1)
                else:
                    dve.wait_ge(ada_acc, t)
                    dve.scalar_tensor_tensor(acc[:], wada[:, t % 2, :], ccol[:, t:t + 1], acc[:], ALU.mult,
                                             ALU.add).then_inc(ada_acc, 1)
            dve.wait_ge(mod_mm, 1)
            ch.link(dve.tensor_copy(colv[:], bk(3)[:, 0:NVEC]))
            dve.wait_ge(mod_mm, 2)
            ch.link(dve.tensor_tensor(modc[:], bk(0)[:, 0:16], colv[:, 0:16], ALU.add))
            dve.tensor_scalar(modc[:, 8:16], modc[:, 8:16], 1.0, None, ALU.add).then_inc(ada_acc, 1)
            dve.wait_ge(small_in, 16 * 12)
            ch.link(dve.tensor_tensor(gate_b[:, 0:HB], gate_b[:, 0:HB], bk(1), ALU.add))
            dve.tensor_tensor(gate_b[:, HB:D], gate_b[:, HB:D], bk(2), ALU.add).then_inc(mod_ready, 1)
            for k in range(KT):
                dve.wait_ge(uf_ready, k + 1)
                ch.link(dve.tensor_copy(uh[:, k, :], uf[:, k % 2, :]))
                dve.tensor_tensor(ul[:, k, :], uf[:, k % 2, :], uh[:, k, :].bitcast(F32), ALU.subtract).then_inc(u_split, 1)

            ch.link(dve.memset(cx[:, 12, :], 0.0))
            d16 = slice(DT0, DT0 + 16)
            dve.wait_ge(dt_v, 2)
            dve.scalar_tensor_tensor(dtw[d16], dtv[d16], -1.0, dtv[d16], ALU.mult, ALU.min).then_inc(dt_abs, 1)
            dve.wait_ge(dt_log, 1)
            ch.link(dve.scalar_tensor_tensor(cx[d16, 12, :], dtv[d16], 0.0, dtw[d16], ALU.max, ALU.add))
            ch.link(dve.tensor_scalar(dtv[d16], cx[d16, 12, :], small[d16, 0:1], -1.0, ALU.mult, ALU.mult))
            for k in range(CHUNKS):
                r = slice(k * P, (k + 1) * P)
                dve.tensor_tensor_scan(cx[AC0:AC0 + 16, 12, r], ones[d16, 0:P], dtv[d16, r], 0.0, ALU.mult,
                                       ALU.add).then_inc(dt_done, 1)
            dve.wait_ge(rope_in, 32)
            ang = csn
            ch.link(dve.tensor_copy(turns, posi[:]))
            ch.link(dve.tensor_scalar(ang[:], turns, rcst[:, 0:1], None, ALU.mult))
            ch.link(dve.tensor_scalar(turns, ang[:], 1.0 / (2 * np.pi), rcst[:, 2:3], ALU.mult, ALU.add))
            ch.link(dve.tensor_scalar(turns, turns, MAGIC, None, ALU.add))
            ch.link(dve.tensor_scalar(turns, turns, MAGIC, None, ALU.subtract))
            for part in (PI2_A, PI2_B, PI2_C):
                ch.link(dve.scalar_tensor_tensor(ang[:], turns, -part, ang[:], ALU.mult, ALU.add))
            ch.link(dve.tensor_scalar(ang[:], ang[:], rcst[:, 1:2], None, ALU.add))
            dve.tensor_scalar(ang[:], ang[:], 3.1415925, -3.1415925, ALU.min, ALU.max).then_inc(csn_arg, 1)
            dve.wait_ge(z_out[0], 16)
            dve.wait_ge(z_out[1], 16)
            dve.wait_ge(csn_ready, 1)
            dve.tensor_tensor(ropex, ropex, csn[:], ALU.mult).then_inc(kr_t, 1)
            dve.wait_ge(kr_swapped, 32)
            dve.tensor_tensor(ropex, ropex, ropes, ALU.add).then_inc(kr_sum, 1)
            dve.wait_ge(krh_ready, 1)
            dve.tensor_tensor(krl[:], ropex, krh[:].bitcast(F32), ALU.subtract).then_inc(kr_ready, 1)
            dve.wait_ge(kr_ready, 1)
            dve.wait_ge(proj_evac, 12)
            ch.link(dve.tensor_tensor(rb[:, 0, :], qk[:, 0, :], qk[:, 0, :], ALU.mult))
            for t in (1, 2):
                ch.link(dve.tensor_tensor(sqs, qk[:, t, :], qk[:, t, :], ALU.mult))
                ch.link(dve.tensor_tensor(rb[:, 0, :], rb[:, 0, :], sqs, ALU.add))
            ch.link(dve.tensor_tensor(rb[:, 1, :], qk[:, 3, :], qk[:, 3, :], ALU.mult))
            ch.link(dve.tensor_tensor(sqs, qk[:, 4, :], qk[:, 4, :], ALU.mult))
            dve.tensor_tensor(rb[:, 1, :], rb[:, 1, :], sqs, ALU.add).then_inc(sq_ready, 1)
            for p in range(2):
                ch.link(dve.memset(xr[:, p, 0:3], 0.0))

            def conv(j, p, taps, bias, dst):
                dve.wait_ge(proj_evac, 2 * j + 14)
                ch.link(dve.tensor_scalar(dst, xr[:, p, 3:3 + S], taps(3), bias, ALU.mult, ALU.add))
                for k in (2, 1):
                    ch.link(dve.scalar_tensor_tensor(dst, xr[:, p, k:k + S], taps(k), dst, ALU.mult, ALU.add))
                dve.scalar_tensor_tensor(dst, xr[:, p, 0:S], taps(0), dst, ALU.mult, ALU.add).then_inc(conv_done, 1)

            for j in range(2):
                conv(j, j, lambda k, j=j: colv[:, C_CONVW + 12 * k + j:C_CONVW + 12 * k + j + 1],
                     colv[:, C_CONVB + j:C_CONVB + j + 1], cx[:, j, :])
            for g in range(2):
                dve.wait_ge(root_ready, g + 1)
                ch.link(dve.reciprocal(rb[:, g, :], rb[:, g, :]))
            for t in range(LAT):
                g = 0 if t < QLT else 1
                dve.scalar_tensor_tensor(qk[:, t, :], qk[:, t, :], colv[:, C_QG + t:C_QG + t + 1], rb[:, g, :],
                                         ALU.mult, ALU.mult).then_inc(lat_ready, 1)
            ch.loop(0, 6)
            with dve.Fori(1, 6) as j2:
                ch.base, ch.n = ch.start + 6 * (j2 - 1), 0
                for p in range(2):
                    j = 2 * j2 + p
                    conv(j, p, lambda k, j=j: colv[:, bass.ds(j + (C_CONVW + 12 * k), 1)],
                         colv[:, bass.ds(j + C_CONVB, 1)], cx[:, bass.ds(j, 1), :].rearrange("p a s -> p (a s)"))
            ch.end(5)

            dve.wait_ge(y_out, 16)
            dve.wait_ge(dt_done, CHUNKS)
            dve.wait_ge(silu_done, CONVT)
            dve.memset(state[:], 0.0).then_inc(state_new, 1)

            def heads(v, a, b):
                return v.rearrange("p (h l) -> p h l", h=a)

            def ssd_round(r, c):
                g = r // 2
                dve.wait_ge(exa_ready, 4 * c + r + 1)
                for i in range(4):
                    h = 4 * r + i
                    dve.scalar_tensor_tensor(dec[:, r % 2, i * P:(i + 1) * P], bk(4 + r % 2)[:, i * P:(i + 1) * P],
                                             bdt[:, 256 + AC0 + h:257 + AC0 + h], mask_ls[:], ALU.subtract, ALU.add)
                dve.tensor_tensor(cdv[:, 1, 4 * r:4 * r + 4], bk(4 + r % 2)[:, P - 1:HB:P],
                                  bdt[:, 256 + AC0 + 4 * r:260 + AC0 + 4 * r], ALU.subtract).then_inc(arg_ready, 1)
                dve.tensor_copy(cdv[:, 0, 4 * r:4 * r + 4], exa[:, r % 2, P - 1:HB:P])
                if r >= 2:
                    dve.wait_ge(y_ready, 4 * c + r - 1)
                ex = exa[:, r % 2, :].rearrange("p (h l) -> p h l", h=4)
                dve.tensor_tensor(cts[:, r % 2, :].rearrange("p (h l) -> p h l", h=4), ex,
                                  stg[:, 10 + g, :].unsqueeze(1).to_broadcast([P, 4, P]), ALU.mult)
                dve.wait_ge(dec_ready, 4 * c + r + 1)
                de = dec[:, r % 2, :].rearrange("p (h l) -> p h l", h=4)
                dve.tensor_tensor(de, de, cbs[:, g * P:(g + 1) * P].unsqueeze(1).to_broadcast([P, 4, P]),
                                  ALU.mult).then_inc(g_ready, 1)

            def y_out_round(r, c):
                dve.wait_ge(y_ready, 4 * c + r + 1)
                if r == 0:
                    dve.wait_ge(xd_ready, c + 1)
                v = bk(6 + r % 2).rearrange("p (j l) -> p j l", j=2)
                for q in range(2):
                    rows = slice(64 * q, 64 * q + 64)
                    ins = dve.tensor_tensor(xd[rows, 2 * r:2 * r + 2, :], v[rows, :, q * P:(q + 1) * P],
                                            xd[rows, 2 * r:2 * r + 2, :], ALU.add)
                ins.then_inc(y_evac, 1)

            with dve.Fori(0, CHUNKS) as c:
                dve.tensor_copy(stg[:], cx[:, :, bass.ds(c * P, P)]).then_inc(stage_ready, 1)
                dve.wait_ge(t_ready, c + 1)
                dve.tensor_copy(bdt[:], bk(6)[:, 0:3 * P]).then_inc(bdt_ready, 1)
                dve.tensor_copy(cbs[:], bk(7)[:, 0:2 * P])
                dve.wait_ge(bdt_ready, c + 1)
                for n in range(2):
                    ins = dve.tensor_tensor(xdt[:, n * HB:(n + 1) * HB].rearrange("p (h d) -> p h d", h=8),
                                            bk(4 + n).rearrange("p (h d) -> p h d", h=8),
                                            bdt[:, 256 + DT0 + 8 * n:264 + DT0 + 8 * n].unsqueeze(2).to_broadcast([P, 8, 64]),
                                            ALU.mult)
                ins.then_inc(xdt_ready, 1)
                ssd_round(0, c)
                ssd_round(1, c)
                y_out_round(0, c)
                ssd_round(2, c)
                y_out_round(1, c)
                ssd_round(3, c)
                y_out_round(2, c)
                dve.wait_ge(dte_ready, c + 1)
                dve.wait_ge(xdt_ready, c + 1)
                dve.tensor_tensor(xdte[:].rearrange("p (h d) -> p h d", h=16), xdt[:].rearrange("p (h d) -> p h d", h=16),
                                  cdv[:, 2, :].unsqueeze(2).to_broadcast([P, 16, 64]), ALU.mult).then_inc(xdte_ready, 1)
                y_out_round(3, c)
                st3 = state[:].rearrange("p (h d) -> p h d", h=16)
                dve.tensor_tensor(st3, st3, cdv[:, 0, :].unsqueeze(2).to_broadcast([P, 16, 64]),
                                  ALU.mult).then_inc(state_decayed, 1)
                dve.wait_ge(state_decayed, c + 1)
                dve.wait_ge(st_ready, c + 1)
                dve.tensor_tensor(state[:], state[:], bank[2][:].rearrange("p a b -> p (a b)"), ALU.add
                                  ).then_inc(state_new, 1)

            def lo_part(u, b, h):
                qnh, qnl, knh, knl, qr, vh, vl = hd[b]
                n = u % 2
                r = slice(n * HB, (n + 1) * HB)
                order = (0, 1, 4, 5, 8, 9)
                if u in order:
                    dve.wait_ge(hp_hi, 6 * h + order.index(u) + 1)
                if u < 2:
                    dve.tensor_tensor(qnl[:, r], unit_bank(u, h), qnh[:, r].bitcast(F32), ALU.subtract).then_inc(hp_evac, 1)
                elif u < 4:
                    dve.wait_ge(hp_ready, 10 * h + u + 1)
                    if u == 2 and not (isinstance(h, int) and h == 0):
                        dve.wait_ge(qr_hi, h)
                    dve.tensor_tensor(ta[:, r], unit_bank(u, h), csn[:, r], ALU.mult).then_inc(hp_evac, 1)
                elif u < 6:
                    dve.tensor_tensor(knl[:, r], unit_bank(u, h), knh[:, r].bitcast(F32), ALU.subtract).then_inc(hp_evac, 1)
                elif u >= 8:
                    t = 4 * (u - 8)
                    dve.tensor_tensor(vl[:, t:t + 4, :], unit_bank(u, h).rearrange("p (t v) -> p t v", v=P),
                                      vh[:, t:t + 4, :].bitcast(F32), ALU.subtract).then_inc(hp_evac, 1)

            def q_rope_sum(h):
                dve.wait_ge(qr_swapped, 32 * h + 32)
                dve.tensor_tensor(ta[:], ta[:], tb[:], ALU.add).then_inc(qr_sum, 1)

            def q_rope_low(b, h):
                qr = hd[b][4]
                dve.wait_ge(qr_hi, h + 1)
                dve.tensor_tensor(qr[64:128, :], ta[64:128, :], qr[64:128, :].bitcast(F32),
                                  ALU.subtract).then_inc(qr_ready, 1)

            def row_max(i, h):
                dve.wait_ge(s_ready, 8 * h + i + 1)
                v = bank[i % 2][:].rearrange("p a b -> p (a b)")
                ch.link(dve.tensor_tensor(v[:, i * P:(i + 1) * P], v[:, i * P:(i + 1) * P], mask_qk[:], ALU.add))
                ch.link(dve.tensor_reduce(small[:, 4 + i % 2:5 + i % 2], v[:, 0:(i + 1) * P], AX.X, ALU.max))
                if not (isinstance(h, int) and h == 0 and i < 2):
                    dve.wait_ge(exp_done, 8 * h + i - 1)
                dve.tensor_scalar(small[:, 8 + i % 2:9 + i % 2], small[:, 4 + i % 2:5 + i % 2], -SCALE, None,
                                  ALU.mult).then_inc(s_max, 1)

            def normalise(i, h):
                dve.wait_ge(exp_done, 8 * h + i + 1)
                ch.link(dve.reciprocal(small[:, 16 + i % 2:17 + i % 2], small[:, 12 + i % 2:13 + i % 2]))
                n = (i + 1) * P
                dve.tensor_scalar(prob[:, i % 2, 0:n], prob[:, i % 2, 0:n], small[:, 16 + i % 2:17 + i % 2], None,
                                  ALU.mult).then_inc(p_ready, 1)

            def turned_low(i, h):
                for t0 in range(0, i + 1, 4):
                    n = TURNED[i] + t0 // 4
                    w = min(i + 1, t0 + 4) - t0
                    dve.wait_ge(pt_hi, 12 * h + n + 1)
                    q = slice((i % 4) * P, (i % 4 + 1) * P)
                    dve.tensor_tensor(ptl[:, t0:t0 + w, q], bk(4 + n % 2)[:, 0:w * P].rearrange("p (t q) -> p t q", q=P),
                                      pth[:, t0:t0 + w, q].bitcast(F32), ALU.subtract).then_inc(pt_split, 1)

            def gate_out(g, h):
                dve.wait_ge(pv_ready, 2 * h + g + 1)
                if g == 0:
                    dve.wait_ge(z_in, 16 * h + 16)
                    if not isinstance(h, int) or h > 0:
                        dve.wait_ge(o_out, 16 * h)
                r = slice(g * HB, (g + 1) * HB)
                dve.tensor_tensor(ob[:, r], bk(6), zs[:, r], ALU.mult).then_inc(o_ready, 1)

            def gated_inverse(u):
                dve.wait_ge(sr_copied, u + 1)
                v = rs[:, u // 2, (u % 2) * HB:(u % 2 + 1) * HB]
                dve.reciprocal(v, v).then_inc(sr_inverse, 1)

            def out_low(n):
                q, half, kt = n % RING, n // 16, n % 16
                if kt >= HEADS:
                    j = kt - HEADS
                    if n == HEADS:
                        dve.wait_ge(rs_ready, 1)
                    dve.wait_ge(mx_in[q], 16 * (n // RING + 1))
                    dve.scalar_tensor_tensor(mxr[q][:], mxr[q][:], colv[:, C_SG + j:C_SG + j + 1],
                                             rs[:, j // 4, half * HB:(half + 1) * HB], ALU.mult,
                                             ALU.mult).then_inc(mx_norm, 1)
                dve.wait_ge(e_hi, 2 * n + 1)
                dve.tensor_tensor(owl[q][:], owr[q][:], owh[q][:].bitcast(F32), ALU.subtract).then_inc(e_split, 1)
                dve.wait_ge(e_hi, 2 * n + 2)
                dve.tensor_tensor(mxl[q][:], mxr[q][:], mxh[q][:].bitcast(F32), ALU.subtract).then_inc(e_split, 1)

            def head(h, b, fill):
                row_max(0, h)
                row_max(1, h)
                normalise(0, h)
                for i in range(8):
                    if i + 1 < 8:
                        normalise(i + 1, h)
                    if i + 2 < 8:
                        row_max(i + 2, h)
                    if fill:
                        lo_part(i, 1 - b, h + 1)
                        if i == 4:
                            q_rope_sum(h + 1)
                        if i == 5:
                            q_rope_low(1 - b, h + 1)
                    turned_low(i, h)
                    if i == 4:
                        gate_out(0, h)
                    if not fill:
                        if 3 <= i < 7:
                            gated_inverse(i - 3)
                        for n in {4: (0,), 5: (1,), 6: (2, 3)}.get(i, ()):
                            out_low(n)
                if fill:
                    lo_part(8, 1 - b, h + 1)
                    lo_part(9, 1 - b, h + 1)
                gate_out(1, h)

            for u in range(10):
                lo_part(u, 0, 0)
                if u == 5:
                    q_rope_sum(0)
                    q_rope_low(0, 0)
            head(0, 0, True)
            per = 2 * (8 * 2 + 8)
            ch.loop(0, per)
            with dve.Fori(0, 3) as hp:
                ch.base, ch.n = ch.start + per * hp, 0
                head(2 * hp + 1, 1, True)
                head(2 * hp + 2, 0, True)
            ch.end(3)
            head(7, 1, False)

            def residual(s):
                dve.wait_ge(bank_done, s + 1)
                return dve.scalar_tensor_tensor(res[:, s, :], res[:, s, :], ALPHA,
                                                bank[s % RT][:].rearrange("p a b -> p (a b)"), ALU.mult, ALU.add)

            def statistics(s):
                ch.link(dve.bn_stats(bns[:, s, 0:6], res[:, s, 0:HB]))
                ch.link(dve.bn_stats(bns[:, s, 6:12], res[:, s, HB:D]))
                dve.bn_aggr(bns[:, s, 12:14], bns[:, s, 0:12]).then_inc(stat_ready, 1)

            def scales(s):
                dve.wait_ge(root_ln, s + 1)
                ch.link(dve.reciprocal(bns[:, s, 17:18], bns[:, s, 16:17]))
                dve.scalar_tensor_tensor(bns[:, s, 18:19], bns[:, s, 12:13], -1.0, bns[:, s, 17:18], ALU.mult,
                                         ALU.mult).then_inc(var_ready, 1)

            def gain(s):
                dve.wait_ge(norm_ready, s + 1)
                dve.tensor_tensor(yn[:, s % RT, :], yn[:, s % RT, :], lgb[:], ALU.mult).then_inc(gain_ready, 1)
                dve.wait_ge(gain_ready, s + 1)
                dve.tensor_tensor(yn[:, s % RT, 0:HB], yn[:, s % RT, 0:HB], lbb[:, 0:HB], ALU.add).then_inc(y_final, 1)

            for n in range(4, 32):
                out_low(n)
                if n == 18:
                    dve.wait_ge(res_in, 16)
                    for s in range(RT):
                        residual(s).then_inc(res_ready, 1)
                    dve.wait_ge(res_ready, RT)
                    dve.wait_ge(ln_in, 32)
                if 20 <= n < 24:
                    statistics(n - 20)
                if 21 <= n < 25:
                    scales(n - 21)
                if 22 <= n < 26:
                    gain(n - 22)
            for s in range(RT, CHUNKS):
                ch.link(residual(s))
                statistics(s)
                if s > RT:
                    gain(s - 1)
                scales(s)
            gain(CHUNKS - 1)


_INS = ["x", "c", "positions", "w_ada", "b_ada", "w_in", "q_norm_g", "w_qb", "kv_norm_g", "w_kvb", "conv_w", "conv_b",
        "dt_bias", "a_log", "d_skip", "ssm_norm_g", "w_out", "ln_g", "ln_b"]


def rope_constants():
    half = ROPE // 2
    inv = (np.float32(1.0) / np.power(np.float32(10000.0), np.arange(half, dtype=np.float32) / np.float32(half))).astype(np.float32)
    phase = np.repeat([np.pi / 2, np.pi / 2, np.pi, 0.0], half)
    return np.stack([np.tile(inv, 4), phase, phase / (2 * np.pi), np.full(P, RMS_EPS)], axis=1).astype(np.float32)


def kernel(**inputs):
    import concourse.bacc as bacc
    from concourse.bass_utils import run_bass_kernel_spmd

    nc = bacc.Bacc("TRN2", target_bir_lowering=False, num_devices=1)
    arrays, args = {}, []
    for name in _INS:
        a = np.ascontiguousarray(inputs[name])
        arrays[f"in_{name}"] = a
        args.append(nc.dram_tensor(f"in_{name}", a.shape, mybir.dt.from_np(a.dtype), kind="ExternalInput").ap())
    arrays["in_rope_constants"] = rope_constants()
    args.append(nc.dram_tensor("in_rope_constants", [P, 4], F32, kind="ExternalInput").ap())
    args.append(nc.dram_tensor("out_0", [1, S, D], F32, kind="ExternalOutput").ap())
    build_layer(nc, *args)
    r = run_bass_kernel_spmd(nc, [arrays], core_ids=[0])
    return r.results[0]["out_0"]
```

```python
from contextlib import ExitStack

import numpy as np

import concourse.bass as bass
from concourse import mybir

F32 = mybir.dt.float32
F32R = mybir.dt.float32r
I32 = mybir.dt.int32
ALU = mybir.AluOpType
ACT = mybir.ActivationFunctionType
AX = mybir.AxisListType

P = 128
D = 1024
S = 1024
KT = D // P
HB = 512
NHALF = S // HB
HEADS = 8
ROPE = 64
QW = 192
QLT = 3
KLT = 2
LAT = QLT + KLT
SSM_H = 16
NST = 8
CONVT = 12
TAPS = 4
CHUNKS = S // P
W_KV_ROPE = 640
W_ZATT = 704
W_XBC = 1728
W_DT = 3264
W_ZSSM = 3280
Z_ATT0 = 5
Z_SSM0 = 13
C_CONVW, C_CONVB, C_QG, C_KVG, C_SG, NVEC = 24, 72, 84, 87, 89, 97
ALPHA = 2.0 ** 0.25
RMS_EPS = 1e-6
LN_EPS = 1e-5
SCALE = 192.0 ** -0.5
NEG = -1.0e30
MAGIC = 12582912.0
PI2_A = 6.28125
PI2_B = 0.0019350051879882812
PI2_C = float(2 * np.pi - 6.28125 - 0.0019350051879882812)
RT = 4
RING = 4
TURNED = (0, 1, 2, 3, 4, 6, 8, 10)
DT0, AC0 = 64, 96
B0 = 64
R_HI, R_LO, R_SEL, NROPEC = 4, 5, 6, 14


def build_layer(nc, x, c, pos, w_ada, b_ada, w_in, qg, w_qb, kvg, w_kvb, conv_w, conv_b, dt_bias,
                a_log, d_skip, ssmg, w_out, ln_g, ln_b, const_in, out):
    scr = nc.dram_tensor("proj_scratch", [21, P, S], F32).ap()
    scy = nc.dram_tensor("ssm_scratch", [NST, P, S], F32).ap()
    scg = nc.dram_tensor("ssm_gated_scratch", [NST, P, S], F32).ap()
    sco = nc.dram_tensor("attn_scratch", [HEADS, P, S], F32).ap()

    ctx = ExitStack()
    with ctx:
        def at(offset, spec):
            made = []
            for name, shape, dt in spec:
                made.append(nc.alloc_sbuf_tensor_at(name, shape, dt, offset=offset))
                offset += -(-int(np.prod(shape[1:])) * 4 // 32) * 32
            return made, offset

        def sem(name):
            return ctx.enter_context(nc.semaphore(name))

        base = -(-nc.sbuf_base // 64) * 64
        (ident, ones, mask_qk, mask_ls, colv, modc, gate_b, dsk, dsr, dtb, alg, ccol, rcst, selc, small), end_c = at(base, [
            ("ident", [P, P], F32), ("ones", [P, P], F32), ("mask_qk", [P, P], F32), ("mask_ls", [P, P], F32),
            ("colv", [P, NVEC], F32), ("modc", [P, 16], F32), ("gate_b", [P, D], F32), ("dsk", [P, NST], F32), ("dsr", [P, SSM_H], F32),
            ("dtb", [P, 1], F32), ("alg", [P, 1], F32), ("ccol", [P, KT], F32), ("rcst", [P, NROPEC], F32), ("selc", [P, 8], F32R),
            ("small", [P, 32], F32)])
        reg_a, reg_b = end_c, end_c + 55 * 1024
        limit = nc.sbuf_usable_end

        (xin,), _ = at(reg_a, [("xin", [P, CHUNKS, D], F32)])
        (cx,), e = at(reg_a, [("cx", [P, 13, S], F32)])
        assert e <= reg_b
        (qlh, qll, ckh, ckl, hwr, hwh, hwl), e = at(reg_a, [
            ("qlh", [P, QLT, S], F32R), ("qll", [P, QLT, S], F32R), ("ckh", [P, KLT, S], F32R),
            ("ckl", [P, KLT, S], F32R), ("hwr", [P, 1280], F32), ("hwh", [P, 1280], F32R), ("hwl", [P, 1280], F32R)])
        assert e <= reg_b
        top = (limit - 3 * S * 4) // 64 * 64
        (csn, krh, krl), _ = at(top, [("csn", [P, S], F32), ("krh", [P, S], F32R), ("krl", [P, S], F32R)])

        (uh, ul, wraw, wh, wl, ost), b1 = at(reg_b, [
            ("uh", [P, KT, S], F32R), ("ul", [P, KT, S], F32R), ("wraw", [P, 2, KT, P], F32),
            ("wh", [P, 2, KT, P], F32R), ("wl", [P, 2, KT, P], F32R), ("ost", [P, 2, S], F32)])
        (acc, wada, uf, vrow), e = at(b1, [("acc", [P, 2, 2 * P], F32), ("wada", [P, 4, KT, 2 * P], F32),
                                           ("uf", [P, 2, S], F32), ("vrow", [NVEC, P], F32)])
        assert e <= limit
        (qk, xr, rb), e = at(b1, [("qk", [P, LAT, S], F32), ("xr", [P, 2, S + 4], F32), ("rb", [P, 2, S], F32)])
        assert e <= top
        posi = nc.alloc_sbuf_tensor_at("posi", [P, S], I32, offset=e - 8 * S)
        ropex, ropes, turns, dtv, sqs, dtw = cx[:, 8, :], cx[:, 9, :], cx[:, 10, :], cx[:, 11, :], cx[:, 10, :], rb[:, 1, :]
        ach = nc.alloc_sbuf_tensor_at("ach", [P, S], F32R, offset=reg_a + 10 * S * 4)
        (stg, bd, xdt, xdte, bdt, cbs, dec, exa, cts, state, xd, cdv), e = at(b1, [
            ("stg", [P, 13, P], F32), ("bd", [P, 2, P], F32R), ("xdt", [P, D], F32), ("xdte", [P, D], F32), ("bdt", [P, B0 + 2 * P], F32),
            ("cbs", [P, 2 * P], F32), ("dec", [P, 2, HB], F32), ("exa", [P, 2, HB], F32),
            ("cts", [P, 2, HB], F32), ("state", [P, D], F32), ("xd", [P, NST, P], F32), ("cdv", [P, 3, SSM_H], F32)])
        assert e <= top

        hd = [at(reg_b + i * 28 * 1024, [
            (f"qnh{i}", [P, S], F32R), (f"qnl{i}", [P, S], F32R), (f"knh{i}", [P, S], F32R),
            (f"knl{i}", [P, S], F32R), (f"qr{i}", [P, S], F32R), (f"vh{i}", [P, CHUNKS, P], F32R),
            (f"vl{i}", [P, CHUNKS, P], F32R)])[0] for i in range(2)]
        (rl, pth, ptl, prob, zs, ob), ta_at = at(reg_b + 56 * 1024, [
            ("rl", [P, 2, S], F32), ("pth", [P, CHUNKS, HB], F32R), ("ptl", [P, CHUNKS, HB], F32R),
            ("prob", [P, 2, S], F32), ("zs", [P, S], F32), ("ob", [P, S], F32)])
        (ta, tb, sqa, vt), e = at(ta_at, [("ta", [P, S], F32), ("tb", [P, S], F32), ("sqa", [P, 2, S], F32), ("vt", [P, S], F32)])
        assert e <= top

        MX, OW = HB * 4, D * 4
        slot_at = [reg_a + q * 2 * (MX + OW) for q in range(3)] + [reg_b]
        raw_at = [reg_b + 2 * (MX + OW), reg_b + 3 * (MX + OW), reg_a + 40 * 1024, reg_a + 40 * 1024 + MX + OW]
        mxh, mxl, owh, owl = zip(*[at(o, [(f"mxh{q}", [P, HB], F32R), (f"mxl{q}", [P, HB], F32R), (f"owh{q}", [P, D], F32R),
                                          (f"owl{q}", [P, D], F32R)])[0] for q, o in enumerate(slot_at)])
        mxr, owr = zip(*[at(o, [(f"mxr{q}", [P, HB], F32), (f"owr{q}", [P, D], F32)])[0] for q, o in enumerate(raw_at)])
        (rs,), _ = at(ta_at, [("rs", [P, 2, S], F32)])
        (res, lgb, lbb, yn, bns), e = at(reg_b + 28 * 1024, [
            ("res", [P, CHUNKS, D], F32), ("lgb", [P, D], F32), ("lbb", [P, D], F32), ("yn", [P, RT, D], F32),
            ("bns", [P, CHUNKS, 24], F32)])
        assert e <= ta_at

        bank = [ctx.enter_context(nc.psum_tensor(f"bank{i}", [P, 2, HB], F32)) for i in range(4)]

        def bk(i):
            return bank[i // 2][:, i % 2, :]

        FIRST = (2, 3, 0, 1, 4, 5, 6, 7, 8, 9)

        def unit_at(u, h):
            return FIRST.index(u) if isinstance(h, int) and h == 0 else u

        def unit_bank(u, h):
            if isinstance(h, int) and h == 0:
                return bk(4 + FIRST.index(u) % 4)
            return bk(6) if u in (1, 3) else bk(7)

        HW_PART = (slice(0, 768), slice(768, 1280))

        c_in = sem("c_in")
        vec_in = sem("vec_in")
        small_in = sem("small_in")
        x_in = [sem(f"x_in{k}") for k in range(KT)]
        ada_in = [sem(f"ada_in{q}") for q in range(4)]
        colv_mm = sem("colv_mm")
        colv_ready = sem("colv_ready")
        gate_in = sem("gate_in")
        gate_acc = sem("gate_acc")
        gate_mm = sem("gate_mm")
        gate_ready = sem("gate_ready")
        consts = sem("consts")
        ada_acc = sem("ada_acc")
        xt_ready = sem("xt_ready")
        uf_ready = sem("uf_ready")
        u_split = sem("u_split")
        u_split_last = sem("u_split_last")
        mod_mm = sem("mod_mm")
        w_in_sem = [sem("w_raw_in0"), sem("w_raw_in1")]
        w_hi = sem("w_hi")
        w_split = sem("w_split")
        proj_ready = sem("proj_ready")
        proj_evac = sem("proj_evac")
        dt_v = sem("dt_v")
        dt_abs = sem("dt_abs")
        dt_log = sem("dt_log")
        dt_done = sem("dt_done")
        conv_done = sem("conv_done")
        silu_done = sem("silu_done")
        sq_ready = sem("sq_ready")
        ss_mm = sem("ss_mm")
        root_ready = sem("root_ready")
        lat_ready = sem("lat_ready")
        z_out = [sem("z_out0"), sem("z_out1")]
        dvec = sem("dve_chain")
        poolc = sem("pool_chain")
        actc = sem("act_chain")
        stage_ready = sem("stage_ready")
        bd_ready = sem("bd_ready")
        t_ready = sem("t_ready")
        bdt_ready = sem("bdt_ready")
        xdt_ready = sem("xdt_ready")
        acb_ready = sem("acb_ready")
        exa_ready = sem("exa_ready")
        arg_ready = sem("arg_ready")
        dec_ready = sem("dec_ready")
        g_ready = sem("g_ready")
        y_ready = sem("y_ready")
        y_evac = sem("y_evac")
        xd_ready = sem("xd_ready")
        state_decayed = sem("state_decayed")
        dte_ready = sem("dte_ready")
        xdte_ready = sem("xdte_ready")
        st_ready = sem("st_ready")
        state_new = sem("state_new")
        y_out = sem("y_out")

        lat_in = [sem("lat_in0"), sem("lat_in1")]
        lat_hi = sem("lat_hi")
        lat_split = sem("lat_split")
        rope_in = sem("rope_in")
        csn_ready = sem("csn_ready")
        csn_arg = sem("csn_arg")
        kr_t = sem("kr_t")
        kr_swapped = sem("kr_swapped")
        kr_sum = sem("kr_sum")
        krh_ready = sem("krh_ready")
        kr_ready = sem("kr_ready")
        hw_in = sem("hw_in")
        hw_hi = sem("hw_hi")
        hw_split = sem("hw_split")
        hp_ready = sem("hp_ready")
        hp_hi = sem("hp_hi")
        hp_evac = sem("hp_evac")
        qr_swapped = sem("qr_swapped")
        qr_sum = sem("qr_sum")
        qr_hi = sem("qr_hi")
        qr_ready = sem("qr_ready")
        s_ready = sem("s_ready")
        s_max = sem("s_max")
        exp_done = sem("exp_done")
        p_ready = sem("p_ready")
        pt_ready = sem("pt_ready")
        pt_hi = sem("pt_hi")
        pt_split = sem("pt_split")
        pv_ready = sem("pv_ready")
        o_ready = sem("o_ready")
        o_out = sem("o_out")
        z_in = sem("z_in")
        y_in = sem("y_in")
        zy_in = sem("zy_in")
        yg_ready = sem("yg_ready")
        yg_out = sem("yg_out")
        sqa_ready = sem("sqa_ready")
        sr_mm = sem("sr_mm")
        sr_copied = sem("sr_copied")
        sr_inverse = sem("sr_inverse")

        mx_in = [sem(f"mx_in{q}") for q in range(RING)]
        mx_norm = sem("mx_norm")
        ow_in = [sem(f"ow_in{q}") for q in range(RING)]
        ow_gated = sem("ow_gated")
        e_hi = sem("e_hi")
        e_split = sem("e_split")
        o_mm = sem("o_mm")
        bank_done = sem("bank_done")
        left_done = sem("left_done")
        res_ready = sem("res_ready")
        res_in = sem("res_in")
        ln_in = sem("ln_in")
        rs_ready = sem("rs_ready")
        norm_ready = sem("norm_ready")
        root_ln = sem("root_ln")
        stat_ready = sem("stat_ready")
        var_ready = sem("var_ready")
        gain_ready = sem("gain_ready")
        y_final = sem("y_final")
        y_final_pool = sem("y_final_pool")
        done = [sem(f"out_stored{q}") for q in range(RT)]

        block = ctx.enter_context(nc.Block())

        class Chain:

            def __init__(self, eng, s):
                self.eng, self.s, self.n, self.base = eng, s, 0, 0

            def link(self, ins):
                ins.then_inc(self.s, 1)
                self.n += 1
                self.eng.wait_ge(self.s, self.base + self.n)

            def loop(self, i, per):
                self.start, self.per = self.n, per
                self.base, self.n = self.start + per * i, 0

            def end(self, count):
                assert self.n == self.per, (self.n, self.per)
                self.base, self.n = 0, self.start + self.per * count

        RIGHT, LEFT = slice(HB, D), slice(0, HB)

        def dt_columns(w):
            return w[:, 0, :, ROPE:P].rearrange("p k (r h) -> p k r h", h=16)

        def u_low(eng, k):
            eng.wait_ge(uf_ready, k + 1)
            return eng.tensor_tensor(ul[:, k, :], uf[:, k % 2, :], uh[:, k, :].bitcast(F32), ALU.subtract)

        def rope_sum(eng, h):
            eng.wait_ge(qr_swapped, 32 * h + 32)
            eng.tensor_tensor(ta[:], ta[:], tb[:], ALU.add).then_inc(qr_sum, 1)

        def rope_low(eng, b, h):
            qr = hd[b][4]
            eng.wait_ge(qr_hi, h + 1)
            eng.tensor_tensor(qr[64:128, :], ta[64:128, :], qr[64:128, :].bitcast(F32),
                              ALU.subtract).then_inc(qr_ready, 1)

        w3 = w_in[0].rearrange("(k p) n -> p k n", p=P)

        @block.sync
        def _(sp):
            sp.dma_start(ccol[:], c[0].rearrange("(p t) -> p t", t=KT)).then_inc(c_in, 16)

            def vectors():
                for dst, src in (
                    (vrow[0:24], b_ada[0].rearrange("(t p) -> t p", p=P)),
                    (vrow[24:72], conv_w[0].rearrange("k (j p) -> (k j) p", p=P)),
                    (vrow[72:84], conv_b[0].rearrange("(t p) -> t p", p=P)),
                    (vrow[84:87], qg[0].rearrange("(t p) -> t p", p=P)),
                    (vrow[87:89], kvg[0].rearrange("(t p) -> t p", p=P)),
                    (vrow[89:97], ssmg[0].rearrange("(t p) -> t p", p=P)),
                ):
                    sp.dma_start(dst, src).then_inc(vec_in, 16)

            def small_inputs():
                for dst, src in (
                    (gate_b[:], b_ada[0, 2 * D:3 * D].partition_broadcast(P)),
                    (dsr[:], d_skip[0].partition_broadcast(P)),
                    (rcst[:], const_in),
                    *[(dst[o:o + 16], src[0].rearrange("(h a) -> h a", a=1))
                      for dst, src in ((dtb, dt_bias), (alg, a_log)) for o in range(DT0, P, 16)],
                ):
                    sp.dma_start(dst, src).then_inc(small_in, 16)

            ada = w_ada[0].rearrange("(p t) (c k n) -> p t c k n", t=KT, k=KT, n=P)
            for k in range(KT):
                sp.dma_start(xin[:, :, k * P:(k + 1) * P],
                             x[0, :, k * P:(k + 1) * P].rearrange("(s p) n -> p s n", p=P)).then_inc(x_in[k], 16)
                if k >= 4:
                    sp.wait_ge(ada_acc, k - 3)
                for part in range(2):
                    sp.dma_start(wada[:, k % 4, :, part * P:(part + 1) * P], ada[:, :, part, k, :]
                                 ).then_inc(ada_in[k % 4], 16)
                if k == 0:
                    vectors()
                    sp.dma_start(wraw[:, 0, :, 0:ROPE], w3[:, :, W_KV_ROPE:W_KV_ROPE + ROPE]).then_inc(w_in_sem[0], 16)
                    sp.dma_start(wraw[:, 0, :, ROPE:ROPE + 16], w3[:, :, W_DT:W_DT + 16]).then_inc(w_in_sem[0], 16)
                    sp.dma_start(wraw[:, 1], w3[:, :, 0:P]).then_inc(w_in_sem[1], 16)
                if k == 3:
                    small_inputs()

            def address(v):
                return v if isinstance(v, int) else sp.snap(v)

            def load_tile(p, col, wait):
                src = w3[:, :, bass.ds(address(col), P)]
                if wait is not None:
                    sp.wait_ge(w_split, wait)
                sp.dma_start(wraw[:, p], src).then_inc(w_in_sem[p], 16)

            def store_z(tile, p, i):
                dst = scr[bass.ds(address(i), 1)]
                sp.wait_ge(proj_evac, tile)
                sp.dma_start(dst, ost[:, p, :]).then_inc(z_out[p], 16)

            def store_y(i):
                col = address(i * P)
                sp.wait_ge(y_evac, 4 * i + 4)
                sp.dma_start(scy[:, :, bass.ds(col, P)].rearrange("j p l -> p j l"), xd[:]).then_inc(y_out, 16)

            for t in range(2, 6):
                load_tile(t % 2, (t - 1) * P, t - 1)
                if t == 3:
                    sp.wait_ge(xt_ready, KT)
                    sp.dma_start(cx[:, 0:KT, :], w_ada[0].rearrange("(p t) n -> p t n", t=KT)[:, :, 2 * D:3 * D]
                                 ).then_inc(gate_in, 16)
            sp.dma_start(posi[:], pos[0].partition_broadcast(P)).then_inc(rope_in, 16)
            sp.wait_ge(proj_evac, 2)
            sp.dma_start(ropex[96:128], ost[0:32, 0, :]).then_inc(rope_in, 16)
            sp.dma_start(ropex[0:64], ost[0:64, 0, :]).then_inc(z_out[0], 16)
            sp.dma_start(ropex[64:96], ost[32:64, 0, :]).then_inc(z_out[1], 16)
            with sp.Fori(0, 4) as j:
                for p in range(2):
                    load_tile(p, W_XBC + (2 * j + p) * P, 2 * j + p + 5)
            sp.wait_ge(lat_ready, LAT)
            sp.dma_start(scr[0:5].rearrange("t p s -> p t s"), qk[:]).then_inc(y_out, 16)
            with sp.Fori(4, 6) as j:
                for p in range(2):
                    load_tile(p, W_XBC + (2 * j + p) * P, 2 * j + p + 5)
            load_tile(0, W_ZATT, 17)
            load_tile(1, W_ZSSM, 18)
            with sp.Fori(0, CHUNKS - 1) as i:
                load_tile(0, W_ZATT + (i + 1) * P, 2 * i + 19)
                load_tile(1, W_ZSSM + (i + 1) * P, 2 * i + 20)
                store_z(4 * i + 38, 0, i + Z_ATT0)
                store_z(4 * i + 40, 1, i + Z_SSM0)
                store_y(i)
            def head_weights(h, wait=None):
                q0, q1, q2 = (address(h * QW + o) for o in (0, 160, 128))
                kv0 = address(h * 256)
                if wait is not None:
                    sp.wait_ge(hw_split, 2 * wait)
                q = w_qb[0].rearrange("(k p) n -> p k n", p=P)
                kv = w_kvb[0].rearrange("(k p) n -> p k n", p=P)
                qv = hwr[:, 0:768].rearrange("p (k n) -> p k n", n=256)
                sp.dma_start(qv[:, :, 0:QW], q[:, :, bass.ds(q0, QW)]).then_inc(hw_in, 16)
                sp.dma_start(qv[:, :, 192:224], q[:, :, bass.ds(q1, 32)]).then_inc(hw_in, 16)
                sp.dma_start(qv[:, :, 224:256], q[:, :, bass.ds(q2, 32)]).then_inc(hw_in, 16)
                sp.dma_start(hwr[:, 768:1280].rearrange("p (k n) -> p k n", n=256),
                             kv[:, :, bass.ds(kv0, 256)]).then_inc(hw_in, 16)

            i = CHUNKS - 1
            def latent(t):
                sp.wait_ge(w_split, 33 + t if t < 2 else 34)
                if t >= 2:
                    sp.wait_ge(lat_split, t - 1)
                sp.dma_start(wraw[:, t % 2], scr[t].rearrange("p (k n) -> p k n", n=P)).then_inc(lat_in[t % 2], 16)

            sp.wait_ge(stage_ready, CHUNKS)
            sp.wait_ge(y_out, 16)
            latent(0)
            latent(1)
            head_weights(0)
            latent(2)
            store_z(4 * i + 38, 0, i + Z_ATT0)
            latent(3)
            latent(4)
            store_z(4 * i + 40, 1, i + Z_SSM0)
            store_y(i)
            sp.wait_ge(z_out[0], 16 * 9)
            sp.wait_ge(z_out[1], 16 * 9)
            sp.wait_ge(y_out, 16 * CHUNKS + 16)
            sp.wait_ge(proj_ready, 68)
            sp.wait_ge(y_evac, 4 * CHUNKS)

            def swap_q(h):
                sp.wait_ge(hp_evac, 2 if isinstance(h, int) and h == 0 else 10 * h + 4)
                sp.dma_start(tb[0:64], ta[64:128]).then_inc(qr_swapped, 16)
                sp.dma_start(tb[64:128], ta[0:64]).then_inc(qr_swapped, 16)

            swap_q(0)

            def mixed_and_weights(n):
                q, half, kt = n % RING, n // 16, n % 16
                if n >= RING:
                    sp.wait_ge(e_split, 2 * (n - RING) + 2)
                sp.dma_start(owr[q][:], w_out[0, kt * P:(kt + 1) * P, :]).then_inc(ow_in[q], 16)
                if kt == HEADS - 1:
                    sp.wait_ge(o_out, 16 * HEADS)
                src = sco[kt] if kt < HEADS else scg[kt - HEADS]
                sp.dma_start(mxr[q][:], src[:, half * HB:(half + 1) * HB]).then_inc(mx_in[q], 16)

            def head_io(h, fill):
                if fill and not (isinstance(h, int) and h == HEADS - 2):
                    head_weights(h + 2, h + 2)
                z_att, z_ssm, head = address(h + Z_ATT0), address(h + Z_SSM0), address(h)
                if not isinstance(h, int) or h > 0:
                    sp.wait_ge(o_ready, 2 * h)
                sp.dma_start(zs[:], scr[bass.ds(z_att, 1)]).then_inc(z_in, 16)
                if not fill:
                    sp.wait_ge(pv_ready, 2 * HEADS - 2)
                    sp.wait_ge(hp_ready, 10 * HEADS)
                    for n in range(RING):
                        mixed_and_weights(n)
                if not isinstance(h, int) or h > 0:
                    sp.wait_ge(yg_out, 16 * h)
                    sp.wait_ge(sqa_ready, h)
                sp.dma_start(rl[:, 0, :], scr[bass.ds(z_ssm, 1)]).then_inc(zy_in, 16)
                sp.dma_start(rl[:, 1, :], scy[bass.ds(head, 1)]).then_inc(y_in, 16)
                if fill:
                    swap_q(h + 1)
                sp.wait_ge(yg_ready, h + 1)
                sp.dma_start(scg[bass.ds(head, 1)], rl[:, 1, :]).then_inc(yg_out, 16)
                sp.wait_ge(o_ready, 2 * h + 2)
                sp.dma_start(sco[bass.ds(head, 1)], ob[:]).then_inc(o_out, 16)

            def store_rows(s):
                sp.wait_ge(y_final, s + 1)
                sp.wait_ge(y_final_pool, s + 1)
                sp.dma_start(out[0, s * P:(s + 1) * P, :], yn[:, s % RT, :]).then_inc(done[s % RT], 16)

            head_weights(1, 1)
            head_io(0, True)
            with sp.Fori(1, HEADS - 2) as h:
                head_io(h, True)
            head_io(HEADS - 2, True)
            head_io(HEADS - 1, False)

            for n in range(4, 32):
                mixed_and_weights(n)
                if n == 8:
                    sp.wait_ge(pv_ready, 2 * HEADS)
                    sp.dma_start(res[:], x[0].rearrange("(s p) d -> p s d", p=P)).then_inc(res_in, 16)
                    sp.dma_start(lgb[:], ln_g[0].partition_broadcast(P)).then_inc(ln_in, 16)
                    sp.dma_start(lbb[:], ln_b[0].partition_broadcast(P)).then_inc(ln_in, 16)
                if 26 <= n < 30:
                    store_rows(n - 26)
            for s in range(RT, CHUNKS - 1):
                store_rows(s)
            for ready, r in ((y_final_pool, RIGHT), (y_final, LEFT)):
                sp.wait_ge(ready, CHUNKS)
                sp.dma_start(out[0, S - P:S, r], yn[:, RT - 1, r]).then_inc(done[RT - 1], 16)
            for q in range(RT):
                sp.wait_ge(done[q], 48 if q == RT - 1 else 32)

        @block.gpsimd
        def _(pool):
            ch = Chain(pool, poolc)
            ch.link(pool.memset(ident[:], 0.0))
            pool.affine_select(ident[:], ident[:], pattern=[[-1, P]], compare_op=ALU.not_equal, fill=1.0,
                               base=0, channel_multiplier=1).then_inc(consts, 1)
            ch.link(pool.memset(mask_qk[:], 0.0))
            pool.affine_select(mask_qk[:], mask_qk[:], pattern=[[-1, P]], compare_op=ALU.is_ge, fill=NEG,
                               base=0, channel_multiplier=1).then_inc(consts, 1)
            ch.link(pool.memset(mask_ls[:], 0.0))
            pool.affine_select(mask_ls[:], mask_ls[:], pattern=[[1, P]], compare_op=ALU.is_ge, fill=NEG,
                               base=0, channel_multiplier=-1).then_inc(consts, 1)
            pool.memset(ones[:], 1.0).then_inc(consts, 1)

            def split_tile(p, tile):
                pool.wait_ge(w_hi, tile + 1)
                pool.tensor_tensor(wl[:, p], wraw[:, p], wh[:, p].bitcast(F32), ALU.subtract).then_inc(w_split, 1)

            pool.wait_ge(w_hi, 1)
            pool.tensor_tensor(wl[:, 0, :, 0:ROPE], wraw[:, 0, :, 0:ROPE], wh[:, 0, :, 0:ROPE].bitcast(F32), ALU.subtract)
            pool.tensor_tensor(dt_columns(wl), wraw[:, 0, :, ROPE:ROPE + 16].unsqueeze(2).to_broadcast([P, KT, 4, 16]),
                               dt_columns(wh).bitcast(F32), ALU.subtract).then_inc(w_split, 1)
            split_tile(1, 1)
            for k in range(KT - 2):
                u_low(pool, k).then_inc(u_split, 1)
            pool.wait_ge(u_split, KT - 2)
            pool.wait_ge(small_in, 16 * 11)
            for q in range(2):
                ch.link(pool.tensor_copy(dsk[64 * q:64 * q + 64, :], dsr[64 * q:64 * q + 64, q:SSM_H:2]))
            pool.wait_ge(w_split, 3)
            split_tile(1, 3)
            with pool.Fori(2, 9) as j:
                for p in range(2):
                    split_tile(p, 2 * j + p)
            with pool.Fori(0, CHUNKS) as i:
                split_tile(0, 2 * i + 18)
                pool.wait_ge(stage_ready, i + 1)
                pool.wait_ge(y_out, 16 * i + 16)
                pool.tensor_tensor(xd[:], stg[:, 0:NST, :], dsk[:].unsqueeze(2).to_broadcast([P, NST, P]),
                                   ALU.mult).then_inc(xd_ready, 1)
                split_tile(1, 2 * i + 19)

            def weights_low(h, part):
                r = HW_PART[part]
                pool.wait_ge(hw_hi, 2 * h + part + 1)
                pool.tensor_tensor(hwl[:, r], hwr[:, r], hwh[:, r].bitcast(F32), ALU.subtract).then_inc(hw_split, 1)

            for t in range(LAT):
                if t == 2:
                    weights_low(0, 0)
                    weights_low(0, 1)
                hi, lo = (v[:, t, :] if t < QLT else w[:, t - QLT, :] for v, w in ((qlh, ckh), (qll, ckl)))
                pool.wait_ge(lat_hi, t + 1)
                pool.tensor_tensor(lo, wraw[:, t % 2].rearrange("p k n -> p (k n)"), hi.bitcast(F32),
                                   ALU.subtract).then_inc(lat_split, 1)

            def ssm_tile(h, g):
                pool.wait_ge(y_in, 16 * h + 16)
                pool.wait_ge(zy_in, 16 * h + 16)
                pool.tensor_tensor(rl[:, 1, :], rl[:, 1, :], rl[:, 0, :], ALU.mult).then_inc(yg_ready, 1)
                pool.wait_ge(yg_ready, h + 1)
                ch.link(pool.tensor_tensor(rl[:, 0, :], rl[:, 1, :], rl[:, 1, :], ALU.mult))
                pool.tensor_tensor(sqa[:, g, :], sqa[:, g, :], rl[:, 0, :], ALU.add).then_inc(sqa_ready, 1)

            def rope_query(b, h):
                rope_sum(pool, h)
                rope_low(pool, b, h)
                pool.wait_ge(qr_ready, h + 1)

            def gain_right(s):
                pool.wait_ge(norm_ready, s + 1)
                v = yn[:, s % RT, RIGHT]
                ch.link(pool.tensor_tensor(v, v, lgb[:, RIGHT], ALU.mult))
                pool.tensor_tensor(v, v, lbb[:, RIGHT], ALU.add).then_inc(y_final_pool, 1)

            def fold_gate(n):
                pool.wait_ge(ow_in[n % RING], 16 * (n // RING + 1))
                pool.tensor_tensor(owr[n % RING][:], owr[n % RING][:], gate_b[:], ALU.mult).then_inc(ow_gated, 1)

            def beside_head(h, b):
                weights_low(h + 1, 1)
                ssm_tile(h, 0 if not isinstance(h, int) else h // 4)
                rope_query(1 - b, h + 1)
                if not (isinstance(h, int) and h == HEADS - 2):
                    weights_low(h + 2, 0)

            weights_low(1, 0)
            pool.wait_ge(y_evac, 4 * CHUNKS)
            ch.link(pool.memset(sqa[:], 0.0))
            ch.loop(0, 2)
            with pool.Fori(0, 2) as pair:
                ch.base, ch.n = ch.start + 2 * pair, 0
                for b in range(2):
                    beside_head(2 * pair + b, b)
            ch.end(2)
            for h in range(4, 7):
                beside_head(h, h % 2)
            for n in range(RING):
                fold_gate(n)
            ssm_tile(7, 1)
            for n in range(RING, 32):
                fold_gate(n)
                if n == 22:
                    pool.wait_ge(ln_in, 32)
                if 24 <= n < 28:
                    gain_right(n - 24)
            for s in range(RT, CHUNKS - 1):
                gain_right(s)
            pool.wait_ge(gain_ready, 1)
            v = yn[:, RT - 1, RIGHT]
            pool.tensor_tensor(v, v, lbb[:, RIGHT], ALU.add).then_inc(y_final_pool, 1)

        @block.tensor
        def _(pe):
            def three(dst, ah, al, bh, bl, start, stop):
                pe.matmul(dst, ah, bh, start=start, stop=False)
                pe.matmul(dst, ah, bl, start=False, stop=False)
                return pe.matmul(dst, al, bh, start=False, stop=stop)

            pe.wait_ge(consts, 4)

            def modulation(k):
                pe.wait_ge(ada_acc, k + 1)
                for part in range(2):
                    mm = pe.matmul(bk(6)[:, 2 * k + part:2 * k + part + 1], acc[:, k % 2, part * P:(part + 1) * P],
                                   ones[:, 0:1], start=True, stop=True)
                mm.then_inc(mod_mm, 1)

            def x_transposes(k):
                pe.wait_ge(x_in[k], 16)
                if k >= 1:
                    pe.wait_ge(uf_ready, k)
                for s in range(CHUNKS):
                    m = pe.transpose(bk(4 + s // 4)[:, (s % 4) * P:(s % 4 + 1) * P],
                                     xin[:, s, k * P:(k + 1) * P], ident[:])
                m.then_inc(xt_ready, 1)

            def proj_mm(p, n, k, start, stop):
                r = slice(n * HB, (n + 1) * HB)
                return three(bk(2 * p + n), wh[:, p, k, :], wl[:, p, k, :],
                             uh[:, k, r], ul[:, k, r], start, stop)

            x_transposes(0)
            pe.wait_ge(vec_in, 16 * 6)
            pe.transpose(bk(7)[:, 0:NVEC], vrow[:], ident[0:NVEC, 0:NVEC]).then_inc(colv_mm, 1)
            modulation(0)
            for k in range(KT):
                if k + 1 < KT:
                    x_transposes(k + 1)
                    modulation(k + 1)
                if k == 0:
                    pe.wait_ge(w_split, 2)
                if k < KT - 2:
                    pe.wait_ge(u_split, k + 1)
                else:
                    pe.wait_ge(u_split_last, k - (KT - 3))
                for p in range(2):
                    for n in range(NHALF):
                        mm = proj_mm(p, n, k, k == 0, k == KT - 1)
                        if k == KT - 1:
                            mm.then_inc(proj_ready, 1)

            def proj_tile(p, tile):
                pe.wait_ge(w_split, tile + 1)
                for n in range(NHALF):
                    pe.wait_ge(proj_evac, 2 * tile + n - 3)
                    for k in range(KT):
                        mm = proj_mm(p, n, k, k == 0, k == KT - 1)
                    mm.then_inc(proj_ready, 1)

            with pe.Fori(1, 3) as j:
                for p in range(2):
                    proj_tile(p, 2 * j + p)
            pe.wait_ge(gate_acc, 1)
            pe.wait_ge(uf_ready, KT)
            for n in range(2):
                mm = pe.matmul(bk(4 + n), ones[:], cx[:, 0, n * HB:(n + 1) * HB], start=True, stop=True)
            mm.then_inc(gate_mm, 1)
            for p in range(2):
                proj_tile(p, 6 + p)
            pe.wait_ge(sq_ready, 1)
            pe.wait_ge(gate_ready, 1)
            for g in range(2):
                for n in range(2):
                    mm = pe.matmul(bk(4 + 2 * g + n), ones[:], rb[:, g, n * HB:(n + 1) * HB], start=True, stop=True)
            mm.then_inc(ss_mm, 1)
            with pe.Fori(4, 9) as j:
                for p in range(2):
                    proj_tile(p, 2 * j + p)

            def proj_part(p, n, part, tile):
                if part == 0:
                    if n == 0:
                        pe.wait_ge(w_split, tile + 1)
                    pe.wait_ge(proj_evac, 2 * tile + n - 3)
                steps = [(k, q) for k in range(KT) for q in range(3)][8 * part:8 * part + 8]
                for k, q in steps:
                    a = wl if q == 2 else wh
                    b = ul if q == 1 else uh
                    mm = pe.matmul(bk(2 * p + n), a[:, p, k, :], b[:, k, n * HB:(n + 1) * HB],
                                   start=(k == 0 and q == 0), stop=(k == KT - 1 and q == 2))
                if part == 2:
                    mm.then_inc(proj_ready, 1)

            def acum_rows(r, c):
                if r == 0:
                    pe.wait_ge(bd_ready, c + 1)
                    pe.wait_ge(xdt_ready, c + 1)
                if r >= 2:
                    pe.wait_ge(arg_ready, 4 * c + r - 1)
                for i in range(2):
                    j = 2 * r + i
                    mm = pe.matmul(bk(4 + r % 2)[:, 2 * i * P:2 * (i + 1) * P], selc[:, j:j + 1].to_broadcast([P, P]),
                                   bd[:].rearrange("p q l -> p (q l)"), start=True, stop=True)
                mm.then_inc(acb_ready, 1)

            def y_round(r, c):
                pe.wait_ge(g_ready, 4 * c + r + 1)
                if r >= 2:
                    pe.wait_ge(y_evac, 4 * c + r - 1)
                for i in range(2):
                    j = 2 * r + i
                    d = bk(6 + r % 2)[:, i * 256:(i + 1) * 256]
                    pe.matmul(d, xdt[:, j * P:(j + 1) * P], dec[:, r % 2, i * 256:(i + 1) * 256], start=True, stop=False)
                    mm = pe.matmul(d, state[:, j * P:(j + 1) * P], cts[:, r % 2, i * 256:(i + 1) * 256],
                                   start=False, stop=True)
                mm.then_inc(y_ready, 1)

            def chunk(c, fills):
                parts = iter([(p, n, part) for p in range(2) for n in range(2) for part in range(3)])
                assert sum(fills) == 12

                def fill(count):
                    for _ in range(count):
                        p, n, part = next(parts)
                        proj_part(p, n, part, 2 * c + 18 + p)

                fill(fills[0])
                pe.wait_ge(stage_ready, c + 1)
                pe.wait_ge(state_new, c + 1)
                for j in range(8):
                    pe.transpose(bk(4 + j // 4)[:, (j % 4) * P:(j % 4 + 1) * P], stg[:, j, :], ident[:])
                for q, j in enumerate((12, 8, 9)):
                    pe.transpose(bk(6)[:, q * P:(q + 1) * P], stg[:, j, :], ident[:])
                for g in range(2):
                    mm = pe.matmul(bk(7)[:, g * P:(g + 1) * P], stg[:, 8 + g, :], stg[:, 10 + g, :], start=True, stop=True)
                mm.then_inc(t_ready, 1)
                fill(fills[1])
                acum_rows(0, c)
                fill(fills[2])
                acum_rows(1, c)
                fill(fills[3])
                y_round(0, c)
                acum_rows(2, c)
                fill(fills[4])
                y_round(1, c)
                acum_rows(3, c)
                fill(fills[5])
                y_round(2, c)
                fill(fills[6])
                y_round(3, c)
                fill(fills[7])
                if isinstance(c, int) and c == CHUNKS - 1:
                    return
                pe.wait_ge(xdte_ready, c + 1)
                for g in range(2):
                    mm = pe.matmul(bk(4 + g), bdt[:, B0 + g * P:B0 + (g + 1) * P], xdte[:, g * HB:(g + 1) * HB],
                                   start=True, stop=True)
                mm.then_inc(st_ready, 1)

            chunk(0, (5, 1, 1, 1, 1, 1, 1, 1))
            with pe.Fori(1, CHUNKS - 1) as c:
                chunk(c, (2, 2, 1, 2, 2, 1, 1, 1))
            chunk(CHUNKS - 1, (2, 2, 1, 2, 2, 1, 1, 1))

            pe.wait_ge(lat_split, QLT)
            pe.wait_ge(y_evac, 4 * CHUNKS)
            wq = [t[:, 0:768].rearrange("p (k n) -> p k n", n=256) for t in (hwh, hwl)]
            wk = [t[:, 768:1280].rearrange("p (k n) -> p k n", n=256) for t in (hwh, hwl)]

            def head_proj(u, b, h):
                if isinstance(h, int) and h == 0 and u == 4:
                    pe.wait_ge(lat_split, LAT)
                if unit_at(u, h) in (0, 4):
                    pe.wait_ge(hw_split, 2 * h + u // 4 + 1)
                if not (isinstance(h, int) and h == 0):
                    if u != 1:
                        pe.wait_ge(hp_evac, 10 * h + (0, 0, 1, 2, 3, 5, 6, 7, 8, 9)[u])
                    elif not (isinstance(h, int) and h == 1):
                        pe.wait_ge(o_ready, 2 * h - 2)
                elif u >= 4:
                    pe.wait_ge(hp_evac, max(u - 3, 8 if u >= 8 else 0))
                bk7 = unit_bank(u, h)
                n = u % 2
                r = slice(n * HB, (n + 1) * HB)
                if u < 4:
                    m0 = P * (u // 2)
                    for k in range(QLT):
                        mm = three(bk7, wq[0][:, k, m0:m0 + P], wq[1][:, k, m0:m0 + P], qlh[:, k, r], qll[:, k, r],
                                   k == 0, k == QLT - 1)
                elif u < 8:
                    m0 = P * (u // 2 - 2)
                    for k in range(KLT):
                        mm = three(bk7, wk[0][:, k, m0:m0 + P], wk[1][:, k, m0:m0 + P], ckh[:, k, r], ckl[:, k, r],
                                   k == 0, k == KLT - 1)
                else:
                    for j in range(4):
                        t = 4 * (u - 8) + j
                        mm = pe.transpose(bk7[:, j * P:(j + 1) * P], vt[:, t * P:(t + 1) * P], ident[:])
                mm.then_inc(hp_ready, 1)

            def scores(i, b, h):
                qnh, qnl, knh, knl, qr, _, _ = hd[b]
                if i == 0:
                    pe.wait_ge(qr_ready, h + 1)
                    pe.wait_ge(hp_evac, 10 * h + 8)
                first = isinstance(h, int) and h == 0 and i < 2
                if not first:
                    pe.wait_ge(exp_done, 8 * h + i - 1)
                q = slice(i * P, (i + 1) * P)
                end = (i + 1) * P
                for k0 in range(0, end, HB):
                    n = max(256, min(HB, end - k0))
                    d = bank[i % 2][:, k0 // HB, 0:n]
                    k = slice(k0, k0 + n)
                    pe.matmul(d, qnh[:, q], knh[:, k], start=True, stop=False)
                    pe.matmul(d, qnh[:, q], knl[:, k], start=False, stop=False)
                    pe.matmul(d, qnl[:, q], knh[:, k], start=False, stop=False)
                    pe.matmul(d, qr[:, q], krh[:, k], start=False, stop=False)
                    mm = pe.matmul(d, qr[:, q], krl[:, k], start=False, stop=True)
                mm.then_inc(s_ready, 1)

            def turn_probs(i, h):
                pe.wait_ge(p_ready, 8 * h + i + 1)
                for t0 in range(0, i + 1, 4):
                    n = TURNED[i] + t0 // 4
                    if not (isinstance(h, int) and h == 0 and n < 2):
                        pe.wait_ge(pt_split, 12 * h + n - 1)
                    for t in range(t0, min(i + 1, t0 + 4)):
                        mm = pe.transpose(bk(4 + n % 2)[:, (t - t0) * P:(t - t0 + 1) * P],
                                          prob[:, i % 2, t * P:(t + 1) * P], ident[:])
                    mm.then_inc(pt_ready, 1)

            def values(g, b, h, fill):
                vh, vl = hd[b][5:]
                if g == 0:
                    pe.wait_ge(hp_evac, 10 * h + (14 if fill else 10))
                pe.wait_ge(pt_split, 12 * h + (4, 12)[g])
                if not (isinstance(h, int) and h == 0 and g == 0):
                    pe.wait_ge(o_ready, 2 * h + g)
                last = 4 * g + 3
                for t in range(last + 1):
                    c0 = max(0, t - 4 * g) * P
                    mm = three(bk(6)[:, c0:HB], vh[:, t, :], vl[:, t, :], pth[:, t, c0:HB], ptl[:, t, c0:HB],
                               t == 0, t == last)
                mm.then_inc(pv_ready, 1)

            def gated_sum(u):
                if u == 0:
                    pe.wait_ge(sqa_ready, HEADS)
                    pe.wait_ge(hp_evac, 10 * HEADS)
                else:
                    pe.wait_ge(sr_copied, u)
                pe.matmul(bk(7), ones[:], sqa[:, u // 2, (u % 2) * HB:(u % 2 + 1) * HB], start=True,
                          stop=True).then_inc(sr_mm, 1)

            def out_rows(n, s, cols=(0, 1)):
                q, half, kt = n % RING, n // 16, n % 16
                if s == 0:
                    pe.wait_ge(e_split, 2 * n + 2)
                if n == 0:
                    for ready, value in (((exp_done, 63),), ((exp_done, 64),), ((pt_split, 96),),
                                         ((o_ready, 16), (sr_copied, 4)))[s]:
                        pe.wait_ge(ready, value)
                if n == 16:
                    pe.wait_ge(res_ready, s + 1)
                rows = slice(s * P, (s + 1) * P)
                for col in cols:
                    c = slice(col * HB, (col + 1) * HB)
                    mm = three(bk(2 * s + col), mxh[q][:, rows], mxl[q][:, rows], owh[q][:, c], owl[q][:, c],
                               kt == 0, kt == 15)
                if cols == (0,):
                    if kt == 15:
                        mm.then_inc(left_done, 1)
                elif kt == 15:
                    mm.then_inc(bank_done, 1)
                elif s == RT - 1:
                    mm.then_inc(o_mm, 1)

            def head(h, b, fill):
                for i in range(8):
                    if fill:
                        head_proj(i, 1 - b, h + 1)
                    if i + 2 < 8:
                        scores(i + 2, b, h)
                    if i == 4:
                        values(0, b, h, fill)
                    if not fill and i == 7:
                        for n in range(RING):
                            out_rows(n, 0)
                    turn_probs(i, h)
                if fill:
                    head_proj(8, 1 - b, h + 1)
                    scores(0, 1 - b, h + 1)
                    scores(1, 1 - b, h + 1)
                    head_proj(9, 1 - b, h + 1)
                else:
                    for n in range(RING):
                        out_rows(n, 1)
                values(1, b, h, fill)

            for u in FIRST[:8]:
                head_proj(u, 0, 0)
            pe.wait_ge(proj_evac, 68)
            pe.wait_ge(kr_ready, 1)
            scores(0, 0, 0)
            scores(1, 0, 0)
            for u in FIRST[8:]:
                head_proj(u, 0, 0)
            pe.wait_ge(hp_evac, 10)
            head(0, 0, True)
            with pe.Fori(0, 3) as hp:
                head(2 * hp + 1, 1, True)
                head(2 * hp + 2, 0, True)
            head(7, 1, False)

            for s in (2, 3):
                for n in range(RING):
                    if s == 2:
                        gated_sum(n)
                    out_rows(n, s)
            for n in range(RING, 28):
                for s in range(RT):
                    out_rows(n, s)
            for s, cols in ((0, (0, 1)), (1, (0, 1)), (2, (0, 1)), (3, (0,)), (3, (1,))):
                for n in range(28, 32):
                    out_rows(n, s, cols)

        @block.scalar
        def _(act):
            ch = Chain(act, actc)
            act.wait_ge(w_in_sem[0], 32)
            act.activation(wh[:, 0, :, 0:ROPE], wraw[:, 0, :, 0:ROPE], ACT.Copy)
            act.activation(dt_columns(wh), wraw[:, 0, :, ROPE:ROPE + 16].unsqueeze(2).to_broadcast([P, KT, 4, 16]),
                           ACT.Copy).then_inc(w_hi, 1)
            act.wait_ge(w_in_sem[1], 16)
            act.activation(wh[:, 1], wraw[:, 1], ACT.Copy).then_inc(w_hi, 1)
            act.wait_ge(colv_ready, 1)
            for k in range(KT):
                act.wait_ge(mod_mm, k + 1)
                for part in range(2):
                    j = 8 * part + k
                    m = act.activation(modc[:, j:j + 1], bk(6)[:, 2 * k + part:2 * k + part + 1], ACT.Identity,
                                       bias=colv[:, j:j + 1])
                ch.link(m)
                act.wait_ge(xt_ready, k + 1)
                if k >= 2:
                    act.wait_ge(u_split, k - 1)
                for dst in (uf[:, k % 2, :], uh[:, k, :]):
                    m = act.activation(dst, bank[2][:].rearrange("p a b -> p (a b)"), ACT.Identity,
                                       bias=modc[:, k:k + 1], scale=modc[:, 8 + k:9 + k])
                m.then_inc(uf_ready, 1)

            def high(p, arrived, tile):
                act.wait_ge(w_in_sem[p], arrived)
                if not isinstance(tile, int) or tile >= 2:
                    act.wait_ge(proj_ready, 2 * tile - 2)
                act.activation(wh[:, p], wraw[:, p], ACT.Copy).then_inc(w_hi, 1)

            def evac(tile, p, dst):
                for n in range(NHALF):
                    act.wait_ge(proj_ready, 2 * tile + n + 1)
                    act.activation(dst[:, n * HB:(n + 1) * HB], bk(2 * p + n), ACT.Copy).then_inc(proj_evac, 1)

            high(0, 48, 2)
            high(1, 32, 3)
            act.wait_ge(small_in, 16 * 11)
            for n in range(NHALF):
                r = slice(n * HB, (n + 1) * HB)
                act.wait_ge(proj_ready, 4 * 0 + 1 + n)
                act.activation(dtv[DT0:P, r], bk(n)[DT0:P], ACT.Identity,
                               bias=dtb[DT0:P]).then_inc(dt_v, 1)
                act.activation(ost[0:ROPE, 0, r], bk(n)[0:ROPE], ACT.Copy).then_inc(proj_evac, 1)
            evac(1, 1, qk[:, 0, :])
            act.activation(small[DT0:P, 0:1], alg[DT0:P], ACT.Exp)
            act.wait_ge(dt_abs, 1)
            ch.link(act.activation(dtw[DT0:P], dtw[DT0:P], ACT.Exp))
            act.activation(dtw[DT0:P], dtw[DT0:P], ACT.Ln, bias=1.0).then_inc(dt_log, 1)
            for t in range(2, 6):
                evac(t, t % 2, qk[:, t - 1, :])
                high(t % 2, 16 * (t // 2 + 2) + (16 if t % 2 == 0 else 0), t + 2)
                if t == 3:
                    act.wait_ge(csn_arg, 1)
                    act.activation(csn[:], csn[:], ACT.Sin).then_inc(csn_ready, 1)
                if t == 4:
                    act.wait_ge(kr_t, 1)
                    act.dma_start(ropes[0:64], ropex[64:128]).then_inc(kr_swapped, 16)
                    act.dma_start(ropes[64:128], ropex[0:64]).then_inc(kr_swapped, 16)
                if t == 5:
                    act.wait_ge(kr_sum, 1)
                    act.activation(krh[:], ropex, ACT.Copy).then_inc(krh_ready, 1)

            def conv_tile(j, p, free, before):
                if free:
                    act.wait_ge(conv_done, j - 1)
                evac(j + 6, p, xr[:, p, 3:3 + S])
                high(p, 16 * (j // 2 + 5) + (16 if p == 0 else 0), j + 8)
                if before is not None:
                    act.wait_ge(conv_done, j)
                    act.activation(cx[:, before, :], cx[:, before, :], ACT.Silu).then_inc(silu_done, 1)

            conv_tile(0, 0, False, None)
            conv_tile(1, 1, False, 0)
            act.wait_ge(ss_mm, 1)
            for g in range(2):
                act.activation(rb[:, g, :], bank[2 + g][:].rearrange("p a b -> p (a b)"), ACT.Sqrt,
                               bias=rcst[:, 3:4], scale=1.0 / (384, 256)[g]).then_inc(root_ready, 1)
            with act.Fori(1, 6) as j2:
                for p in range(2):
                    j = 2 * j2 + p
                    act.wait_ge(conv_done, j - 1)
                    evac(j + 6, p, xr[:, p, 3:3 + S])
                    high(p, 16 * j2 + (96 if p == 0 else 80), j + 8)
                    act.wait_ge(conv_done, j)
                    v = cx[:, bass.ds(j - 1, 1), :]
                    act.activation(v, v, ACT.Silu).then_inc(silu_done, 1)
            act.wait_ge(conv_done, CONVT)
            act.activation(cx[:, CONVT - 1, :], cx[:, CONVT - 1, :], ACT.Silu).then_inc(silu_done, 1)

            def z_half(i, p, n):
                act.wait_ge(proj_ready, 4 * i + 36 + 2 * p + n + 1)
                if n == 0:
                    act.wait_ge(z_out[p], 16 * i + 16)
                act.activation(ost[:, p, n * HB:(n + 1) * HB], bk(2 * p + n), ACT.Silu).then_inc(proj_evac, 1)

            def exp_rows(r, c):
                act.wait_ge(acb_ready, 4 * c + r + 1)
                act.activation(exa[:, r % 2, :], bk(4 + r % 2), ACT.Exp).then_inc(exa_ready, 1)

            def exp_decay(r, c):
                act.wait_ge(arg_ready, 4 * c + r + 1)
                act.activation(dec[:, r % 2, :], dec[:, r % 2, :], ACT.Exp).then_inc(dec_ready, 1)

            def chunk(c, more):
                exp_rows(0, c)
                exp_decay(0, c)
                exp_rows(1, c)
                exp_decay(1, c)
                if not more:
                    latent_high(0)
                act.wait_ge(g_ready, 4 * c + 1)
                exp_rows(2, c)
                exp_decay(2, c)
                if not more:
                    latent_high(1)
                z_half(c, 0, 0)
                z_half(c, 0, 1)
                if more:
                    high(0, 16 * c + 192, 2 * c + 20)
                else:
                    weights_high(0, 0)
                    weights_high(0, 1)
                    latent_high(2)
                act.wait_ge(g_ready, 4 * c + 2)
                exp_rows(3, c)
                exp_decay(3, c)
                act.wait_ge(arg_ready, 4 * c + 4)
                if more:
                    act.activation(cdv[:, 2, :], cdv[:, 1, :], ACT.Exp).then_inc(dte_ready, 1)
                else:
                    latent_high(3)
                z_half(c, 1, 0)
                if not more:
                    latent_high(4)
                z_half(c, 1, 1)
                if more:
                    high(1, 16 * c + 176, 2 * c + 21)

            def weights_high(h, part):
                r = HW_PART[part]
                if part == 0:
                    act.wait_ge(hw_in, 64 * h + 64)
                if not isinstance(h, int) or h > 0:
                    act.wait_ge(hp_ready, 10 * h - (6, 2)[part])
                act.activation(hwh[:, r], hwr[:, r], ACT.Copy).then_inc(hw_hi, 1)

            def latent_high(t):
                hi = qlh[:, t, :] if t < QLT else ckh[:, t - QLT, :]
                act.wait_ge(lat_in[t % 2], 16 * (t // 2 + 1))
                act.activation(hi, wraw[:, t % 2].rearrange("p k n -> p (k n)"), ACT.Copy).then_inc(lat_hi, 1)

            with act.Fori(0, CHUNKS - 1) as c:
                chunk(c, True)
            chunk(CHUNKS - 1, False)

            act.wait_ge(y_evac, 4 * CHUNKS)

            def hi_part(u, b, h):
                qnh, _, knh, _, _, vh, _ = hd[b]
                act.wait_ge(hp_ready, 10 * h + unit_at(u, h) + 1)
                n = u % 2
                r = slice(n * HB, (n + 1) * HB)
                if u < 2:
                    act.activation(qnh[:, r], unit_bank(u, h), ACT.Copy).then_inc(hp_hi, 1)
                elif u in (4, 5):
                    act.activation(knh[:, r], unit_bank(u, h), ACT.Copy).then_inc(hp_hi, 1)
                elif u in (6, 7):
                    if u == 6 and not (isinstance(h, int) and h == 0):
                        act.wait_ge(hp_ready, 10 * h)
                    act.activation(vt[:, r], unit_bank(u, h), ACT.Copy).then_inc(hp_evac, 1)
                elif u >= 8:
                    act.activation(vh[:, 4 * (u - 8):4 * (u - 8) + 4, :], unit_bank(u, h).rearrange("p (t v) -> p t v", v=P),
                                   ACT.Copy).then_inc(hp_hi, 1)

            def qr_high(b, h):
                act.wait_ge(qr_sum, h + 1)
                act.activation(hd[b][4][:], ta[:], ACT.Copy).then_inc(qr_hi, 1)

            def probs(i, b, h):
                act.wait_ge(s_max, 8 * h + i + 1)
                if not (isinstance(h, int) and h == 0 and i < 2):
                    act.wait_ge(pt_ready, 12 * h + (-2, 0, 1, 2, 3, 4, 6, 8)[i])
                n = (i + 1) * P
                act.activation(prob[:, i % 2, 0:n], bank[i % 2][:].rearrange("p a b -> p (a b)")[:, 0:n], ACT.Exp,
                               bias=small[:, 8 + i % 2:9 + i % 2], scale=SCALE,
                               accum_out=small[:, 12 + i % 2:13 + i % 2]).then_inc(exp_done, 1)

            def turned_high(i, h):
                for t0 in range(0, i + 1, 4):
                    n = TURNED[i] + t0 // 4
                    w = min(i + 1, t0 + 4) - t0
                    act.wait_ge(pt_ready, 12 * h + n + 1)
                    if n == 4:
                        act.wait_ge(pv_ready, 2 * h + 1)
                    if n == 0 and not (isinstance(h, int) and h == 0):
                        act.wait_ge(pv_ready, 2 * h)
                    act.activation(pth[:, t0:t0 + w, (i % 4) * P:(i % 4 + 1) * P],
                                   bk(4 + n % 2)[:, 0:w * P].rearrange("p (t q) -> p t q", q=P),
                                   ACT.Copy).then_inc(pt_hi, 1)

            def gated_copy(u):
                act.wait_ge(sr_mm, u + 1)
                act.activation(rs[:, u // 2, (u % 2) * HB:(u % 2 + 1) * HB], bk(7), ACT.Identity, bias=rcst[:, 3:4],
                               scale=1.0 / HB).then_inc(sr_copied, 1)

            def out_high(n):
                q = n % RING
                if n == 0:
                    act.wait_ge(hp_ready, 10 * HEADS)
                if n == 3:
                    act.wait_ge(pv_ready, 2 * HEADS - 2)
                if n >= RING:
                    m = n - RING
                    if m % 16 == 15:
                        act.wait_ge(bank_done, RT)
                    else:
                        act.wait_ge(o_mm, m - m // 16 + 1)
                act.wait_ge(ow_gated, n + 1)
                act.activation(owh[q][:], owr[q][:], ACT.Copy).then_inc(e_hi, 1)
                act.wait_ge(mx_in[q], 16 * (n // RING + 1))
                if n % 16 >= HEADS:
                    act.wait_ge(mx_norm, 8 * (n // 16) + n % 16 - 7)
                act.activation(mxh[q][:], mxr[q][:], ACT.Copy).then_inc(e_hi, 1)

            def head(h, b, fill, more=True):
                for i in range(8):
                    if i + 1 < 8:
                        probs(i + 1, b, h)
                    if fill and i not in (2, 3):
                        if i == 5:
                            qr_high(1 - b, h + 1)
                        hi_part(i, 1 - b, h + 1)
                    turned_high(i, h)
                    if fill and more and i == 6:
                        weights_high(h + 2, 0)
                    if not fill:
                        for n in {4: (0,), 5: (1,), 6: (2, 3)}.get(i, ()):
                            out_high(n)
                if fill:
                    hi_part(8, 1 - b, h + 1)
                    probs(0, 1 - b, h + 1)
                    hi_part(9, 1 - b, h + 1)
                    if more:
                        weights_high(h + 2, 1)

            for u in FIRST:
                if u == 6:
                    qr_high(0, 0)
                if u == 8:
                    weights_high(1, 0)
                    probs(0, 0, 0)
                if u not in (2, 3):
                    hi_part(u, 0, 0)
            weights_high(1, 1)
            head(0, 0, True)
            with act.Fori(0, 2) as hp:
                head(2 * hp + 1, 1, True)
                head(2 * hp + 2, 0, True)
            head(5, 1, True)
            head(6, 0, True, False)
            head(7, 1, False)
            for u in range(4):
                gated_copy(u)

            def gated_root():
                act.wait_ge(sr_inverse, 4)
                act.activation(rs[:].rearrange("p g s -> p (g s)"), rs[:].rearrange("p g s -> p (g s)"), ACT.Sqrt
                               ).then_inc(rs_ready, 1)

            def deviation(s):
                act.wait_ge(stat_ready, s + 1)
                act.activation(bns[:, s, 16:17], bns[:, s, 13:14], ACT.Sqrt, bias=small[:, 20:21]).then_inc(root_ln, 1)

            def centred(s):
                act.wait_ge(var_ready, s + 1)
                if s >= RT:
                    act.wait_ge(done[s % RT], 16)
                for r in ((slice(0, D),) if s < CHUNKS - 1 else (RIGHT, LEFT)):
                    act.activation(yn[:, s % RT, r], res[:, s, r], ACT.Identity, bias=bns[:, s, 18:19],
                                   scale=bns[:, s, 17:18]).then_inc(norm_ready, 1)

            for n in range(4, 32):
                out_high(n)
                if n == 7:
                    gated_root()
                if 20 <= n < 24:
                    deviation(n - 20)
                if 21 <= n < 25:
                    centred(n - 21)
            for s in range(RT, CHUNKS):
                deviation(s)
                centred(s)

        @block.vector
        def _(dve):
            ch = Chain(dve, dvec)
            dve.memset(small[:, 20:21], LN_EPS)
            dve.wait_ge(c_in, 16)

            def scaled_sum(dst, w):
                ch.link(dve.tensor_scalar(dst, w(0), ccol[:, 0:1], None, ALU.mult))
                for t in range(1, KT):
                    ins = dve.scalar_tensor_tensor(dst, w(t), ccol[:, t:t + 1], dst, ALU.mult, ALU.add)
                    if t < KT - 1:
                        ch.link(ins)
                return ins

            for k in range(KT):
                dve.wait_ge(ada_in[k % 4], 32 * (k // 4 + 1))
                if k >= 2:
                    dve.wait_ge(mod_mm, k - 1)
                scaled_sum(acc[:, k % 2, :], lambda t, k=k: wada[:, k % 4, t, :]).then_inc(ada_acc, 1)
                if k == 0:
                    dve.wait_ge(colv_mm, 1)
                    ch.link(dve.tensor_copy(colv[:], bk(7)[:, 0:NVEC]))
                    dve.tensor_scalar(colv[:, 8:16], colv[:, 8:16], 1.0, None, ALU.add).then_inc(colv_ready, 1)
            for k in (KT - 2, KT - 1):
                u_low(dve, k).then_inc(u_split_last, 1)

            dve.wait_ge(w_hi, 3)
            dve.wait_ge(w_split, 2)
            dve.tensor_tensor(wl[:, 0], wraw[:, 0], wh[:, 0].bitcast(F32), ALU.subtract).then_inc(w_split, 1)

            ch.link(dve.memset(cx[:, 12, :], 0.0))
            dve.wait_ge(small_in, 16 * 11)
            ch.link(dve.tensor_copy(selc[:], rcst[:, R_SEL:R_SEL + 8]))
            d16 = slice(DT0, DT0 + 16)
            d64 = slice(DT0, P)
            dve.wait_ge(dt_v, 2)
            dve.scalar_tensor_tensor(dtw[d64], dtv[d64], -1.0, dtv[d64], ALU.mult, ALU.min).then_inc(dt_abs, 1)
            dve.wait_ge(dt_log, 1)
            ch.link(dve.scalar_tensor_tensor(cx[d64, 12, :], dtv[d64], 0.0, dtw[d64], ALU.max, ALU.add))
            ch.link(dve.tensor_scalar(dtv[d64], cx[d64, 12, :], small[d64, 0:1], -1.0, ALU.mult, ALU.mult))
            twice, rows = dtv[0:32], slice(0, 32)
            for k in range(CHUNKS):
                r = slice(k * P, (k + 1) * P)
                dve.tensor_tensor_scan(cx[AC0:AC0 + 16, 12, r], ones[d16, 0:P], dtv[d16, r], 0.0, ALU.mult, ALU.add)
                dve.tensor_tensor_scan(twice[:, r], ones[AC0:P, 0:P], dtv[AC0:P, r], 0.0, ALU.mult,
                                       ALU.add).then_inc(dt_done, 1)
            dve.wait_ge(dt_done, CHUNKS)
            ch.link(dve.tensor_copy(ach[rows], twice))
            ch.link(dve.tensor_scalar(cx[rows, 12, :], twice, rcst[rows, R_LO:R_LO + 1], None, ALU.mult))
            ch.link(dve.scalar_tensor_tensor(cx[rows, 12, :], ach[rows].bitcast(F32), rcst[rows, R_HI:R_HI + 1],
                                             cx[rows, 12, :], ALU.mult, ALU.add))
            dve.wait_ge(gate_in, 16)
            scaled_sum(cx[:, 0, :], lambda t: cx[:, t, :]).then_inc(gate_acc, 1)
            dve.wait_ge(rope_in, 32)
            dve.wait_ge(small_in, 16 * 11)
            ang = csn
            ch.link(dve.tensor_copy(turns, posi[:]))
            ch.link(dve.tensor_scalar(ang[:], turns, rcst[:, 0:1], None, ALU.mult))
            ch.link(dve.tensor_scalar(turns, ang[:], 1.0 / (2 * np.pi), rcst[:, 2:3], ALU.mult, ALU.add))
            ch.link(dve.tensor_scalar(turns, turns, MAGIC, None, ALU.add))
            ch.link(dve.tensor_scalar(turns, turns, MAGIC, None, ALU.subtract))
            for part in (PI2_A, PI2_B, PI2_C):
                ch.link(dve.scalar_tensor_tensor(ang[:], turns, -part, ang[:], ALU.mult, ALU.add))
            ch.link(dve.tensor_scalar(ang[:], ang[:], rcst[:, 1:2], None, ALU.add))
            dve.tensor_scalar(ang[:], ang[:], 3.1415925, -3.1415925, ALU.min, ALU.max).then_inc(csn_arg, 1)
            dve.wait_ge(z_out[0], 16)
            dve.wait_ge(z_out[1], 16)
            dve.wait_ge(csn_ready, 1)
            dve.tensor_tensor(ropex, ropex, csn[:], ALU.mult).then_inc(kr_t, 1)
            dve.wait_ge(kr_swapped, 32)
            dve.tensor_tensor(ropex, ropex, ropes, ALU.add).then_inc(kr_sum, 1)
            dve.wait_ge(krh_ready, 1)
            dve.tensor_tensor(krl[:], ropex, krh[:].bitcast(F32), ALU.subtract).then_inc(kr_ready, 1)
            dve.wait_ge(kr_ready, 1)
            dve.wait_ge(gate_mm, 1)
            dve.tensor_tensor(gate_b[:], gate_b[:], bank[2][:].rearrange("p a b -> p (a b)"), ALU.add
                              ).then_inc(gate_ready, 1)
            dve.wait_ge(proj_evac, 12)
            ch.link(dve.tensor_tensor(rb[:, 0, :], qk[:, 0, :], qk[:, 0, :], ALU.mult))
            for t in (1, 2):
                ch.link(dve.tensor_tensor(sqs, qk[:, t, :], qk[:, t, :], ALU.mult))
                ch.link(dve.tensor_tensor(rb[:, 0, :], rb[:, 0, :], sqs, ALU.add))
            ch.link(dve.tensor_tensor(rb[:, 1, :], qk[:, 3, :], qk[:, 3, :], ALU.mult))
            ch.link(dve.tensor_tensor(sqs, qk[:, 4, :], qk[:, 4, :], ALU.mult))
            dve.tensor_tensor(rb[:, 1, :], rb[:, 1, :], sqs, ALU.add).then_inc(sq_ready, 1)
            for p in range(2):
                ch.link(dve.memset(xr[:, p, 0:3], 0.0))

            def conv(j, p, taps, bias, dst):
                dve.wait_ge(proj_evac, 2 * j + 14)
                ch.link(dve.tensor_scalar(dst, xr[:, p, 3:3 + S], taps(3), bias, ALU.mult, ALU.add))
                for k in (2, 1):
                    ch.link(dve.scalar_tensor_tensor(dst, xr[:, p, k:k + S], taps(k), dst, ALU.mult, ALU.add))
                dve.scalar_tensor_tensor(dst, xr[:, p, 0:S], taps(0), dst, ALU.mult, ALU.add).then_inc(conv_done, 1)

            for j in range(2):
                conv(j, j, lambda k, j=j: colv[:, C_CONVW + 12 * k + j:C_CONVW + 12 * k + j + 1],
                     colv[:, C_CONVB + j:C_CONVB + j + 1], cx[:, j, :])
            for g in range(2):
                dve.wait_ge(root_ready, g + 1)
                ch.link(dve.reciprocal(rb[:, g, :], rb[:, g, :]))
            for t in range(LAT):
                g = 0 if t < QLT else 1
                dve.scalar_tensor_tensor(qk[:, t, :], qk[:, t, :], colv[:, C_QG + t:C_QG + t + 1], rb[:, g, :],
                                         ALU.mult, ALU.mult).then_inc(lat_ready, 1)
            ch.loop(0, 6)
            with dve.Fori(1, 6) as j2:
                ch.base, ch.n = ch.start + 6 * (j2 - 1), 0
                for p in range(2):
                    j = 2 * j2 + p
                    conv(j, p, lambda k, j=j: colv[:, bass.ds(j + (C_CONVW + 12 * k), 1)],
                         colv[:, bass.ds(j + C_CONVB, 1)], cx[:, bass.ds(j, 1), :].rearrange("p a s -> p (a s)"))
            ch.end(5)

            dve.wait_ge(y_out, 16)
            dve.wait_ge(dt_done, CHUNKS)
            dve.wait_ge(silu_done, CONVT)
            dve.memset(bd[:].bitcast(F32), 0.0)
            dve.memset(state[:], 0.0).then_inc(state_new, 1)

            def ssd_round(r, c):
                g = r // 2
                dve.wait_ge(exa_ready, 4 * c + r + 1)
                for i in range(4):
                    h = 4 * r + i
                    dve.scalar_tensor_tensor(dec[:, r % 2, i * P:(i + 1) * P], bk(4 + r % 2)[:, i * P:(i + 1) * P],
                                             bdt[:, AC0 - DT0 + h:AC0 - DT0 + h + 1], mask_ls[:], ALU.subtract, ALU.add)
                dve.tensor_tensor(cdv[:, 1, 4 * r:4 * r + 4], bk(4 + r % 2)[:, P - 1:HB:P],
                                  bdt[:, AC0 - DT0 + 4 * r:AC0 - DT0 + 4 * r + 4], ALU.subtract).then_inc(arg_ready, 1)
                dve.tensor_copy(cdv[:, 0, 4 * r:4 * r + 4], exa[:, r % 2, P - 1:HB:P])
                if r >= 2:
                    dve.wait_ge(y_ready, 4 * c + r - 1)
                ex = exa[:, r % 2, :].rearrange("p (h l) -> p h l", h=4)
                dve.tensor_tensor(cts[:, r % 2, :].rearrange("p (h l) -> p h l", h=4), ex,
                                  stg[:, 10 + g, :].unsqueeze(1).to_broadcast([P, 4, P]), ALU.mult)
                dve.wait_ge(dec_ready, 4 * c + r + 1)
                de = dec[:, r % 2, :].rearrange("p (h l) -> p h l", h=4)
                dve.tensor_tensor(de, de, cbs[:, g * P:(g + 1) * P].unsqueeze(1).to_broadcast([P, 4, P]),
                                  ALU.mult).then_inc(g_ready, 1)

            def y_out_round(r, c):
                dve.wait_ge(y_ready, 4 * c + r + 1)
                if r == 0:
                    dve.wait_ge(xd_ready, c + 1)
                v = bk(6 + r % 2).rearrange("p (j l) -> p j l", j=2)
                for q in range(2):
                    rows = slice(64 * q, 64 * q + 64)
                    ins = dve.tensor_tensor(xd[rows, 2 * r:2 * r + 2, :], v[rows, :, q * P:(q + 1) * P],
                                            xd[rows, 2 * r:2 * r + 2, :], ALU.add)
                ins.then_inc(y_evac, 1)

            def chunk(c, more):
                dve.tensor_copy(stg[:], cx[:, :, bass.ds(c * P, P)]).then_inc(stage_ready, 1)
                dve.wait_ge(stage_ready, c + 1)
                dve.tensor_copy(bd[0:32, 0, :], stg[0:32, 12, :])
                dve.tensor_copy(bd[32:64, 1, :], stg[0:32, 12, :]).then_inc(bd_ready, 1)
                dve.wait_ge(t_ready, c + 1)
                dve.tensor_copy(bdt[:], bk(6)[:, DT0:3 * P]).then_inc(bdt_ready, 1)
                dve.tensor_copy(cbs[:], bk(7)[:, 0:2 * P])
                dve.wait_ge(bdt_ready, c + 1)
                for n in range(2):
                    ins = dve.tensor_tensor(xdt[:, n * HB:(n + 1) * HB].rearrange("p (h d) -> p h d", h=8),
                                            bk(4 + n).rearrange("p (h d) -> p h d", h=8),
                                            bdt[:, 8 * n:8 * n + 8].unsqueeze(2).to_broadcast([P, 8, 64]),
                                            ALU.mult)
                ins.then_inc(xdt_ready, 1)
                ssd_round(0, c)
                ssd_round(1, c)
                y_out_round(0, c)
                ssd_round(2, c)
                y_out_round(1, c)
                ssd_round(3, c)
                y_out_round(2, c)
                if not more:
                    y_out_round(3, c)
                    return
                dve.wait_ge(dte_ready, c + 1)
                dve.wait_ge(xdt_ready, c + 1)
                dve.tensor_tensor(xdte[:].rearrange("p (h d) -> p h d", h=16), xdt[:].rearrange("p (h d) -> p h d", h=16),
                                  cdv[:, 2, :].unsqueeze(2).to_broadcast([P, 16, 64]), ALU.mult).then_inc(xdte_ready, 1)
                y_out_round(3, c)
                st3 = state[:].rearrange("p (h d) -> p h d", h=16)
                dve.tensor_tensor(st3, st3, cdv[:, 0, :].unsqueeze(2).to_broadcast([P, 16, 64]),
                                  ALU.mult).then_inc(state_decayed, 1)
                dve.wait_ge(state_decayed, c + 1)
                dve.wait_ge(st_ready, c + 1)
                dve.tensor_tensor(state[:], state[:], bank[2][:].rearrange("p a b -> p (a b)"), ALU.add
                                  ).then_inc(state_new, 1)

            with dve.Fori(0, CHUNKS - 1) as c:
                chunk(c, True)
            chunk(CHUNKS - 1, False)

            def lo_part(u, b, h):
                qnh, qnl, knh, knl, qr, vh, vl = hd[b]
                n = u % 2
                r = slice(n * HB, (n + 1) * HB)
                order = (0, 1, 4, 5, 8, 9)
                if u in order:
                    dve.wait_ge(hp_hi, 6 * h + order.index(u) + 1)
                if u < 2:
                    dve.tensor_tensor(qnl[:, r], unit_bank(u, h), qnh[:, r].bitcast(F32), ALU.subtract).then_inc(hp_evac, 1)
                elif u < 4:
                    dve.wait_ge(hp_ready, 10 * h + unit_at(u, h) + 1)
                    if u == 2 and not (isinstance(h, int) and h == 0):
                        dve.wait_ge(qr_ready, h)
                    dve.tensor_tensor(ta[:, r], unit_bank(u, h), csn[:, r], ALU.mult).then_inc(hp_evac, 1)
                elif u < 6:
                    dve.tensor_tensor(knl[:, r], unit_bank(u, h), knh[:, r].bitcast(F32), ALU.subtract).then_inc(hp_evac, 1)
                elif u >= 8:
                    t = 4 * (u - 8)
                    dve.tensor_tensor(vl[:, t:t + 4, :], unit_bank(u, h).rearrange("p (t v) -> p t v", v=P),
                                      vh[:, t:t + 4, :].bitcast(F32), ALU.subtract).then_inc(hp_evac, 1)

            def row_max(i, h):
                dve.wait_ge(s_ready, 8 * h + i + 1)
                v = bank[i % 2][:].rearrange("p a b -> p (a b)")
                ch.link(dve.tensor_tensor(v[:, i * P:(i + 1) * P], v[:, i * P:(i + 1) * P], mask_qk[:], ALU.add))
                ch.link(dve.tensor_reduce(small[:, 4 + i % 2:5 + i % 2], v[:, 0:(i + 1) * P], AX.X, ALU.max))
                if not (isinstance(h, int) and h == 0 and i < 2):
                    dve.wait_ge(exp_done, 8 * h + i - 1)
                dve.tensor_scalar(small[:, 8 + i % 2:9 + i % 2], small[:, 4 + i % 2:5 + i % 2], -SCALE, None,
                                  ALU.mult).then_inc(s_max, 1)

            def normalise(i, h):
                dve.wait_ge(exp_done, 8 * h + i + 1)
                ch.link(dve.reciprocal(small[:, 16 + i % 2:17 + i % 2], small[:, 12 + i % 2:13 + i % 2]))
                n = (i + 1) * P
                dve.tensor_scalar(prob[:, i % 2, 0:n], prob[:, i % 2, 0:n], small[:, 16 + i % 2:17 + i % 2], None,
                                  ALU.mult).then_inc(p_ready, 1)

            def turned_low(i, h):
                for t0 in range(0, i + 1, 4):
                    n = TURNED[i] + t0 // 4
                    w = min(i + 1, t0 + 4) - t0
                    dve.wait_ge(pt_hi, 12 * h + n + 1)
                    q = slice((i % 4) * P, (i % 4 + 1) * P)
                    dve.tensor_tensor(ptl[:, t0:t0 + w, q], bk(4 + n % 2)[:, 0:w * P].rearrange("p (t q) -> p t q", q=P),
                                      pth[:, t0:t0 + w, q].bitcast(F32), ALU.subtract).then_inc(pt_split, 1)

            def gate_out(g, h):
                dve.wait_ge(pv_ready, 2 * h + g + 1)
                if g == 0:
                    dve.wait_ge(z_in, 16 * h + 16)
                    if not isinstance(h, int) or h > 0:
                        dve.wait_ge(o_out, 16 * h)
                r = slice(g * HB, (g + 1) * HB)
                dve.tensor_tensor(ob[:, r], bk(6), zs[:, r], ALU.mult).then_inc(o_ready, 1)

            def gated_inverse(u):
                dve.wait_ge(sr_copied, u + 1)
                v = rs[:, u // 2, (u % 2) * HB:(u % 2 + 1) * HB]
                dve.reciprocal(v, v).then_inc(sr_inverse, 1)

            def out_low(n):
                q, half, kt = n % RING, n // 16, n % 16
                if kt >= HEADS:
                    j = kt - HEADS
                    if n == HEADS:
                        dve.wait_ge(rs_ready, 1)
                    dve.wait_ge(mx_in[q], 16 * (n // RING + 1))
                    dve.scalar_tensor_tensor(mxr[q][:], mxr[q][:], colv[:, C_SG + j:C_SG + j + 1],
                                             rs[:, j // 4, half * HB:(half + 1) * HB], ALU.mult,
                                             ALU.mult).then_inc(mx_norm, 1)
                dve.wait_ge(e_hi, 2 * n + 1)
                dve.tensor_tensor(owl[q][:], owr[q][:], owh[q][:].bitcast(F32), ALU.subtract).then_inc(e_split, 1)
                dve.wait_ge(e_hi, 2 * n + 2)
                dve.tensor_tensor(mxl[q][:], mxr[q][:], mxh[q][:].bitcast(F32), ALU.subtract).then_inc(e_split, 1)

            def head(h, b, fill):
                normalise(0, h)
                for i in range(8):
                    if i + 1 < 8:
                        normalise(i + 1, h)
                    if fill:
                        lo_part(i, 1 - b, h + 1)
                    if i + 2 < 8:
                        row_max(i + 2, h)
                    turned_low(i, h)
                    if i == 5:
                        gate_out(0, h)
                    if not fill:
                        for n in {4: (0,), 5: (1,), 6: (2, 3)}.get(i, ()):
                            out_low(n)
                if fill:
                    lo_part(8, 1 - b, h + 1)
                    row_max(0, h + 1)
                    row_max(1, h + 1)
                    lo_part(9, 1 - b, h + 1)
                gate_out(1, h)

            for u in FIRST:
                if u == 4:
                    rope_sum(dve, 0)
                if u == 8:
                    rope_low(dve, 0, 0)
                    row_max(0, 0)
                    row_max(1, 0)
                lo_part(u, 0, 0)
            head(0, 0, True)
            per = 2 * (8 * 2 + 8)
            ch.loop(0, per)
            with dve.Fori(0, 3) as hp:
                ch.base, ch.n = ch.start + per * hp, 0
                head(2 * hp + 1, 1, True)
                head(2 * hp + 2, 0, True)
            ch.end(3)
            head(7, 1, False)

            def residual(s, r=slice(0, D)):
                return dve.scalar_tensor_tensor(res[:, s, r], res[:, s, r], ALPHA,
                                                bank[s % RT][:].rearrange("p a b -> p (a b)")[:, r], ALU.mult, ALU.add)

            def half_statistics(s, half):
                ch.link(dve.bn_stats(bns[:, s, 6 * half:6 * half + 6], res[:, s, (LEFT, RIGHT)[half]]))

            def statistics(s):
                dve.bn_aggr(bns[:, s, 12:14], bns[:, s, 0:12]).then_inc(stat_ready, 1)

            def scales(s):
                dve.wait_ge(root_ln, s + 1)
                ch.link(dve.reciprocal(bns[:, s, 17:18], bns[:, s, 16:17]))
                dve.scalar_tensor_tensor(bns[:, s, 18:19], bns[:, s, 12:13], -1.0, bns[:, s, 17:18], ALU.mult,
                                         ALU.mult).then_inc(var_ready, 1)

            def gain(s):
                v = yn[:, s % RT, LEFT]
                if s < CHUNKS - 1:
                    dve.wait_ge(norm_ready, s + 1)
                else:
                    w = yn[:, s % RT, RIGHT]
                    dve.wait_ge(norm_ready, CHUNKS)
                    dve.tensor_tensor(w, w, lgb[:, RIGHT], ALU.mult).then_inc(gain_ready, 1)
                    dve.wait_ge(norm_ready, CHUNKS + 1)
                ch.link(dve.tensor_tensor(v, v, lgb[:, LEFT], ALU.mult))
                dve.tensor_tensor(v, v, lbb[:, LEFT], ALU.add).then_inc(y_final, 1)

            for n in range(4, 32):
                out_low(n)
                if n < 8:
                    gated_inverse(n - 4)
                if n == 18:
                    dve.wait_ge(res_in, 16)
                    for s in range(RT):
                        dve.wait_ge(bank_done, s + 1)
                        residual(s).then_inc(res_ready, 1)
                    dve.wait_ge(res_ready, RT)
                    dve.wait_ge(ln_in, 32)
                if 20 <= n < 24:
                    half_statistics(n - 20, 0)
                    half_statistics(n - 20, 1)
                    statistics(n - 20)
                if 21 <= n < 25:
                    scales(n - 21)
                if 22 <= n < 26:
                    gain(n - 22)
            for s in range(RT, CHUNKS):
                if s < CHUNKS - 1:
                    dve.wait_ge(bank_done, s + 1)
                    ch.link(residual(s))
                    half_statistics(s, 0)
                    half_statistics(s, 1)
                else:
                    dve.wait_ge(left_done, 1)
                    ch.link(residual(s, LEFT))
                    half_statistics(s, 0)
                    dve.wait_ge(bank_done, s + 1)
                    ch.link(residual(s, RIGHT))
                    half_statistics(s, 1)
                statistics(s)
                if RT < s < CHUNKS - 1:
                    gain(s - 1)
                scales(s)
            gain(CHUNKS - 2)
            gain(CHUNKS - 1)


_INS = ["x", "c", "positions", "w_ada", "b_ada", "w_in", "q_norm_g", "w_qb", "kv_norm_g", "w_kvb", "conv_w", "conv_b",
        "dt_bias", "a_log", "d_skip", "ssm_norm_g", "w_out", "ln_g", "ln_b"]


def constants():
    half = ROPE // 2
    inv = (np.float32(1.0) / np.power(np.float32(10000.0), np.arange(half, dtype=np.float32) / np.float32(half))).astype(np.float32)
    phase = np.repeat([np.pi / 2, np.pi / 2, np.pi, 0.0], half)
    t = np.zeros((P, NROPEC), np.float32)
    t[:, 0], t[:, 1], t[:, 2], t[:, 3] = np.tile(inv, 4), phase, phase / (2 * np.pi), RMS_EPS
    t[0:16, R_HI], t[16:32, R_HI], t[16:32, R_LO] = 1.0, -1.0, 1.0
    for j in range(8):
        for block in range(2):
            head = 2 * j + block
            t[[32 * block + head, 32 * block + 16 + head], R_SEL + j] = 1.0
    return t


def kernel(**inputs):
    import concourse.bacc as bacc
    from concourse.bass_utils import run_bass_kernel_spmd

    nc = bacc.Bacc("TRN2", target_bir_lowering=False, num_devices=1)
    arrays, args = {}, []
    for name in _INS:
        a = np.ascontiguousarray(inputs[name])
        arrays[f"in_{name}"] = a
        args.append(nc.dram_tensor(f"in_{name}", a.shape, mybir.dt.from_np(a.dtype), kind="ExternalInput").ap())
    arrays["in_constants"] = constants()
    args.append(nc.dram_tensor("in_constants", [P, NROPEC], F32, kind="ExternalInput").ap())
    args.append(nc.dram_tensor("out_0", [1, S, D], F32, kind="ExternalOutput").ap())
    build_layer(nc, *args)
    r = run_bass_kernel_spmd(nc, [arrays], core_ids=[0])
    return r.results[0]["out_0"]
```
